# Optimizing a Trainium2 kernel written in Bass

```python
import math
import jax
import jax.numpy as jnp
from jax import lax
import numpy as np

D_MODEL = 1024
BATCH = 1
SEQ = 1024
DEPTH = 1

GRID_W = 64
CTX_LEN = 256
MIX_WIDTH = D_MODEL
ATTN_WIDTH = D_MODEL // 2
HEAD_DIM = 64
N_Q_HEADS = ATTN_WIDTH // HEAD_DIM
N_KV_HEADS = 2
GQA_GROUP = N_Q_HEADS // N_KV_HEADS
WINDOW = 128
BLOCK = 128
CONV_WIDTH_CH = MIX_WIDTH - ATTN_WIDTH
CONV_KERNEL = 31
FFN_HIDDEN = 2816
FFN_CONV = 3
ROPE_BASE = 10000.0
ROPE_AXIS_DIM = HEAD_DIM // 2
NORM_EPS = 1e-6
NEG_INF = -1e30

Q_COLS = N_Q_HEADS * HEAD_DIM
KV_COLS = N_KV_HEADS * HEAD_DIM
GLU_COLS = 2 * CONV_WIDTH_CH
IN_COLS = Q_COLS + 2 * KV_COLS + GLU_COLS

kernel_name = "hybrid_window_gqa_conformer_convffn_dit_layer"

def rms_norm(x, w):
    xf = x.astype(jnp.float32)
    y = xf * lax.rsqrt(jnp.mean(xf * xf, axis=-1, keepdims=True) + NORM_EPS)
    return (y * w.astype(jnp.float32)).astype(x.dtype)

def layer_norm(x, w, b):
    xf = x.astype(jnp.float32)
    mu = jnp.mean(xf, axis=-1, keepdims=True)
    var = jnp.mean(jnp.square(xf - mu), axis=-1, keepdims=True)
    y = (xf - mu) * lax.rsqrt(var + NORM_EPS)
    return (y * w.astype(jnp.float32) + b.astype(jnp.float32)).astype(x.dtype)

def modulate(h, shift, scale):
    return h * (1 + scale) + shift

def depthwise_conv(u, w, b):
    width = w.shape[0]
    pad = (width - 1) // 2
    y = lax.conv_general_dilated(
        u, w[:, None, :].astype(u.dtype), window_strides=(1,),
        padding=[(pad, pad)], dimension_numbers=("NWC", "WIO", "NWC"),
        feature_group_count=u.shape[-1])
    return y + b.astype(u.dtype)

def axial_rope_tables(row, col):
    inv = ROPE_BASE ** (-jnp.arange(0, ROPE_AXIS_DIM, 2, dtype=jnp.float32) / ROPE_AXIS_DIM)
    ang_r = row.astype(jnp.float32)[:, None] * inv
    ang_c = col.astype(jnp.float32)[:, None] * inv
    ang = jnp.concatenate([ang_r, ang_r, ang_c, ang_c], axis=-1)
    return jnp.cos(ang), jnp.sin(ang)

def rotate_half(u):
    u1, u2 = jnp.split(u, 2, axis=-1)
    return jnp.concatenate([-u2, u1], axis=-1)

def apply_axial_rope(x, cos, sin):
    s, hd = cos.shape
    shape = (s,) + (1,) * (x.ndim - 3) + (hd,)
    cos = cos.reshape(shape).astype(x.dtype)
    sin = sin.reshape(shape).astype(x.dtype)
    xr, xc = jnp.split(x, 2, axis=-1)
    rotated = jnp.concatenate([rotate_half(xr), rotate_half(xc)], axis=-1)
    return x * cos + rotated * sin

def windowed_gqa_with_context(q, k, v, k_ctx, v_ctx, sink):
    b, s = q.shape[0], q.shape[1]
    nb = s // BLOCK
    n_ctx = k_ctx.shape[1]
    scale = 1.0 / math.sqrt(HEAD_DIM)
    k_pad = jnp.pad(k, ((0, 0), (BLOCK, BLOCK), (0, 0), (0, 0)))
    v_pad = jnp.pad(v, ((0, 0), (BLOCK, BLOCK), (0, 0), (0, 0)))
    q_blocks = jnp.moveaxis(q.reshape(b, nb, BLOCK, N_KV_HEADS, GQA_GROUP, HEAD_DIM), 1, 0)
    offs_q = jnp.arange(BLOCK)
    offs_k = jnp.arange(3 * BLOCK)
    sink_col = jnp.broadcast_to(sink.astype(jnp.float32)[None, :, :, None, None],
                                (b, N_KV_HEADS, GQA_GROUP, BLOCK, 1))

    def one_block(args):
        i, qb = args
        kb = lax.dynamic_slice_in_dim(k_pad, i * BLOCK, 3 * BLOCK, axis=1)
        vb = lax.dynamic_slice_in_dim(v_pad, i * BLOCK, 3 * BLOCK, axis=1)
        qpos = i * BLOCK + offs_q
        kpos = (i - 1) * BLOCK + offs_k
        valid = ((jnp.abs(qpos[:, None] - kpos[None, :]) <= WINDOW)
                 & (kpos[None, :] >= 0) & (kpos[None, :] < s))
        s_loc = jnp.einsum("bqhgd,bkhd->bhgqk", qb, kb).astype(jnp.float32) * scale
        s_loc = jnp.where(valid, s_loc, NEG_INF)
        s_ctx = jnp.einsum("bqhgd,bkhd->bhgqk", qb, k_ctx).astype(jnp.float32) * scale
        p = jax.nn.softmax(jnp.concatenate([sink_col, s_ctx, s_loc], axis=-1), axis=-1)
        p = p.astype(v.dtype)
        o = (jnp.einsum("bhgqk,bkhd->bqhgd", p[..., 1:1 + n_ctx], v_ctx)
             + jnp.einsum("bhgqk,bkhd->bqhgd", p[..., 1 + n_ctx:], vb))
        return o

    out = lax.map(one_block, (jnp.arange(nb), q_blocks))
    return jnp.moveaxis(out, 0, 1).reshape(b, s, N_KV_HEADS * GQA_GROUP * HEAD_DIM)

def setup_inputs(seed: int = 0) -> dict:
    key = jax.random.key(seed)
    ks = jax.random.split(key, 24)
    f32 = jnp.float32

    def nrm(k, shape, scale):
        return jax.random.normal(k, shape, f32) * scale

    L = DEPTH
    return {
        "x": nrm(ks[0], (BATCH, SEQ, D_MODEL), 1.0),
        "c": nrm(ks[1], (BATCH, D_MODEL), 1.0),
        "ctx": nrm(ks[2], (BATCH, CTX_LEN, D_MODEL), 1.0),
        "c_ctx": nrm(ks[3], (D_MODEL,), 1.0),
        "w_mod": nrm(ks[4], (L, D_MODEL, 6 * D_MODEL), 0.5 * D_MODEL ** -0.5),
        "b_mod": nrm(ks[5], (L, 6 * D_MODEL), 0.02),
        "norm_mix_w": 1.0 + nrm(ks[6], (L, D_MODEL), 0.02),
        "w_in": nrm(ks[7], (L, D_MODEL, IN_COLS), D_MODEL ** -0.5),
        "q_norm_w": 1.0 + nrm(ks[8], (L, HEAD_DIM), 0.02),
        "k_norm_w": 1.0 + nrm(ks[9], (L, HEAD_DIM), 0.02),
        "sink_logit": nrm(ks[10], (L, N_Q_HEADS), 0.5),
        "conv_w": nrm(ks[11], (L, CONV_KERNEL, CONV_WIDTH_CH), CONV_KERNEL ** -0.5),
        "conv_b": nrm(ks[12], (L, CONV_WIDTH_CH), 0.02),
        "conv_norm_w": 1.0 + nrm(ks[13], (L, CONV_WIDTH_CH), 0.02),
        "conv_norm_b": nrm(ks[14], (L, CONV_WIDTH_CH), 0.02),
        "w_out": nrm(ks[15], (L, MIX_WIDTH, D_MODEL), MIX_WIDTH ** -0.5),
        "norm_ffn_w": 1.0 + nrm(ks[16], (L, D_MODEL), 0.02),
        "w_up": nrm(ks[17], (L, D_MODEL, 2 * FFN_HIDDEN), D_MODEL ** -0.5),
        "ffn_conv_w": nrm(ks[18], (L, FFN_CONV, 2 * FFN_HIDDEN), FFN_CONV ** -0.5),
        "ffn_conv_b": nrm(ks[19], (L, 2 * FFN_HIDDEN), 0.02),
        "w_down": nrm(ks[20], (L, FFN_HIDDEN, D_MODEL), FFN_HIDDEN ** -0.5),
    }

def reference(x, c, ctx, c_ctx, w_mod, b_mod, norm_mix_w, w_in, q_norm_w, k_norm_w,
              sink_logit, conv_w, conv_b, conv_norm_w, conv_norm_b, w_out,
              norm_ffn_w, w_up, ffn_conv_w, ffn_conv_b, w_down):
    b, s, d = x.shape
    rows = s // GRID_W
    row = jnp.broadcast_to(jnp.arange(rows)[:, None], (rows, GRID_W)).reshape(s)
    col = jnp.broadcast_to(jnp.arange(GRID_W)[None, :], (rows, GRID_W)).reshape(s)
    cos, sin = axial_rope_tables(row, col)

    for l in range(DEPTH):
        mod = jax.nn.silu(c) @ w_mod[l] + b_mod[l]
        sh1, sc1, g1, sh2, sc2, g2 = [m[:, None, :] for m in jnp.split(mod, 6, axis=-1)]
        mod_ctx = jax.nn.silu(c_ctx) @ w_mod[l] + b_mod[l]
        sh1c, sc1c = mod_ctx[:d], mod_ctx[d:2 * d]

        h = modulate(rms_norm(x, norm_mix_w[l]), sh1, sc1)
        hc = modulate(rms_norm(ctx, norm_mix_w[l]), sh1c, sc1c)
        proj = h @ w_in[l]
        q = proj[..., :Q_COLS].reshape(b, s, N_KV_HEADS, GQA_GROUP, HEAD_DIM)
        k = proj[..., Q_COLS:Q_COLS + KV_COLS].reshape(b, s, N_KV_HEADS, HEAD_DIM)
        v = proj[..., Q_COLS + KV_COLS:Q_COLS + 2 * KV_COLS].reshape(b, s, N_KV_HEADS, HEAD_DIM)
        glu_in = proj[..., Q_COLS + 2 * KV_COLS:]

        kv_ctx = hc @ w_in[l][:, Q_COLS:Q_COLS + 2 * KV_COLS]
        n_ctx = ctx.shape[1]
        k_ctx = rms_norm(kv_ctx[..., :KV_COLS].reshape(b, n_ctx, N_KV_HEADS, HEAD_DIM), k_norm_w[l])
        v_ctx = kv_ctx[..., KV_COLS:].reshape(b, n_ctx, N_KV_HEADS, HEAD_DIM)

        q = apply_axial_rope(rms_norm(q, q_norm_w[l]), cos, sin)
        k = apply_axial_rope(rms_norm(k, k_norm_w[l]), cos, sin)
        sink = sink_logit[l].reshape(N_KV_HEADS, GQA_GROUP)
        attn_out = windowed_gqa_with_context(q, k, v, k_ctx, v_ctx, sink)

        ga, gb = jnp.split(glu_in, 2, axis=-1)
        u = ga * jax.nn.sigmoid(gb)
        u = depthwise_conv(u, conv_w[l], conv_b[l])
        u = jax.nn.silu(layer_norm(u, conv_norm_w[l], conv_norm_b[l]))

        mix = jnp.concatenate([attn_out, u], axis=-1) @ w_out[l]
        x = x + g1 * mix

        h2 = modulate(rms_norm(x, norm_ffn_w[l]), sh2, sc2)
        up = depthwise_conv(h2 @ w_up[l], ffn_conv_w[l], ffn_conv_b[l])
        gate, val = jnp.split(up, 2, axis=-1)
        x = x + g2 * ((jax.nn.silu(gate) * val) @ w_down[l])
    return x


_drawn_inputs = setup_inputs


def setup_inputs(seed=0):
    import zlib

    import numpy as np

    out = dict(_drawn_inputs(seed))
    spreads = {}
    factors = {'ctx': 4.848,
     'b_mod': 2.882,
     'norm_mix_w': 8.0,
     'q_norm_w': 8.0,
     'k_norm_w': 8.0,
     'sink_logit': 8.0,
     'conv_b': 21.568,
     'conv_norm_w': 31.651,
     'conv_norm_b': 31.278,
     'norm_ffn_w': 8.0,
     'ffn_conv_b': 8.0}
    for name, (base, spread) in spreads.items():
        noise = np.random.default_rng([zlib.crc32(name.encode()), seed]).standard_normal(out[name].shape)
        drawn = base * np.exp(spread * noise) if base else spread * noise
        out[name] = jnp.asarray(drawn.astype(out[name].dtype))
    for name, factor in factors.items():
        out[name] = (out[name] * factor).astype(out[name].dtype)
    return out
```

```python
import math
from contextlib import ExitStack

import concourse.bass as bass
from concourse import mybir

F32 = mybir.dt.float32
F32R = mybir.dt.float32r
ALU = mybir.AluOpType
ACT = mybir.ActivationFunctionType
AX = mybir.AxisListType

P = 128
D = 1024
T = 1024
CTX = 256
KT = D // P
TT = T // P
CT = CTX // P
HALF = 512
HD = 64
NH = 8
NG = 2
GQ = NH // NG
QC = NH * HD
KVC = 2 * NG * HD
QKV = QC + KVC
CC = 512
CTL = CC // P
TAPS = 31
PAD = TAPS // 2
FF = 2816
FT = FF // P
EPS = 1e-6
SCALE = 1.0 / math.sqrt(HD)
MASKED = -1e30
KEYS = CTX + T

C_C, C_CTX, C_NMIX, C_NFFN, C_BMOD = 0, 8, 16, 24, 32
C_CONVB, C_CNW, C_CNB = 80, 84, 88
N_A = 92
C_FB, C_FW0 = N_A, N_A + FT * 2
C_FW1, C_FW2 = N_A + FT * 4, N_A + FT * 6
C_CONVW = N_A + FT * 8
N_COLS = C_CONVW + CTL * TAPS


class Memory:

    def __init__(self, nc, base):
        self.nc, self.base = nc, base

    def at(self, kib, name, shape, dt=F32):
        return self.nc.alloc_sbuf_tensor_at(name, shape, dt, offset=self.base + int(kib * 1024))


def build(nc, x, c, ctx, c_ctx, w_mod, b_mod, norm_mix_w, w_in, q_norm_w, k_norm_w, sink_logit,
          conv_w, conv_b, conv_norm_w, conv_norm_b, w_out, norm_ffn_w, w_up, ffn_conv_w,
          ffn_conv_b, w_down, rope, out):
    es = ExitStack()
    with es:
        mem = Memory(nc, 16512)
        at = mem.at
        ps = es.enter_context(nc.psum_tensor("ps", [P, 8, HALF], F32))
        x1_dram = nc.dram_tensor("x1_scratch", (T, D), F32, kind="Internal").ap()

        def sem(name):
            return es.enter_context(nc.semaphore(name))

        ident = at(0, "ident", [P, P])
        identr = at(0.5, "identr", [P, P], F32R)
        ones = at(1, "ones", [P, P])
        mask_prev = at(1.5, "mask_prev", [P, P], F32R)
        mask_next = at(2, "mask_next", [P, P], F32R)
        cols = at(2.5, "cols", [P, N_COLS])
        scal = at(4.25, "scal", [P, 256])
        g1b = at(5.5, "g1b", [P, D])
        g2b = at(9.5, "g2b", [P, D])
        ffs = at(13.5, "ffs", [P, FT, 8])
        meanw = at(14.5, "meanw", [P, P])
        maskf = at(15, "maskf", [P, 2, P])
        sinks = at(16, "sinks", [P, 2, NH])
        qkw = at(16.25, "qkw", [P, 2, HD])
        nat = scal[:, 0:16].rearrange("p (k two) -> p k two", two=2)
        ss = scal[:, 16:26]
        rst = scal[:, 26:36]
        modl = scal[:, 36:52]
        modc = scal[:, 52:68]
        A1, Ac = scal[:, 68:76], scal[:, 76:84]
        mod2 = scal[:, 84:100]
        A2 = scal[:, 100:108]
        ss2 = scal[:, 108:116]
        rs2 = scal[:, 116:124]
        ffcur = [scal[:, 128:136], scal[:, 136:144]]
        msq = at(16.75, "msq", [P, TT + CT, NH + NG])
        hx = at(143, "hx", [P, KT, 2, T], F32R)

        def f(ap):
            return ap.bitcast(F32)

        xs = at(18, "xs", [P, TT, D])
        xnT = at(50, "xnT", [P, KT, T])
        hc32 = at(18, "hc32", [P, KT, CTX])
        hcx = at(83, "hcx", [P, KT, 2, CTX], F32R)
        wm = at(99, "wm", [P, 3, 2 * D])
        junk = at(123, "junk", [P, D])
        cx = at(131, "cx", [P, CT, D])
        vecs = at(139, "vecs", [P, 4, P])
        NV = 3
        with ExitStack() as s1:
            sem1 = lambda n: s1.enter_context(nc.semaphore(n))
            vec_in, row_in = sem1("vec_in"), sem1("row_in")
            x_in = [sem1(f"x_in{t}") for t in range(TT + CT)]
            wm_in = [sem1(f"wm_in{i}") for i in range(NV)]
            const_step, const_done = sem1("const_step"), sem1("const_done")
            vecT, cols_done, silu_done = sem1("vecT"), sem1("cols_done"), sem1("silu_done")
            sq_done, ms_done, sqrt_done, rst_done = sem1("sq_done"), sem1("ms_done"), sem1("sqrt_done"), sem1("rst_done")
            xn_done, xT, xT_out = sem1("xn_done"), sem1("xT"), sem1("xT_out")
            mod_mm, mod_done, ab_done = sem1("mod_mm"), sem1("mod_done"), sem1("ab_done")
            h_mod, h_hi, h_lo = sem1("h_mod"), sem1("h_hi"), sem1("h_lo")
            hc_mod, hc_hi = sem1("hc_mod"), sem1("hc_hi")
            ffs_done = sem1("ffs_done")
            block = s1.enter_context(nc.Block())

            rows = lambda v, n: v.rearrange("(r q) -> r q", q=P)
            parts = [(0, C_C, 8, c[0]), (0, C_CTX, 8, c_ctx), (0, C_NMIX, 8, norm_mix_w[0]),
                     (0, C_NFFN, 8, norm_ffn_w[0]), (0, C_BMOD, 48, b_mod[0]), (0, C_CONVB, 4, conv_b[0]),
                     (0, C_CNW, 4, conv_norm_w[0]), (0, C_CNB, 4, conv_norm_b[0]),
                     (1, 0, 2 * FT, ffn_conv_b[0]), (1, 2 * FT, 2 * FT, ffn_conv_w[0, 0]),
                     (2, 0, 2 * FT, ffn_conv_w[0, 1]), (2, 2 * FT, 2 * FT, ffn_conv_w[0, 2])]
            vec_total = 16 * (len(parts) + 1)

            @block.sync
            def _(sp):
                for v, r0, n, src in parts:
                    sp.dma_start(vecs[r0:r0 + n, v, :], rows(src, n)).then_inc(vec_in, 16)
                sp.dma_start(vecs[0:TAPS * CTL, 3, :], conv_w[0].rearrange("w (r q) -> (w r) q", q=P)).then_inc(vec_in, 16)
                for k in range(KT):
                    if k >= NV:
                        sp.wait_ge(mod_mm, k - NV + 1)
                    sp.dma_start(wm[:, k % NV, :], w_mod[0, k * P:(k + 1) * P, 0:2 * D]).then_inc(wm_in[k % NV], 16)
                sp.dma_start(sinks[:, 0, :], sink_logit[0].partition_broadcast(P)).then_inc(row_in, 16)
                sp.dma_start(qkw[:, 0, :], q_norm_w[0].partition_broadcast(P)).then_inc(row_in, 16)
                sp.dma_start(qkw[:, 1, :], k_norm_w[0].partition_broadcast(P)).then_inc(row_in, 16)

            @block.gpsimd
            def _(pool):
                pool.memset(ident[:], 0.0).then_inc(const_step, 1)
                pool.memset(maskf[:], 0.0).then_inc(const_step, 1)
                pool.memset(ones[:], 1.0).then_inc(const_done, 1)
                pool.memset(meanw[:], 1.0 / CC).then_inc(const_done, 1)
                pool.wait_ge(const_step, 2)
                pool.affine_select(out=ident[:], in_=ident[:], compare_op=ALU.not_equal, fill=1.0, base=0,
                                   pattern=[[-1, P]], channel_multiplier=1).then_inc(const_done, 1)
                pool.affine_select(out=maskf[:, 0, :], in_=maskf[:, 0, :], compare_op=ALU.is_ge, fill=MASKED,
                                   base=0, pattern=[[1, P]], channel_multiplier=-1).then_inc(const_step, 1)
                pool.affine_select(out=maskf[:, 1, :], in_=maskf[:, 1, :], compare_op=ALU.is_ge, fill=MASKED,
                                   base=0, pattern=[[-1, P]], channel_multiplier=1).then_inc(const_step, 1)
                pool.wait_ge(const_done, 3)
                pool.tensor_copy(identr[:], ident[:]).then_inc(const_done, 1)
                pool.wait_ge(const_step, 4)
                pool.tensor_copy(mask_prev[:], maskf[:, 0, :]).then_inc(const_done, 1)
                pool.tensor_copy(mask_next[:], maskf[:, 1, :]).then_inc(const_done, 1)

            @block.tensor
            def _(pe):
                pe.wait_ge(const_done, 3)
                pe.wait_ge(vec_in, vec_total)
                off = 0
                for v, n in enumerate((N_A, 4 * FT, 4 * FT, TAPS * CTL)):
                    last = pe.transpose(ps[:, 7, off:off + n], vecs[0:n, v, :], ident[0:n, 0:n])
                    off += n
                last.then_inc(vecT, 1)

                def x_item(n):
                    hh, k = divmod(n, KT)
                    if n % KT == 0:
                        pe.wait_ge(xn_done, 4 * (hh + 1))
                    if n >= 7:
                        pe.wait_ge(xT_out, n - 6)
                    for t in range(4):
                        last = pe.transpose(ps[:, n % 7, t * P:(t + 1) * P], xs[:, 4 * hh + t, k * P:(k + 1) * P], ident[:])
                    last.then_inc(xT, 1)

                def mod_item(k):
                    pe.wait_ge(wm_in[k % NV], 16 * (k // NV + 1))
                    if k == 0:
                        pe.wait_ge(silu_done, 2)
                    for j in range(16):
                        last = pe.matmul(ps[:, 7, 2 * j:2 * j + 2], wm[:, k % NV, j * P:(j + 1) * P], nat[:, k, :],
                                         start=(k == 0 and j == 0), stop=(k == KT - 1), skip_group_check=True)
                    last.then_inc(mod_mm, 1)

                for k in range(4):
                    mod_item(k)
                for n in range(KT):
                    x_item(n)
                for k in range(4, KT):
                    mod_item(k)
                for n in range(KT, 2 * KT):
                    x_item(n)
                for n in range(2 * KT, 2 * KT + 4):
                    pe.wait_ge(xT_out, n - 6)
                    if n == 2 * KT:
                        pe.wait_ge(xn_done, TT + CT)
                    for kk in range(2):
                        for t in range(CT):
                            k = 2 * (n - 2 * KT) + kk
                            last = pe.transpose(ps[:, n % 7, (2 * kk + t) * P:(2 * kk + t + 1) * P],
                                                cx[:, t, k * P:(k + 1) * P], ident[:])
                    last.then_inc(xT, 1)

            @block.scalar
            def _(act):
                for t in range(TT):
                    act.dma_start(xs[:, t, :], x[0, t * P:(t + 1) * P, :]).then_inc(x_in[t], 16)
                for t in range(CT):
                    act.dma_start(cx[:, t, :], ctx[0, t * P:(t + 1) * P, :]).then_inc(x_in[TT + t], 16)
                act.wait_ge(cols_done, 1)
                act.activation(nat[:, :, 0], cols[:, C_C:C_C + KT], ACT.Silu).then_inc(silu_done, 1)
                act.activation(nat[:, :, 1], cols[:, C_CTX:C_CTX + KT], ACT.Silu).then_inc(silu_done, 1)
                for t in range(TT + CT):
                    act.wait_ge(x_in[t], 16)
                    if t:
                        act.wait_ge(sq_done, t)
                    act.activation(junk[:], xs[:, t, :] if t < TT else cx[:, t - TT, :], ACT.Square,
                                   accum_out=ss[:, t:t + 1]).then_inc(sq_done, 1)
                act.wait_ge(ms_done, 1)
                act.activation(rst, ss, ACT.Sqrt).then_inc(sqrt_done, 1)
                for n in range(2 * KT):
                    hh, k = divmod(n, KT)
                    act.wait_ge(xT, n + 1)
                    act.activation(xnT[:, k, hh * HALF:(hh + 1) * HALF], ps[:, n % 7, :], ACT.Copy).then_inc(xT_out, 1)
                act.wait_ge(ab_done, 2)
                for n in range(4):
                    act.wait_ge(xT, 2 * KT + n + 1)
                    for kk in range(2):
                        k = 2 * n + kk
                        last = act.activation(hc32[:, k, :], ps[:, (2 * KT + n) % 7, kk * CTX:(kk + 1) * CTX], ACT.Identity,
                                              scale=Ac[:, k:k + 1], bias=modc[:, k:k + 1])
                        last.then_inc(hc_mod, 1)
                for k in range(KT):
                    act.wait_ge(h_mod, k + 1)
                    act.activation(hx[:, k, 0, :], xnT[:, k, :], ACT.Copy).then_inc(h_hi, 1)
                act.wait_ge(hc_mod, KT)
                act.activation(hcx[:, :, 0, :], hc32[:], ACT.Copy).then_inc(hc_hi, 1)

            @block.vector
            def _(dve):
                dve.wait_ge(vecT, 1)
                dve.tensor_copy(cols[:], ps[:, 7, 0:N_COLS]).then_inc(cols_done, 1)
                dve.wait_ge(sq_done, TT + CT)
                dve.tensor_scalar(ss, ss, 1.0 / D, EPS, ALU.mult, ALU.add).then_inc(ms_done, 1)
                dve.wait_ge(sqrt_done, 1)
                dve.reciprocal(rst, rst).then_inc(rst_done, 1)
                dve.wait_ge(rst_done, 1)
                for t in range(TT + CT):
                    v = xs[:, t, :] if t < TT else cx[:, t - TT, :]
                    dve.tensor_scalar(v, v, rst[:, t:t + 1], None, ALU.mult).then_inc(xn_done, 1)
                for i, c0 in enumerate((C_FW0, C_FW1, C_FW2, C_FB)):
                    for g in range(2):
                        dve.tensor_copy(ffs[:, :, 4 * g + i], cols[:, c0 + g * FT:c0 + (g + 1) * FT]).then_inc(ffs_done, 1)
                dve.wait_ge(row_in, 48)
                dve.tensor_scalar(sinks[:, 1, :], sinks[:, 0, :], -1.0, None, ALU.mult).then_inc(ffs_done, 1)
                dve.wait_ge(mod_mm, KT)
                m = ps[:, 7, 0:32].rearrange("p (j two) -> p j two", two=2)
                for i, dst in enumerate((modl, modc)):
                    dve.tensor_tensor(out=dst, in0=m[:, :, i], in1=cols[:, C_BMOD:C_BMOD + 16], op=ALU.add).then_inc(mod_done, 1)
                dve.wait_ge(mod_done, 2)
                for src, dst in ((modl, A1), (modc, Ac)):
                    dve.scalar_tensor_tensor(out=dst, in0=src[:, 8:16], scalar=1.0, in1=cols[:, C_NMIX:C_NMIX + KT],
                                             op0=ALU.add, op1=ALU.mult).then_inc(ab_done, 1)
                dve.wait_ge(ab_done, 2)
                dve.wait_ge(xT_out, 2 * KT)

                def low(k):
                    dve.wait_ge(h_hi, k + 1)
                    dve.tensor_tensor(out=hx[:, k, 1, :], in0=xnT[:, k, :], in1=f(hx[:, k, 0, :]), op=ALU.subtract).then_inc(h_lo, 1)

                for k in range(KT):
                    dve.tensor_scalar(xnT[:, k, :], xnT[:, k, :], A1[:, k:k + 1], modl[:, k:k + 1], ALU.mult, ALU.add).then_inc(h_mod, 1)
                    if k >= 1:
                        low(k - 1)
                low(KT - 1)
                dve.wait_ge(hc_hi, 1)
                dve.tensor_tensor(out=hcx[:, :, 1, :], in0=hc32[:], in1=f(hcx[:, :, 0, :]), op=ALU.subtract).then_inc(h_lo, 1)

        UW = T + 2 * PAD
        u = at(18, "u", [P, CTL, UW])
        cacc = at(34.75, "cacc", [P, CTL, T])
        qw_raw = at(75, "qw_raw", [P, 2, QKV])
        qwh = at(51, "qwh", [P, KT, QKV], F32R)
        qwl = at(119, "qwl", [P, KT, QKV], F32R)
        gw_raw = at(99, "gw_raw", [P, KT, P])
        gwh = at(103, "gwh", [P, 2, KT, P], F32R)
        gwl = at(111, "gwl", [P, 2, KT, P], F32R)
        qraw = at(83, "qraw", [P, TT, QC])
        kvraw = at(99, "kvraw", [P, CT + TT, KVC])
        ptmp = at(109, "ptmp", [P, T])
        DVE_CONV = CTL - 1
        NGL = 2 * CTL
        with ExitStack() as s2:
            sem2 = lambda n: s2.enter_context(nc.semaphore(n))
            gw_in, gw_hi, gw_lo, gl_mm = sem2("gw_in"), sem2("gw_hi"), sem2("gw_lo"), sem2("gl_mm")
            qw_in = [sem2("qw_in0"), sem2("qw_in1")]
            qw_hi, qw_lo, qkv_mm, qkv_out = sem2("qw_hi"), sem2("qw_lo"), sem2("qkv_mm"), sem2("qkv_out")
            pad_done, gate_done, u_done = sem2("pad_done"), sem2("gate_done"), sem2("u_done")
            tap_done, ptap_mul, ptap_add = sem2("tap_done"), sem2("ptap_mul"), sem2("ptap_add")
            block = s2.enter_context(nc.Block())
            win = w_in[0].rearrange("(k p) n -> p k n", p=P)

            def glu_col(n):
                return QKV + (CC if n % 2 == 0 else 0) + (n // 2) * P

            @block.sync
            def _(sp):
                for n in range(NGL):
                    if n:
                        sp.wait_ge(gw_lo, n)
                    sp.dma_start(gw_raw[:], win[:, :, glu_col(n):glu_col(n) + P]).then_inc(gw_in, 16)
                    if n >= 2:
                        sp.wait_ge(qw_lo, n - 1)
                    sp.dma_start(qw_raw[:, n % 2, :], w_in[0, n * P:(n + 1) * P, 0:QKV]).then_inc(qw_in[n % 2], 16)

            @block.tensor
            def _(pe):
                for n in range(NGL):
                    b = 2 * (n % 4)
                    pe.wait_ge(gw_lo, n + 1)
                    if n >= 4:
                        pe.wait_ge(u_done, (n - 4) // 2 + 1)
                    for k in range(KT):
                        for hh in range(2):
                            o, s = ps[:, b + hh, :], slice(hh * HALF, (hh + 1) * HALF)
                            pe.matmul(o, gwh[:, n % 2, k, :], hx[:, k, 0, s], start=(k == 0), stop=False)
                            pe.matmul(o, gwh[:, n % 2, k, :], hx[:, k, 1, s], start=False, stop=False)
                        for hh in range(2):
                            o, s = ps[:, b + hh, :], slice(hh * HALF, (hh + 1) * HALF)
                            last = pe.matmul(o, gwl[:, n % 2, k, :], hx[:, k, 0, s], start=False, stop=(k == KT - 1))
                    last.then_inc(gl_mm, 1)
                pe.wait_ge(qw_lo, KT)
                for m in range(CT + TT):
                    b = 2 * (m % 4)
                    pe.wait_ge(u_done, 3 if m < 2 else CTL)
                    if m >= 4:
                        pe.wait_ge(qkv_out, m - 3)
                    for k in range(KT):
                        if m < CT:
                            h = [hcx[:, k, v, m * P:(m + 1) * P] for v in range(2)]
                        else:
                            h = [hx[:, k, v, (m - CT) * P:(m - CT + 1) * P] for v in range(2)]
                        for v in range(2):
                            for lo in range(2 - v):
                                w = (qwh, qwl)[lo]
                                first, end = (k == 0 and v == 0 and lo == 0), (k == KT - 1 and v == 1)
                                if m >= CT:
                                    pe.matmul(ps[:, b, :], h[v], w[:, k, 0:QC], start=first, stop=end)
                                last = pe.matmul(ps[:, b + 1, 0:KVC], h[v], w[:, k, QC:QKV], start=first, stop=end)
                    last.then_inc(qkv_mm, 1)

            @block.scalar
            def _(act):
                def split_glu(n):
                    act.wait_ge(gw_in, 16 * (n + 1))
                    if n >= 2:
                        act.wait_ge(gl_mm, n - 1)
                    act.activation(gwh[:, n % 2], gw_raw[:], ACT.Copy).then_inc(gw_hi, 1)

                def split_qkv(k):
                    act.wait_ge(qw_in[k % 2], 16 * (k // 2 + 1))
                    act.activation(qwh[:, k, :], qw_raw[:, k % 2, :], ACT.Copy).then_inc(qw_hi, 1)

                split_glu(0)
                split_qkv(0)
                split_glu(1)
                split_qkv(1)
                act.wait_ge(pad_done, 1)
                for n in range(NGL):
                    act.wait_ge(gl_mm, n + 1)
                    if n % 2 == 0:
                        ct, b = n // 2, 2 * (n % 4)
                        act.activation(u[:, ct, PAD:PAD + T], ps[:, b:b + 2, :].rearrange("p b n -> p (b n)"),
                                       ACT.Sigmoid).then_inc(gate_done, 1)
                    if n + 2 < NGL:
                        split_glu(n + 2)
                        split_qkv(n + 2)
                for m in range(CT + TT):
                    b = 2 * (m % 4)
                    act.wait_ge(qkv_mm, m + 1)
                    if m >= CT:
                        act.activation(qraw[:, m - CT, :], ps[:, b, :], ACT.Copy)
                    act.activation(kvraw[:, m, :], ps[:, b + 1, 0:KVC], ACT.Copy).then_inc(qkv_out, 1)

            @block.gpsimd
            def _(pool):
                pool.memset(u[:], 0.0).then_inc(pad_done, 1)
                pool.wait_ge(u_done, CTL)
                ct = CTL - 1
                for i in range(TAPS):
                    w = cols[:, C_CONVW + i * CTL + ct:C_CONVW + i * CTL + ct + 1]
                    if i == 0:
                        pool.tensor_scalar(cacc[:, ct, :], u[:, ct, 0:T], w, cols[:, C_CONVB + ct:C_CONVB + ct + 1],
                                           ALU.mult, ALU.add).then_inc(ptap_add, 1)
                        continue
                    if i > 1:
                        pool.wait_ge(ptap_add, i)
                    pool.tensor_scalar(ptmp[:], u[:, ct, i:i + T], w, None, ALU.mult).then_inc(ptap_mul, 1)
                    pool.wait_ge(ptap_mul, i)
                    pool.wait_ge(ptap_add, i)
                    pool.tensor_tensor(out=cacc[:, ct, :], in0=cacc[:, ct, :], in1=ptmp[:], op=ALU.add).then_inc(ptap_add, 1)

            @block.vector
            def _(dve):
                def split_glu(n):
                    dve.wait_ge(gw_hi, n + 1)
                    dve.tensor_tensor(out=gwl[:, n % 2], in0=gw_raw[:], in1=f(gwh[:, n % 2]), op=ALU.subtract).then_inc(gw_lo, 1)

                def split_qkv(k):
                    dve.wait_ge(qw_hi, k + 1)
                    dve.tensor_tensor(out=qwl[:, k, :], in0=qw_raw[:, k % 2, :], in1=f(qwh[:, k, :]), op=ALU.subtract).then_inc(qw_lo, 1)

                done = [0]

                def taps(count):
                    for _ in range(count):
                        if done[0] == DVE_CONV * TAPS:
                            return
                        ct, i = divmod(done[0], TAPS)
                        w = cols[:, C_CONVW + i * CTL + ct:C_CONVW + i * CTL + ct + 1]
                        if i == 0:
                            dve.wait_ge(u_done, ct + 1)
                            ins = dve.tensor_scalar(cacc[:, ct, :], u[:, ct, 0:T], w, cols[:, C_CONVB + ct:C_CONVB + ct + 1],
                                                    ALU.mult, ALU.add)
                        else:
                            dve.wait_ge(tap_done, done[0])
                            ins = dve.scalar_tensor_tensor(out=cacc[:, ct, :], in0=u[:, ct, i:i + T], scalar=w,
                                                           in1=cacc[:, ct, :], op0=ALU.mult, op1=ALU.add)
                        ins.then_inc(tap_done, 1)
                        done[0] += 1

                for n in range(2):
                    split_glu(n)
                    split_qkv(n)
                for n in range(NGL):
                    if n + 2 < NGL:
                        split_glu(n + 2)
                        split_qkv(n + 2)
                    if n % 2 == 1:
                        ct, b = n // 2, 2 * (n % 4)
                        dve.wait_ge(gate_done, ct + 1)
                        dve.wait_ge(gl_mm, n + 1)
                        dve.tensor_tensor(out=u[:, ct, PAD:PAD + T], in0=ps[:, b:b + 2, :].rearrange("p b n -> p (b n)"),
                                          in1=u[:, ct, PAD:PAD + T], op=ALU.mult).then_inc(u_done, 1)
                    if n:
                        taps(7)
                taps(DVE_CONV * TAPS)

        NK = CT + TT
        tabs = at(18, "tabs", [P, 4, TT, HD])
        qst = [at(26, "qst0", [P, NH, 2, HD], F32R), at(139, "qst1", [P, NH, 2, HD], F32R)]
        cs = at(30, "cs", [P, 2, TT, HD])
        qT = at(51, "qT", [P, NH, T], F32R)
        vd = at(109, "vd", [P, NK, NG, 2, P], F32R)
        ka = at(129, "ka", [P, NK, NG, HD])
        kb = at(134, "kb", [P, NK, NG, HD])
        kst = at(143, "kst", [P, NK, NG, 2, P], F32R)
        sqq = at(163, "sqq", [P, 2, QC])
        qa = at(167, "qa", [P, 2, QC])
        qb = at(171, "qb", [P, 2, QC])
        kT = at(175, "kT", [P, NG, 2, KEYS], F32R)
        ko = at(195, "ko", [P, NK, NG, HD])
        sqk = at(200, "sqk", [P, NK, NG, HD])
        kraw = kvraw[:, :, 0:NG * HD].rearrange("p t (g d) -> p t g d", g=NG)
        vraw = kvraw[:, :, NG * HD:KVC].rearrange("p t (g d) -> p t g d", g=NG)
        with ExitStack() as s3:
            sem3 = lambda n: s3.enter_context(nc.semaphore(n))
            cs_in, tab_done, sq_k, sq_q, sum_done = sem3("cs_in"), sem3("tab_done"), sem3("sq_k"), sem3("sq_q"), sem3("sum_done")
            ms3, sqrt3, rs3 = sem3("ms3"), sem3("sqrt3"), sem3("rs3")
            v_hi, v_lo = sem3("v_hi"), sem3("v_lo")
            k_norm, k_mul, k_rot, k_hi, k_lo = sem3("k_norm"), sem3("k_mul"), sem3("k_rot"), sem3("k_hi"), sem3("k_lo")
            q_norm, q_sin, q_cos, q_rot, q_hi, q_lo = (sem3(n) for n in ("q_norm", "q_sin", "q_cos", "q_rot", "q_hi", "q_lo"))
            qkT, qkT_out = sem3("qkT"), sem3("qkT_out")
            block = s3.enter_context(nc.Block())
            h3 = lambda ap: ap.rearrange("p (h d) -> p h d", h=NH)

            @block.sync
            def _(sp):
                sp.dma_start(cs[:], rope.rearrange("w (t p) d -> p w t d", p=P)).then_inc(cs_in, 16)

            @block.scalar
            def _(act):
                act.activation(sqk[:], kraw, ACT.Square).then_inc(sq_k, 1)
                for t in range(TT):
                    if t >= 2:
                        act.wait_ge(sum_done, t)
                    act.activation(sqq[:, t % 2, :], qraw[:, t, :], ACT.Square).then_inc(sq_q, 1)
                for r in range(2):
                    act.activation(vd[:, :, :, 0, r * HD:(r + 1) * HD], vraw, ACT.Copy).then_inc(v_hi, 1)
                act.wait_ge(ms3, 1)
                act.activation(msq[:], msq[:], ACT.Sqrt).then_inc(sqrt3, 1)
                act.wait_ge(k_rot, 2)
                for r in range(2):
                    act.activation(kst[:, :, :, 0, r * HD:(r + 1) * HD], ko[:], ACT.Copy).then_inc(k_hi, 1)

                def q_high(t):
                    act.wait_ge(q_rot, t + 1)
                    if t >= 2:
                        act.wait_ge(qkT, NK + 2 * (t - 1))
                    act.activation(qst[t % 2][:, :, 0, :], h3(qa[:, t % 2, :]), ACT.Copy).then_inc(q_hi, 1)

                q_high(0)
                for n in range(NK):
                    act.wait_ge(qkT, n + 1)
                    act.activation(kT[:, :, :, n * P:(n + 1) * P],
                                   ps[:, n % 8, :].rearrange("p (g v k) -> p g v k", g=NG, v=2), ACT.Copy).then_inc(qkT_out, 1)
                for t in range(TT):
                    if t + 1 < TT:
                        q_high(t + 1)
                    for hh in range(2):
                        n = NK + 2 * t + hh
                        act.wait_ge(qkT, n + 1)
                        act.activation(qT[:, 4 * hh:4 * hh + 4, t * P:(t + 1) * P],
                                       ps[:, n % 8, :].rearrange("p (h k) -> p h k", h=4), ACT.Copy).then_inc(qkT_out, 1)

            @block.gpsimd
            def _(pool):
                for t in range(TT):
                    pool.wait_ge(q_norm, t + 1)
                    if t >= 2:
                        pool.wait_ge(q_rot, t - 1)
                    a4 = qa[:, t % 2, :].rearrange("p (e x d) -> p e x d", e=2 * NH, x=2)
                    b4 = qb[:, t % 2, :].rearrange("p (e x d) -> p e x d", e=2 * NH, x=2)
                    sn = tabs[:, 1, t, :].rearrange("p (a x d) -> p a x d", a=2, x=2)
                    for half in range(2):
                        for a in range(2):
                            last = pool.tensor_tensor(out=b4[:, a::2, half, :], in0=a4[:, a::2, 1 - half, :],
                                                      in1=sn[:, a:a + 1, half, :].to_broadcast([P, NH, 16]), op=ALU.mult)
                            last.then_inc(q_sin, 1)

            @block.vector
            def _(dve):
                dve.wait_ge(cs_in, 16)
                sn = cs[:, 1].rearrange("p t (a x d) -> p t a x d", a=2, x=2)
                for i in range(2):
                    dve.tensor_tensor(out=tabs[:, 2 * i], in0=cs[:, 0], in1=qkw[:, i:i + 1, :].to_broadcast([P, TT, HD]),
                                      op=ALU.mult).then_inc(tab_done, 1)
                    w4 = qkw[:, i, :].rearrange("p (a x d) -> p a x d", a=2, x=2)
                    dst = tabs[:, 2 * i + 1].rearrange("p t (a x d) -> p t a x d", a=2, x=2)
                    for half in range(2):
                        for a in range(2):
                            dve.tensor_tensor(out=dst[:, :, a, half, :], in0=sn[:, :, a, half, :],
                                              in1=w4[:, a:a + 1, 1 - half, :].to_broadcast([P, TT, 16]), op=ALU.mult).then_inc(tab_done, 1)
                for m in range(CT):
                    dve.memset(msq[:, m, 0:NH], 1.0).then_inc(tab_done, 1)
                dve.wait_ge(sq_k, 1)
                dve.tensor_reduce(out=msq[:, :, NH:NH + NG], in_=sqk[:], axis=AX.X, op=ALU.add).then_inc(sum_done, 1)
                for t in range(TT):
                    dve.wait_ge(sq_q, t + 1)
                    dve.tensor_reduce(out=msq[:, CT + t, 0:NH], in_=h3(sqq[:, t % 2, :]), axis=AX.X, op=ALU.add).then_inc(sum_done, 1)
                dve.wait_ge(tab_done, 12)
                dve.wait_ge(sum_done, TT + 1)
                dve.tensor_scalar(msq[:], msq[:], 1.0 / HD, EPS, ALU.mult, ALU.add).then_inc(ms3, 1)
                for r in range(2):
                    dve.wait_ge(v_hi, r + 1)
                    dve.tensor_tensor(out=vd[:, :, :, 1, r * HD:(r + 1) * HD], in0=vraw, in1=f(vd[:, :, :, 0, r * HD:(r + 1) * HD]),
                                      op=ALU.subtract).then_inc(v_lo, 1)
                dve.wait_ge(sqrt3, 1)
                dve.reciprocal(msq[:], msq[:]).then_inc(rs3, 1)
                dve.wait_ge(rs3, 1)
                dve.tensor_tensor(out=ka[:], in0=kraw, in1=msq[:, :, NH:NH + NG].unsqueeze(3).to_broadcast([P, NK, NG, HD]),
                                  op=ALU.mult).then_inc(k_norm, 1)

                def q_normed(t):
                    if t >= 2:
                        dve.wait_ge(q_lo, t - 1)
                    dve.tensor_tensor(out=h3(qa[:, t % 2, :]), in0=h3(qraw[:, t, :]),
                                      in1=msq[:, CT + t, 0:NH].unsqueeze(2).to_broadcast([P, NH, HD]), op=ALU.mult).then_inc(q_norm, 1)

                q_normed(0)
                q_normed(1)
                dve.wait_ge(k_norm, 1)
                dve.tensor_tensor(out=ko[:, 0:CT], in0=ka[:, 0:CT], in1=qkw[:, 1:2, :].unsqueeze(1).to_broadcast([P, CT, NG, HD]),
                                  op=ALU.mult).then_inc(k_rot, 1)
                dve.tensor_tensor(out=ko[:, CT:], in0=ka[:, CT:], in1=tabs[:, 2].unsqueeze(2).to_broadcast([P, TT, NG, HD]),
                                  op=ALU.mult).then_inc(k_mul, 1)
                ka5 = ka[:].rearrange("p t g (a x d) -> p t g a x d", a=2, x=2)
                kb5 = kb[:].rearrange("p t g (a x d) -> p t g a x d", a=2, x=2)
                sk = tabs[:, 3].rearrange("p t (a x d) -> p t a x d", a=2, x=2)
                for g in range(NG):
                    for half in range(2):
                        dve.tensor_tensor(out=kb5[:, CT:, g, :, half, :], in0=ka5[:, CT:, g, :, 1 - half, :], in1=sk[:, :, :, half, :],
                                          op=ALU.mult).then_inc(k_mul, 1)
                dve.wait_ge(k_mul, 5)
                dve.tensor_tensor(out=ko[:, CT:], in0=ko[:, CT:], in1=kb[:, CT:], op=ALU.add).then_inc(k_rot, 1)

                def q_rotate(t):
                    dve.wait_ge(q_sin, 4 * (t + 1))
                    dve.tensor_tensor(out=h3(qa[:, t % 2, :]), in0=h3(qa[:, t % 2, :]), in1=tabs[:, 0, t:t + 1, :].to_broadcast([P, NH, HD]),
                                      op=ALU.mult).then_inc(q_cos, 1)
                    dve.wait_ge(q_cos, t + 1)
                    dve.tensor_tensor(out=qa[:, t % 2, :], in0=qa[:, t % 2, :], in1=qb[:, t % 2, :], op=ALU.add).then_inc(q_rot, 1)

                q_rotate(0)
                for r in range(2):
                    dve.wait_ge(k_hi, r + 1)
                    dve.tensor_tensor(out=kst[:, :, :, 1, r * HD:(r + 1) * HD], in0=ko[:], in1=f(kst[:, :, :, 0, r * HD:(r + 1) * HD]),
                                      op=ALU.subtract).then_inc(k_lo, 1)
                for t in range(TT):
                    dve.wait_ge(q_hi, t + 1)
                    dve.tensor_tensor(out=qst[t % 2][:, :, 1, :], in0=h3(qa[:, t % 2, :]), in1=f(qst[t % 2][:, :, 0, :]),
                                      op=ALU.subtract).then_inc(q_lo, 1)
                    if t + 2 < TT:
                        q_normed(t + 2)
                    if t + 1 < TT:
                        q_rotate(t + 1)

            @block.tensor
            def _(pe):
                pe.wait_ge(k_lo, 2)
                for n in range(NK + 2 * TT):
                    if n >= 8:
                        pe.wait_ge(qkT_out, n - 7)
                    if n < NK:
                        src = [kst[:, n, j // 2, j % 2, :] for j in range(4)]
                    else:
                        t, hh = divmod(n - NK, 2)
                        pe.wait_ge(q_lo, t + 1)
                        src = [qst[t % 2][:, 4 * hh + j].rearrange("p v d -> p (v d)") for j in range(4)]
                    for j in range(4):
                        last = pe.transpose(ps[:, n % 8, j * P:(j + 1) * P].bitcast(F32R), src[j], identr[:])
                    last.then_inc(qkT, 1)

        wm2 = at(18, "wm2", [P, 4, D])
        SW = CTX + 3 * P
        pbuf = [at(129, "p0", [P, GQ, SW]), at(99, "p1", [P, GQ, SW])]
        pth = at(195, "pth", [P, 2, HALF], F32R)
        ptl = at(199, "ptl", [P, 2, HALF], F32R)
        brow = [at(203, "brow0", [1, D]), at(139, "brow1", [1, D])]
        st = [scal[:, 144 + 16 * i:160 + 16 * i].rearrange("p (s h) -> p s h", s=4) for i in range(2)]
        NGRP = 2 * TT

        def key_tiles(i):
            return [0, 1] + [CT + j for j in (i - 1, i, i + 1) if 0 <= j < TT]

        first_item = [0]
        for n in range(NGRP):
            first_item.append(first_item[-1] + len(key_tiles(n // NG)))
        G_SECTIONS = (2, 5)
        C_SECTIONS = (3, 4)
        with ExitStack() as s4:
            sem4 = lambda n: s4.enter_context(nc.semaphore(n))
            wm2_in = [sem4(f"wm2_in{i}") for i in range(4)]
            brow_in, col_mm, row_acc, row_mul = sem4("brow_in"), sem4("col_mm"), sem4("row_acc"), sem4("row_mul")
            row_mm, row_out, mod2_done, a2_done = sem4("row_mm"), sem4("row_out"), sem4("mod2_done"), sem4("a2_done")
            qk_mm, max_done, negm_done, exp_done = sem4("qk_mm"), sem4("max_done"), sem4("negm_done"), sem4("exp_done")
            arg_done, sexp_done, den_done, rec_done, pn_done = (sem4(n) for n in ("arg_done", "sexp_done", "den_done", "rec_done", "pn_done"))
            pt_T, pt_hi, pt_lo, pv_mm, o_hi, o_lo = (sem4(n) for n in ("pt_T", "pt_hi", "pt_lo", "pv_mm", "o_hi", "o_lo"))
            block = s4.enter_context(nc.Block())

            @block.sync
            def _(sp):
                for r in range(2):
                    sp.dma_start(brow[r][:], b_mod[0:1, G_SECTIONS[r] * D:(G_SECTIONS[r] + 1) * D]).then_inc(brow_in, 16)
                for q in range(4 * KT):
                    n = q // 2
                    if n >= 2:
                        sp.wait_ge(col_mm if q % 2 == 0 else row_acc, n - 1)
                    sec = (C_SECTIONS if q % 2 == 0 else G_SECTIONS)[n // KT]
                    k = n % KT
                    sp.dma_start(wm2[:, q % 4, :], w_mod[0, k * P:(k + 1) * P, sec * D:(sec + 1) * D]).then_inc(wm2_in[q % 4], 16)

            @block.gpsimd
            def _(pool):
                muls = 0
                for n in range(2 * KT):
                    q, k, dst = 2 * n + 1, n % KT, (g1b, g2b)[n // KT]
                    pool.wait_ge(wm2_in[q % 4], 16 * (q // 4 + 1))
                    if k == 0:
                        pool.tensor_scalar(dst[:], wm2[:, q % 4, :], nat[:, k, 0:1], None, ALU.mult).then_inc(row_acc, 1)
                        continue
                    pool.tensor_scalar(wm2[:, q % 4, :], wm2[:, q % 4, :], nat[:, k, 0:1], None, ALU.mult).then_inc(row_mul, 1)
                    muls += 1
                    pool.wait_ge(row_mul, muls)
                    pool.wait_ge(row_acc, n)
                    pool.tensor_tensor(out=dst[:], in0=dst[:], in1=wm2[:, q % 4, :], op=ALU.add).then_inc(row_acc, 1)

            def head_steps(n):
                i, g = divmod(n, NG)
                return i, g, key_tiles(i)

            @block.tensor
            def _(pe):
                def scores(n, hl):
                    i, g, kts = head_steps(n)
                    hh = 4 * n + hl
                    b = 2 * (hh % 2)
                    if hh >= 2:
                        pe.wait_ge(exp_done, hh - 1)
                    q = qT[:, GQ * g + hl, i * P:(i + 1) * P]
                    lat = kts[2] * P
                    pe.matmul(ps[:, b, 0:CTX], q, kT[:, g, 0, 0:CTX], start=True, stop=False)
                    pe.matmul(ps[:, b, 0:CTX], q, kT[:, g, 1, 0:CTX], start=False, stop=True)
                    o = ps[:, b, CTX:CTX + 2 * P]
                    pe.matmul(o, q, kT[:, g, 0, lat:lat + 2 * P], start=True, stop=False)
                    last = pe.matmul(o, q, kT[:, g, 1, lat:lat + 2 * P], start=False, stop=False)
                    if i > 0:
                        last = pe.matmul(ps[:, b, CTX:CTX + P], identr[:], mask_prev[:], start=False, stop=True)
                    else:
                        last = pe.matmul(ps[:, b, CTX + P:CTX + 2 * P], identr[:], mask_next[:], start=False, stop=True)
                    if 0 < i < TT - 1:
                        o = ps[:, b + 1, 0:P]
                        pe.matmul(o, q, kT[:, g, 0, lat + 2 * P:lat + 3 * P], start=True, stop=False)
                        pe.matmul(o, q, kT[:, g, 1, lat + 2 * P:lat + 3 * P], start=False, stop=False)
                        last = pe.matmul(o, identr[:], mask_next[:], start=False, stop=True)
                    last.then_inc(qk_mm, 1)

                def turn(n, j):
                    it = first_item[n] + j
                    if j == 0:
                        pe.wait_ge(pn_done, 4 * (n + 1))
                    if it >= 2:
                        pe.wait_ge(pt_lo, it - 1)
                    for hl in range(GQ):
                        last = pe.transpose(ps[:, 4 + it % 2, hl * P:(hl + 1) * P], pbuf[n % 2][:, hl, j * P:(j + 1) * P], ident[:])
                    last.then_inc(pt_T, 1)

                def values(n, j):
                    i, g, kts = head_steps(n)
                    it = first_item[n] + j
                    if j == 0 and n:
                        pe.wait_ge(o_lo, 2 * n)
                    pe.wait_ge(pt_lo, it + 1)
                    o, v, s = ps[:, 6, :], kts[j], it % 2
                    pe.matmul(o, vd[:, v, g, 0, :], pth[:, s, :], start=(j == 0), stop=False)
                    pe.matmul(o, vd[:, v, g, 0, :], ptl[:, s, :], start=False, stop=False)
                    pe.matmul(o, vd[:, v, g, 1, :], pth[:, s, :], start=False, stop=(j == len(kts) - 1)).then_inc(pv_mm, 1)

                def mod_columns(n):
                    q = 2 * n
                    pe.wait_ge(wm2_in[q % 4], 16 * (q // 4 + 1))
                    for j in range(KT):
                        c0 = (n // KT) * KT + j
                        last = pe.matmul(ps[:, 7, c0:c0 + 1], wm2[:, q % 4, j * P:(j + 1) * P], nat[:, n % KT, 0:1],
                                         start=(n == 0 and j == 0), stop=(n % KT == KT - 1), skip_group_check=True)
                    last.then_inc(col_mm, 1)

                for hl in range(GQ):
                    scores(0, hl)
                for n in range(NGRP):
                    m = len(key_tiles(n // NG))
                    for j in range(m):
                        if n + 1 < NGRP and j < GQ:
                            scores(n + 1, j)
                        turn(n, j)
                        if j:
                            values(n, j - 1)
                    mod_columns(n)
                    values(n, m - 1)
                pe.wait_ge(row_acc, 2 * KT)
                pe.wait_ge(brow_in, 32)
                for r in range(2):
                    for hh in range(2):
                        o, s = ps[:, 2 * r + hh, :], slice(hh * HALF, (hh + 1) * HALF)
                        pe.matmul(o, ones[:], (g1b, g2b)[r][:, s], start=True, stop=False)
                        pe.matmul(o, ones[0:1, :], brow[r][0:1, s], start=False, stop=True).then_inc(row_mm, 1)

            def score_ap(hh, w):
                b = 2 * (hh % 2)
                return ps[:, b:b + 2, :].rearrange("p b n -> p (b n)")[:, 0:w]

            @block.scalar
            def _(act):
                def exps(n, hl):
                    hh = 4 * n + hl
                    w = P * len(key_tiles(n // NG))
                    act.wait_ge(negm_done, hh + 1)
                    if hl == 0 and n >= 2:
                        act.wait_ge(pt_T, first_item[n - 1])
                    act.activation(pbuf[n % 2][:, hl, 0:w], score_ap(hh, w), ACT.Exp, scale=SCALE,
                                   bias=st[n % 2][:, 1, hl:hl + 1], accum_out=st[n % 2][:, 2, hl:hl + 1]).then_inc(exp_done, 1)

                for hl in range(GQ):
                    exps(0, hl)
                for n in range(NGRP):
                    i, g, kts = head_steps(n)
                    act.wait_ge(arg_done, n + 1)
                    act.activation(st[n % 2][:, 3, :], st[n % 2][:, 3, :], ACT.Exp).then_inc(sexp_done, 1)
                    for j in range(len(kts)):
                        if n + 1 < NGRP and j < GQ:
                            exps(n + 1, j)
                        it = first_item[n] + j
                        act.wait_ge(pt_T, it + 1)
                        if it >= 2:
                            act.wait_ge(pv_mm, it - 1)
                        act.activation(pth[:, it % 2, :], ps[:, 4 + it % 2, :], ACT.Copy).then_inc(pt_hi, 1)
                    act.wait_ge(pv_mm, first_item[n + 1])
                    for r in range(2):
                        o = ps[r * HD:(r + 1) * HD, 6, :].rearrange("p (h k) -> p h k", h=GQ)[:, r::2, :]
                        act.activation(hx[r * HD:(r + 1) * HD, 2 * g:2 * g + 2, 0, i * P:(i + 1) * P], o, ACT.Copy).then_inc(o_hi, 1)
                for r in range(2):
                    for hh in range(2):
                        act.wait_ge(row_mm, 2 * r + hh + 1)
                        if r == 0 and hh == 0:
                            act.wait_ge(row_mm, 4)
                        act.activation((g1b, g2b)[r][:, hh * HALF:(hh + 1) * HALF], ps[:, 2 * r + hh, :], ACT.Copy).then_inc(row_out, 1)

            @block.vector
            def _(dve):
                def maxima(n, hl):
                    hh = 4 * n + hl
                    w = P * len(key_tiles(n // NG))
                    s = st[n % 2]
                    dve.wait_ge(qk_mm, hh + 1)
                    dve.reduce_max(s[:, 0, hl:hl + 1], score_ap(hh, w), axis=AX.X).then_inc(max_done, 1)
                    dve.wait_ge(max_done, hh + 1)
                    h = GQ * (n % NG) + hl
                    dve.tensor_scalar(s[:, 1, hl:hl + 1], s[:, 0, hl:hl + 1], -SCALE, sinks[:, 1, h:h + 1],
                                      ALU.mult, ALU.min).then_inc(negm_done, 1)

                for hl in range(GQ):
                    maxima(0, hl)
                for n in range(NGRP):
                    i, g, kts = head_steps(n)
                    s = st[n % 2]
                    dve.wait_ge(negm_done, 4 * (n + 1))
                    dve.tensor_tensor(out=s[:, 3, :], in0=sinks[:, 0, GQ * g:GQ * (g + 1)], in1=s[:, 1, :], op=ALU.add).then_inc(arg_done, 1)
                    dve.wait_ge(sexp_done, n + 1)
                    dve.wait_ge(exp_done, 4 * (n + 1))
                    dve.tensor_tensor(out=s[:, 2, :], in0=s[:, 2, :], in1=s[:, 3, :], op=ALU.add).then_inc(den_done, 1)
                    dve.wait_ge(den_done, n + 1)
                    dve.reciprocal(s[:, 2, :], s[:, 2, :]).then_inc(rec_done, 1)
                    dve.wait_ge(rec_done, n + 1)
                    w = P * len(kts)
                    for hl in range(GQ):
                        p = pbuf[n % 2][:, hl, 0:w]
                        dve.tensor_scalar(p, p, s[:, 2, hl:hl + 1], None, ALU.mult).then_inc(pn_done, 1)
                    for j in range(len(kts)):
                        if n + 1 < NGRP and j < GQ:
                            maxima(n + 1, j)
                        it = first_item[n] + j
                        dve.wait_ge(pt_hi, it + 1)
                        dve.tensor_tensor(out=ptl[:, it % 2, :], in0=ps[:, 4 + it % 2, :], in1=f(pth[:, it % 2, :]),
                                          op=ALU.subtract).then_inc(pt_lo, 1)
                    for r in range(2):
                        dve.wait_ge(o_hi, 2 * n + r + 1)
                        rows_ = slice(r * HD, (r + 1) * HD)
                        o = ps[rows_, 6, :].rearrange("p (h k) -> p h k", h=GQ)[:, r::2, :]
                        dve.tensor_tensor(out=hx[rows_, 2 * g:2 * g + 2, 1, i * P:(i + 1) * P], in0=o,
                                          in1=f(hx[rows_, 2 * g:2 * g + 2, 0, i * P:(i + 1) * P]), op=ALU.subtract).then_inc(o_lo, 1)
                dve.wait_ge(col_mm, 2 * KT)
                dve.tensor_tensor(out=mod2, in0=ps[:, 7, 0:2 * KT], in1=cols[:, C_BMOD + 3 * KT:C_BMOD + 5 * KT], op=ALU.add).then_inc(mod2_done, 1)
                dve.wait_ge(mod2_done, 1)
                dve.scalar_tensor_tensor(out=A2, in0=mod2[:, KT:], scalar=1.0, in1=cols[:, C_NFFN:C_NFFN + KT],
                                         op0=ALU.add, op1=ALU.mult).then_inc(a2_done, 1)

        lt = at(18, "lt", [P, CTL, T])
        woh = at(51, "woh", [P, KT, D], F32R)
        wol = at(83, "wol", [P, KT, D], F32R)
        wo_raw = at(115, "wo_raw", [P, 2, D])
        xt = at(123, "xt", [P, 3, D])
        hm = at(135, "hm", [P, KT, P])
        rstd = at(139, "rstd", [P, T])
        with ExitStack() as s5:
            sem5 = lambda n: s5.enter_context(nc.semaphore(n))
            wo_in = [sem5("wo_in0"), sem5("wo_in1")]
            wo_hi, wo_lo, xt_in = sem5("wo_hi"), sem5("wo_lo"), [sem5(f"xt_in{i}") for i in range(3)]
            mean_mm, cent, sq5, var_mm, eps_done, sqrt5, rec5, scaled, silu5, u_hi, u_lo = (
                sem5(n) for n in ("mean_mm", "cent", "sq5", "var_mm", "eps_done", "sqrt5", "rec5", "scaled", "silu5", "u_hi", "u_lo"))
            wo_mm, gated, x1_done, x1_out = sem5("wo_mm"), sem5("gated"), sem5("x1_done"), sem5("x1_out")
            ssq, ms5, sq2, r5, xn5, xT5, mod5, h2_hi, h2_lo = (
                sem5(n) for n in ("ssq", "ms5", "sq2", "r5", "xn5", "xT5", "mod5", "h2_hi", "h2_lo"))
            block = s5.enter_context(nc.Block())

            @block.sync
            def _(sp):
                for k in range(KT):
                    if k >= 2:
                        sp.wait_ge(wo_lo, k - 1)
                    sp.dma_start(wo_raw[:, k % 2, :], w_out[0, k * P:(k + 1) * P, :]).then_inc(wo_in[k % 2], 16)
                for t in range(TT):
                    if t >= 3:
                        sp.wait_ge(xn5, t - 2)
                        sp.wait_ge(xT5, t - 2)
                    sp.dma_start(xt[:, t % 3, :], x[0, t * P:(t + 1) * P, :]).then_inc(xt_in[t % 3], 16)

            @block.gpsimd
            def _(pool):
                for t in range(TT):
                    pool.wait_ge(x1_done, t + 1)
                    pool.dma_start(x1_dram[t * P:(t + 1) * P, :], xt[:, t % 3, :]).then_inc(x1_out, 16)
                pool.wait_ge(x1_out, 16 * TT)

            @block.tensor
            def _(pe):
                def mean_of(buf, signal):
                    for hh in range(2):
                        for ct in range(CTL):
                            last = pe.matmul(ps[:, hh + (2 if signal is var_mm else 0), :], meanw[:], buf[:, ct, hh * HALF:(hh + 1) * HALF],
                                             start=(ct == 0), stop=(ct == CTL - 1))
                    last.then_inc(signal, 1)

                mean_of(cacc, mean_mm)
                pe.wait_ge(sq5, CTL)
                mean_of(lt, var_mm)

                def project(t):
                    b = 4 + 2 * (t % 2)
                    if t == 0:
                        pe.wait_ge(wo_lo, KT)
                        pe.wait_ge(u_lo, CTL)
                    if t >= 2:
                        pe.wait_ge(gated, t - 1)
                    for k in range(KT):
                        for v in range(2):
                            a = hx[:, k, v, t * P:(t + 1) * P]
                            for lo in range(2 - v):
                                for hh in range(2):
                                    last = pe.matmul(ps[:, b + hh, :], a, (woh, wol)[lo][:, k, hh * HALF:(hh + 1) * HALF],
                                                     start=(k == 0 and v == 0 and lo == 0), stop=(k == KT - 1 and v == 1))
                    last.then_inc(wo_mm, 1)

                def turn(t):
                    b = 2 * (t % 2)
                    pe.wait_ge(xn5, t + 1)
                    if t >= 2:
                        pe.wait_ge(mod5, t - 1)
                    for k in range(KT):
                        last = pe.transpose(ps[:, b + k // 4, (k % 4) * P:(k % 4 + 1) * P], xt[:, t % 3, k * P:(k + 1) * P], ident[:])
                    last.then_inc(xT5, 1)

                for t in range(TT):
                    project(t)
                    if t:
                        turn(t - 1)
                turn(TT - 1)

            @block.scalar
            def _(act):
                for ct in range(CTL):
                    act.wait_ge(cent, ct + 1)
                    act.activation(lt[:, ct, :], cacc[:, ct, :], ACT.Square).then_inc(sq5, 1)
                for k in range(KT):
                    act.wait_ge(wo_in[k % 2], 16 * (k // 2 + 1))
                    act.activation(woh[:, k, :], wo_raw[:, k % 2, :], ACT.Copy).then_inc(wo_hi, 1)
                act.wait_ge(eps_done, 1)
                act.activation(rstd[:], rstd[:], ACT.Sqrt).then_inc(sqrt5, 1)
                for ct in range(CTL):
                    act.wait_ge(scaled, ct + 1)
                    act.activation(lt[:, ct, :], cacc[:, ct, :], ACT.Silu, scale=cols[:, C_CNW + ct:C_CNW + ct + 1],
                                   bias=cols[:, C_CNB + ct:C_CNB + ct + 1]).then_inc(silu5, 1)
                for ct in range(CTL):
                    act.wait_ge(silu5, ct + 1)
                    act.activation(hx[:, CTL + ct, 0, :], lt[:, ct, :], ACT.Copy).then_inc(u_hi, 1)
                for t in range(TT):
                    act.wait_ge(x1_done, t + 1)
                    if t:
                        act.wait_ge(h2_lo, t)
                    act.activation(hm[:].rearrange("p k n -> p (k n)"), xt[:, t % 3, :], ACT.Square, accum_out=ss2[:, t:t + 1]).then_inc(ssq, 1)
                    act.wait_ge(ms5, t + 1)
                    act.activation(ss2[:, t:t + 1], ss2[:, t:t + 1], ACT.Sqrt).then_inc(sq2, 1)
                    act.wait_ge(xT5, t + 1)
                    b = 2 * (t % 2)
                    for k in range(KT):
                        ins = act.activation(hm[:, k, :], ps[:, b + k // 4, (k % 4) * P:(k % 4 + 1) * P], ACT.Identity,
                                             scale=A2[:, k:k + 1], bias=mod2[:, k:k + 1])
                    ins.then_inc(mod5, 1)
                    act.wait_ge(mod5, t + 1)
                    act.activation(hx[:, :, 0, t * P:(t + 1) * P], hm[:], ACT.Copy).then_inc(h2_hi, 1)

            @block.vector
            def _(dve):
                both = lambda b: ps[:, b:b + 2, :].rearrange("p b n -> p (b n)")
                dve.wait_ge(mean_mm, 1)
                for ct in range(CTL):
                    dve.tensor_tensor(out=cacc[:, ct, :], in0=cacc[:, ct, :], in1=both(0), op=ALU.subtract).then_inc(cent, 1)
                for k in range(KT):
                    dve.wait_ge(wo_hi, k + 1)
                    dve.tensor_tensor(out=wol[:, k, :], in0=wo_raw[:, k % 2, :], in1=f(woh[:, k, :]), op=ALU.subtract).then_inc(wo_lo, 1)
                dve.wait_ge(var_mm, 1)
                dve.tensor_scalar(rstd[:], both(2), EPS, None, ALU.add).then_inc(eps_done, 1)
                dve.wait_ge(sqrt5, 1)
                dve.reciprocal(rstd[:], rstd[:]).then_inc(rec5, 1)
                dve.wait_ge(rec5, 1)
                for ct in range(CTL):
                    dve.tensor_tensor(out=cacc[:, ct, :], in0=cacc[:, ct, :], in1=rstd[:], op=ALU.mult).then_inc(scaled, 1)
                for ct in range(CTL):
                    dve.wait_ge(u_hi, ct + 1)
                    dve.tensor_tensor(out=hx[:, CTL + ct, 1, :], in0=lt[:, ct, :], in1=f(hx[:, CTL + ct, 0, :]), op=ALU.subtract).then_inc(u_lo, 1)

                def residual(t):
                    b = 4 + 2 * (t % 2)
                    dve.wait_ge(wo_mm, t + 1)
                    dve.tensor_tensor(out=rstd[:], in0=both(b), in1=g1b[:], op=ALU.mult).then_inc(gated, 1)
                    dve.wait_ge(xt_in[t % 3], 16 * (t // 3 + 1))
                    dve.wait_ge(gated, t + 1)
                    dve.tensor_tensor(out=xt[:, t % 3, :], in0=xt[:, t % 3, :], in1=rstd[:], op=ALU.add).then_inc(x1_done, 1)
                    dve.wait_ge(ssq, t + 1)
                    dve.tensor_scalar(ss2[:, t:t + 1], ss2[:, t:t + 1], 1.0 / D, EPS, ALU.mult, ALU.add).then_inc(ms5, 1)
                    dve.wait_ge(sq2, t + 1)
                    dve.reciprocal(rs2[:, t:t + 1], ss2[:, t:t + 1]).then_inc(r5, 1)
                    dve.wait_ge(r5, t + 1)
                    dve.wait_ge(x1_out, 16 * (t + 1))
                    dve.tensor_scalar(xt[:, t % 3, :], xt[:, t % 3, :], rs2[:, t:t + 1], None, ALU.mult).then_inc(xn5, 1)

                for t in range(TT):
                    residual(t)
                    dve.wait_ge(h2_hi, t + 1)
                    dve.tensor_tensor(out=hx[:, :, 1, t * P:(t + 1) * P], in0=hm[:], in1=f(hx[:, :, 0, t * P:(t + 1) * P]),
                                      op=ALU.subtract).then_inc(h2_lo, 1)

        hid = at(18, "hid", [P, FT, T])
        up_raw = at(106, "up_raw", [P, 2, KT, P])
        uph = at(114, "uph", [P, 2, KT, P], F32R)
        upl = at(122, "upl", [P, 2, KT, P], F32R)
        y = at(130, "y", [P, 2, T])
        with ExitStack() as s6:
            sem6 = lambda n: s6.enter_context(nc.semaphore(n))
            up_in = [sem6("up_in0"), sem6("up_in1")]
            up_hi, up_lo, up_mm = sem6("up_hi"), sem6("up_lo"), sem6("up_mm")
            cur_done, mid_tap, left_tap, side_taps, act_done, hid_done = (
                sem6(n) for n in ("cur_done", "mid_tap", "left_tap", "side_taps", "act_done", "hid_done"))
            block = s6.enter_context(nc.Block())
            wup = w_up[0].rearrange("(k p) n -> p k n", p=P)

            def pairs(eng, body):
                for j in range(2):
                    body(j, j % 2, True, False)
                with eng.Fori(2, FT - 2, 2) as i:
                    for s in range(2):
                        body(i + s, s, False, False)
                for j in range(FT - 2, FT):
                    body(j, j % 2, False, True)

            @block.sync
            def _(sp):
                def load(j, g, wait):
                    if wait:
                        sp.wait_ge(up_lo, 2 * j + g - 1)
                    start = g * FF + j * P
                    sp.dma_start(up_raw[:, g], wup[:, :, bass.ds(start, P)]).then_inc(up_in[g], 16)

                for g in range(2):
                    load(0, g, False)
                with sp.Fori(1, FT) as j:
                    for g in range(2):
                        load(j, g, True)

            @block.tensor
            def _(pe):
                def body(j, s, first, final):
                    for g in range(2):
                        b = 4 * s + 2 * g
                        pe.wait_ge(up_lo, 2 * j + g + 1)
                        if not first:
                            pe.wait_ge(side_taps, 2 * (j - 2) + g + 1)
                        for k in range(KT):
                            for hh in range(2):
                                o, c_ = ps[:, b + hh, :], slice(hh * HALF, (hh + 1) * HALF)
                                pe.matmul(o, uph[:, g, k, :], hx[:, k, 0, c_], start=(k == 0), stop=False)
                                pe.matmul(o, uph[:, g, k, :], hx[:, k, 1, c_], start=False, stop=False)
                            for hh in range(2):
                                o, c_ = ps[:, b + hh, :], slice(hh * HALF, (hh + 1) * HALF)
                                last = pe.matmul(o, upl[:, g, k, :], hx[:, k, 0, c_], start=False, stop=(k == KT - 1))
                        last.then_inc(up_mm, 1)

                pairs(pe, body)

            def bank_pair(s, g):
                return ps[:, 4 * s + 2 * g:4 * s + 2 * g + 2, :].rearrange("p b n -> p (b n)")

            @block.scalar
            def _(act):
                def split(j, g, first):
                    act.wait_ge(up_in[g], 16 * (j + 1))
                    if not first:
                        act.wait_ge(up_mm, 2 * (j - 1) + g + 1)
                    act.activation(uph[:, g], up_raw[:, g], ACT.Copy).then_inc(up_hi, 1)

                def body(j, s, first, final, last=False):
                    for g in range(2):
                        if not last:
                            split(j + 1, g, False)
                        act.wait_ge(up_mm, 2 * j + g + 1)
                        act.wait_ge(cur_done, j + 1)
                        if not (first and s == 0):
                            act.wait_ge(hid_done, j)
                        act.activation(y[:, g, :], bank_pair(s, g), ACT.Identity, scale=ffcur[s][:, 4 * g + 1:4 * g + 2],
                                       bias=ffcur[s][:, 4 * g + 3:4 * g + 4]).then_inc(mid_tap, 1)
                    act.wait_ge(side_taps, 2 * j + 1)
                    act.activation(y[:, 0, :], y[:, 0, :], ACT.Silu).then_inc(act_done, 1)

                split(0, 0, True)
                split(0, 1, True)
                for j in range(2):
                    body(j, j % 2, True, False)
                with act.Fori(2, FT - 2, 2) as i:
                    for s in range(2):
                        body(i + s, s, False, False)
                body(FT - 2, 0, False, True)
                body(FT - 1, 1, False, True, last=True)

            @block.vector
            def _(dve):
                def split(j, g):
                    dve.wait_ge(up_hi, 2 * j + g + 1)
                    dve.tensor_tensor(out=upl[:, g], in0=up_raw[:, g], in1=f(uph[:, g]), op=ALU.subtract).then_inc(up_lo, 1)

                def body(j, s, first, final, last=False):
                    dve.tensor_scalar(ffcur[s].unsqueeze(1), ffs[:, bass.ds(j, 1), :], 1.0, None, ALU.mult).then_inc(cur_done, 1)
                    dve.wait_ge(cur_done, j + 1)
                    for g in range(2):
                        if not last:
                            split(j + 1, g)
                        p = bank_pair(s, g)
                        dve.wait_ge(mid_tap, 2 * j + g + 1)
                        dve.scalar_tensor_tensor(out=y[:, g, 1:T], in0=p[:, 0:T - 1], scalar=ffcur[s][:, 4 * g:4 * g + 1],
                                                 in1=y[:, g, 1:T], op0=ALU.mult, op1=ALU.add).then_inc(left_tap, 1)
                        dve.wait_ge(left_tap, 2 * j + g + 1)
                        dve.scalar_tensor_tensor(out=y[:, g, 0:T - 1], in0=p[:, 1:T], scalar=ffcur[s][:, 4 * g + 2:4 * g + 3],
                                                 in1=y[:, g, 0:T - 1], op0=ALU.mult, op1=ALU.add).then_inc(side_taps, 1)
                    dve.wait_ge(act_done, j + 1)
                    dve.wait_ge(side_taps, 2 * j + 2)
                    dve.tensor_tensor(out=hid[:, bass.ds(j, 1), :], in0=y[:, 0:1, :], in1=y[:, 1:2, :], op=ALU.mult).then_inc(hid_done, 1)

                split(0, 0)
                split(0, 1)
                for j in range(2):
                    body(j, j % 2, True, False)
                with dve.Fori(2, FT - 2, 2) as i:
                    for s in range(2):
                        body(i + s, s, False, False)
                body(FT - 2, 0, False, True)
                body(FT - 1, 1, False, True, last=True)

        dn_raw = at(106, "dn_raw", [P, 2, HALF])
        dnh = at(110, "dnh", [P, 2, HALF], F32R)
        dnl = at(114, "dnl", [P, 2, HALF], F32R)
        ah = at(118, "ah", [P, 2, T], F32R)
        al = at(126, "al", [P, 2, T], F32R)
        x1 = at(134, "x1", [P, TT, D])
        gout = at(166, "gout", [P, TT, HALF])
        with ExitStack() as s7:
            sem7 = lambda n: s7.enter_context(nc.semaphore(n))
            x1_in = sem7("x1_in")
            dn_in = [sem7("dn_in0"), sem7("dn_in1")]
            dn_hi, dn_lo, a_hi, a_lo, dn_mm, bank_mm, bank_out, res_done, stored = (
                sem7(n) for n in ("dn_hi", "dn_lo", "a_hi", "a_lo", "dn_mm", "bank_mm", "bank_out", "res_done", "stored"))
            block = s7.enter_context(nc.Block())

            def steps(eng, body):
                for half in range(2):
                    n0 = half * FT
                    for k in range(2):
                        body(n0 + k, k, half, k % 2, "first" if k == 0 else "peeled")
                    with eng.Fori(2, FT - 2, 2) as i:
                        for s in range(2):
                            body(i + (n0 + s), i + s, half, s, "loop")
                    for k in range(FT - 2, FT):
                        body(n0 + k, k, half, k % 2, "last" if k == FT - 1 else "loop")

            def early(kind, half):
                return half == 0 and kind in ("first", "peeled")

            @block.sync
            def _(sp):
                sp.dma_start(x1[:], x1_dram.rearrange("(t p) d -> p t d", p=P)).then_inc(x1_in, 16)

                def body(n, k, half, s, kind):
                    if not early(kind, half):
                        sp.wait_ge(dn_lo, n - 1)
                    sp.dma_start(dn_raw[:, s, :], w_down[0, bass.ds(k * P, P), half * HALF:(half + 1) * HALF]).then_inc(dn_in[s], 16)

                steps(sp, body)

            @block.tensor
            def _(pe):
                def body(n, k, half, s, kind):
                    pe.wait_ge(dn_lo, n + 1)
                    pe.wait_ge(a_lo, n + 1)
                    for t in range(TT):
                        if kind == "first" and half:
                            pe.wait_ge(bank_out, t + 1)
                        c_ = slice(t * P, (t + 1) * P)
                        pe.matmul(ps[:, t, :], ah[:, s, c_], dnh[:, s, :], start=(kind == "first"), stop=False)
                        pe.matmul(ps[:, t, :], ah[:, s, c_], dnl[:, s, :], start=False, stop=False)
                        last = pe.matmul(ps[:, t, :], al[:, s, c_], dnh[:, s, :], start=False, stop=(kind == "last"))
                        if kind == "last":
                            last.then_inc(bank_mm, 1)
                        elif t == TT - 1:
                            last.then_inc(dn_mm, 1)

                steps(pe, body)

            def wait_step_done(eng, n, half, kind, k):
                if early(kind, half):
                    return
                if half and kind in ("first", "peeled"):
                    if kind == "first":
                        eng.wait_ge(dn_mm, FT - 1)
                    else:
                        eng.wait_ge(bank_mm, TT)
                    return
                eng.wait_ge(dn_mm, n - 1 - half)

            @block.scalar
            def _(act):
                def body(n, k, half, s, kind):
                    act.wait_ge(dn_in[s], 8 * (n - s) + 16)
                    wait_step_done(act, n, half, kind, k)
                    act.activation(dnh[:, s, :], dn_raw[:, s, :], ACT.Copy).then_inc(dn_hi, 1)

                steps(act, body)

            @block.vector
            def _(dve):
                def drain(half):
                    for t in range(TT):
                        dve.wait_ge(bank_mm, half * TT + t + 1)
                        if half and t == 0:
                            dve.wait_ge(stored, 16 * TT)
                        dve.tensor_tensor(out=gout[:, t, :], in0=ps[:, t, :], in1=g2b[:, half * HALF:(half + 1) * HALF],
                                          op=ALU.mult).then_inc(bank_out, 1)

                def body(n, k, half, s, kind):
                    wait_step_done(dve, n, half, kind, k)
                    dve.tensor_scalar(ah[:, s:s + 1, :], hid[:, bass.ds(k, 1), :], 1.0, None, ALU.mult).then_inc(a_hi, 1)
                    dve.wait_ge(dn_hi, n + 1)
                    dve.tensor_tensor(out=dnl[:, s, :], in0=dn_raw[:, s, :], in1=f(dnh[:, s, :]), op=ALU.subtract).then_inc(dn_lo, 1)
                    dve.wait_ge(a_hi, n + 1)
                    dve.tensor_tensor(out=al[:, s:s + 1, :], in0=hid[:, bass.ds(k, 1), :], in1=f(ah[:, s:s + 1, :]),
                                      op=ALU.subtract).then_inc(a_lo, 1)

                for half in range(2):
                    n0 = half * FT
                    for k in range(2):
                        if half and k == 0:
                            body(n0, 0, 1, 0, "first")
                            drain(0)
                        else:
                            body(n0 + k, k, half, k % 2, "first" if k == 0 else "peeled")
                    with dve.Fori(2, FT - 2, 2) as i:
                        for s in range(2):
                            body(i + (n0 + s), i + s, half, s, "loop")
                    for k in range(FT - 2, FT):
                        body(n0 + k, k, half, k % 2, "last" if k == FT - 1 else "loop")
                drain(1)

            @block.gpsimd
            def _(pool):
                pool.wait_ge(x1_in, 16)
                for half in range(2):
                    for t in range(TT):
                        pool.wait_ge(bank_out, half * TT + t + 1)
                        v = gout[:, t, :]
                        pool.tensor_tensor(out=v, in0=v, in1=x1[:, t, half * HALF:(half + 1) * HALF], op=ALU.add).then_inc(res_done, 1)
                        pool.wait_ge(res_done, half * TT + t + 1)
                        pool.dma_start(out[0, t * P:(t + 1) * P, half * HALF:(half + 1) * HALF], v).then_inc(stored, 16)
                pool.wait_ge(stored, 2 * TT * 16)


def rope_table(np):
    axis = HD // 2
    inv = (np.float32(10000.0) ** (-np.arange(0, axis, 2, dtype=np.float32) / np.float32(axis))).astype(np.float32)
    pos = np.arange(T)
    ang_r = (pos // 64).astype(np.float32)[:, None] * inv
    ang_c = (pos % 64).astype(np.float32)[:, None] * inv
    sign = np.repeat(np.array([-1.0, 1.0, -1.0, 1.0], np.float32), axis // 2)
    ang = np.concatenate([ang_r, ang_r, ang_c, ang_c], axis=-1)
    return np.stack([np.cos(ang), np.sin(ang) * sign]).astype(np.float32)


INPUTS = ["x", "c", "ctx", "c_ctx", "w_mod", "b_mod", "norm_mix_w", "w_in", "q_norm_w", "k_norm_w", "sink_logit",
          "conv_w", "conv_b", "conv_norm_w", "conv_norm_b", "w_out", "norm_ffn_w", "w_up", "ffn_conv_w",
          "ffn_conv_b", "w_down"]


def kernel(**inputs):
    import numpy as np
    import concourse.bacc as bacc
    from concourse.bass_utils import run_bass_kernel_spmd

    nc = bacc.Bacc("TRN2", target_bir_lowering=False, num_devices=1)
    arrays, args = {}, []
    for name in INPUTS + ["rope"]:
        a = np.ascontiguousarray(rope_table(np) if name == "rope" else inputs[name])
        arrays[f"in_{name}"] = a
        args.append(nc.dram_tensor(f"in_{name}", a.shape, mybir.dt.from_np(a.dtype), kind="ExternalInput").ap())
    args.append(nc.dram_tensor("out_latent", (1, T, D), F32, kind="ExternalOutput").ap())
    build(nc, *args)
    result = run_bass_kernel_spmd(nc, [arrays], core_ids=[0])
    return result.results[0]["out_latent"]
```

```python
import math
from contextlib import ExitStack

import concourse.bass as bass
from concourse import mybir

F32 = mybir.dt.float32
F32R = mybir.dt.float32r
ALU = mybir.AluOpType
ACT = mybir.ActivationFunctionType
AX = mybir.AxisListType

P = 128
D = 1024
T = 1024
CTX = 256
KT = D // P
TT = T // P
CT = CTX // P
HALF = 512
HD = 64
NH = 8
NG = 2
GQ = NH // NG
QC = NH * HD
KVC = 2 * NG * HD
QKV = QC + KVC
CC = 512
CTL = CC // P
TAPS = 31
PAD = TAPS // 2
FF = 2816
FT = FF // P
EPS = 1e-6
SCALE = 1.0 / math.sqrt(HD)
MASKED = -1e30
KEYS = CTX + T

C_C, C_CTX, C_NMIX, C_NFFN, C_BMOD = 0, 8, 16, 24, 32
C_CONVB, C_CNW, C_CNB = 80, 84, 88
N_A = 92
C_FB, C_FW0 = N_A, N_A + FT * 2
C_FW1, C_FW2 = N_A + FT * 4, N_A + FT * 6
C_CONVW = N_A + FT * 8
N_COLS = C_CONVW + CTL * TAPS


class Memory:

    def __init__(self, nc, base):
        self.nc, self.base = nc, base

    def at(self, kib, name, shape, dt=F32):
        return self.nc.alloc_sbuf_tensor_at(name, shape, dt, offset=self.base + int(kib * 1024))


def build(nc, x, c, ctx, c_ctx, w_mod, b_mod, norm_mix_w, w_in, q_norm_w, k_norm_w, sink_logit,
          conv_w, conv_b, conv_norm_w, conv_norm_b, w_out, norm_ffn_w, w_up, ffn_conv_w,
          ffn_conv_b, w_down, rope, out):
    es = ExitStack()
    with es:
        mem = Memory(nc, 16512)
        at = mem.at
        ps = es.enter_context(nc.psum_tensor("ps", [P, 8, HALF], F32))
        x1_dram = nc.dram_tensor("x1_scratch", (T, D), F32, kind="Internal").ap()

        def sem(name):
            return es.enter_context(nc.semaphore(name))

        wo_in = [sem(f"wo_in{i}") for i in range(4)]
        up_in = [sem("up_in0"), sem("up_in1")]
        dn_in = [sem("dn_in0"), sem("dn_in1")]

        ident = at(0, "ident", [P, P])
        identr = at(0.5, "identr", [P, P], F32R)
        ones = at(1, "ones", [P, P])
        mask_prev = at(1.5, "mask_prev", [P, P], F32R)
        mask_next = at(2, "mask_next", [P, P], F32R)
        cols = at(2.5, "cols", [P, N_COLS])
        scal = at(4.25, "scal", [P, 256])
        g1b = at(5.5, "g1b", [P, D])
        g2b = at(9.5, "g2b", [P, D])
        ffs = at(13.5, "ffs", [P, FT, 8])
        meanw = at(14.5, "meanw", [P, P])
        maskf = at(15, "maskf", [P, 2, P])
        sinks = at(16, "sinks", [P, 2, NH])
        qkw = at(16.25, "qkw", [P, 2, HD])
        nat = scal[:, 0:16].rearrange("p (k two) -> p k two", two=2)
        ss = scal[:, 16:26]
        rst = scal[:, 26:36]
        modl = scal[:, 36:52]
        modc = scal[:, 52:68]
        A1, Ac = scal[:, 68:76], scal[:, 76:84]
        mod2 = scal[:, 84:100]
        A2 = scal[:, 100:108]
        ss2 = scal[:, 108:116]
        rs2 = scal[:, 116:124]
        ffcur = [scal[:, 128:136], scal[:, 136:144]]
        msq = at(16.75, "msq", [P, TT + CT, NH + NG])
        hx = at(143, "hx", [P, KT, 2, T], F32R)

        def f(ap):
            return ap.bitcast(F32)

        xs = at(18, "xs", [P, TT, D])
        xnT = at(50, "xnT", [P, KT, T])
        hc32 = at(18, "hc32", [P, KT, CTX])
        hcx = at(83, "hcx", [P, KT, 2, CTX], F32R)
        wm = at(99, "wm", [P, 3, 2 * D])
        junk = at(123, "junk", [P, D])
        cx = at(131, "cx", [P, CT, D])
        vecs = at(139, "vecs", [P, 4, P])
        NV = 3
        with ExitStack() as s1:
            sem1 = lambda n: s1.enter_context(nc.semaphore(n))
            vec_in, row_in = sem1("vec_in"), sem1("row_in")
            x_in = [sem1(f"x_in{t}") for t in range((TT + CT) // 2)]
            wm_in = [sem1(f"wm_in{i}") for i in range(NV)]
            const_step, const_done = sem1("const_step"), sem1("const_done")
            vecT, cols_done, silu_done = sem1("vecT"), sem1("cols_done"), sem1("silu_done")
            sq_done, ms_done, sqrt_done, rst_done = sem1("sq_done"), sem1("ms_done"), sem1("sqrt_done"), sem1("rst_done")
            xn_done, xT, xT_out = sem1("xn_done"), sem1("xT"), sem1("xT_out")
            mod_mm, mod_done, ab_done = sem1("mod_mm"), sem1("mod_done"), sem1("ab_done")
            h_mod, h_hi, h_lo = sem1("h_mod"), sem1("h_hi"), sem1("h_lo")
            hc_mod, hc_hi = sem1("hc_mod"), sem1("hc_hi")
            ffs_done = sem1("ffs_done")
            block = s1.enter_context(nc.Block())

            rows = lambda v, n: v.rearrange("(r q) -> r q", q=P)
            parts = [(0, C_C, 8, c[0]), (0, C_CTX, 8, c_ctx), (0, C_NMIX, 8, norm_mix_w[0]),
                     (0, C_NFFN, 8, norm_ffn_w[0]), (0, C_BMOD, 48, b_mod[0]), (0, C_CONVB, 4, conv_b[0]),
                     (0, C_CNW, 4, conv_norm_w[0]), (0, C_CNB, 4, conv_norm_b[0]),
                     (1, 0, 2 * FT, ffn_conv_b[0]), (1, 2 * FT, 2 * FT, ffn_conv_w[0, 0]),
                     (2, 0, 2 * FT, ffn_conv_w[0, 1]), (2, 2 * FT, 2 * FT, ffn_conv_w[0, 2])]
            vec_total = 16 * (len(parts) + 1)

            @block.sync
            def _(sp):
                for v, r0, n, src in parts:
                    sp.dma_start(vecs[r0:r0 + n, v, :], rows(src, n)).then_inc(vec_in, 16)
                sp.dma_start(vecs[0:TAPS * CTL, 3, :], conv_w[0].rearrange("w (r q) -> (w r) q", q=P)).then_inc(vec_in, 16)
                for k in range(KT):
                    if k >= NV:
                        sp.wait_ge(mod_mm, k - NV + 1)
                    sp.dma_start(wm[:, k % NV, :], w_mod[0, k * P:(k + 1) * P, 0:2 * D]).then_inc(wm_in[k % NV], 16)
                sp.dma_start(sinks[:, 0, :], sink_logit[0].partition_broadcast(P)).then_inc(row_in, 16)
                sp.dma_start(qkw[:, 0, :], q_norm_w[0].partition_broadcast(P)).then_inc(row_in, 16)
                sp.dma_start(qkw[:, 1, :], k_norm_w[0].partition_broadcast(P)).then_inc(row_in, 16)

            @block.gpsimd
            def _(pool):
                pool.memset(ident[:], 0.0).then_inc(const_step, 1)
                pool.memset(maskf[:], 0.0).then_inc(const_step, 1)
                pool.memset(ones[:], 1.0).then_inc(const_done, 1)
                pool.memset(meanw[:], 1.0 / CC).then_inc(const_done, 1)
                pool.wait_ge(const_step, 2)
                pool.affine_select(out=ident[:], in_=ident[:], compare_op=ALU.not_equal, fill=1.0, base=0,
                                   pattern=[[-1, P]], channel_multiplier=1).then_inc(const_done, 1)
                pool.affine_select(out=maskf[:, 0, :], in_=maskf[:, 0, :], compare_op=ALU.is_ge, fill=MASKED,
                                   base=0, pattern=[[1, P]], channel_multiplier=-1).then_inc(const_step, 1)
                pool.affine_select(out=maskf[:, 1, :], in_=maskf[:, 1, :], compare_op=ALU.is_ge, fill=MASKED,
                                   base=0, pattern=[[-1, P]], channel_multiplier=1).then_inc(const_step, 1)
                pool.wait_ge(const_done, 3)
                pool.tensor_copy(identr[:], ident[:]).then_inc(const_done, 1)
                pool.wait_ge(const_step, 4)
                pool.tensor_copy(mask_prev[:], maskf[:, 0, :]).then_inc(const_done, 1)
                pool.tensor_copy(mask_next[:], maskf[:, 1, :]).then_inc(const_done, 1)

            @block.tensor
            def _(pe):
                pe.wait_ge(const_done, 3)
                pe.wait_ge(vec_in, vec_total)
                off = 0
                for v, n in enumerate((N_A, 4 * FT, 4 * FT, TAPS * CTL)):
                    last = pe.transpose(ps[:, 7, off:off + n], vecs[0:n, v, :], ident[0:n, 0:n])
                    off += n
                last.then_inc(vecT, 1)

                def x_item(n):
                    hh, k = divmod(n, KT)
                    if n % KT == 0:
                        pe.wait_ge(xn_done, 4 * (hh + 1))
                    if n >= 7:
                        pe.wait_ge(xT_out, n - 6)
                    for t in range(4):
                        last = pe.transpose(ps[:, n % 7, t * P:(t + 1) * P], xs[:, 4 * hh + t, k * P:(k + 1) * P], ident[:])
                    last.then_inc(xT, 1)

                def mod_item(k):
                    pe.wait_ge(wm_in[k % NV], 16 * (k // NV + 1))
                    if k == 0:
                        pe.wait_ge(silu_done, 2)
                    for j in range(16):
                        last = pe.matmul(ps[:, 7, 2 * j:2 * j + 2], wm[:, k % NV, j * P:(j + 1) * P], nat[:, k, :],
                                         start=(k == 0 and j == 0), stop=(k == KT - 1), skip_group_check=True)
                    last.then_inc(mod_mm, 1)

                for k in range(4):
                    mod_item(k)
                for n in range(KT):
                    x_item(n)
                for k in range(4, KT):
                    mod_item(k)
                for n in range(KT, 2 * KT):
                    x_item(n)
                for n in range(2 * KT, 2 * KT + 4):
                    pe.wait_ge(xT_out, n - 6)
                    if n == 2 * KT:
                        pe.wait_ge(xn_done, TT + CT)
                    for kk in range(2):
                        for t in range(CT):
                            k = 2 * (n - 2 * KT) + kk
                            last = pe.transpose(ps[:, n % 7, (2 * kk + t) * P:(2 * kk + t + 1) * P],
                                                cx[:, t, k * P:(k + 1) * P], ident[:])
                    last.then_inc(xT, 1)

            @block.scalar
            def _(act):
                for t in range(TT):
                    act.dma_start(xs[:, t, :], x[0, t * P:(t + 1) * P, :]).then_inc(x_in[t // 2], 16)
                for t in range(CT):
                    act.dma_start(cx[:, t, :], ctx[0, t * P:(t + 1) * P, :]).then_inc(x_in[(TT + t) // 2], 16)
                act.wait_ge(cols_done, 1)
                act.activation(nat[:, :, 0], cols[:, C_C:C_C + KT], ACT.Silu).then_inc(silu_done, 1)
                act.activation(nat[:, :, 1], cols[:, C_CTX:C_CTX + KT], ACT.Silu).then_inc(silu_done, 1)
                for t in range(TT + CT):
                    act.wait_ge(x_in[t // 2], 32)
                    if t:
                        act.wait_ge(sq_done, t)
                    act.activation(junk[:], xs[:, t, :] if t < TT else cx[:, t - TT, :], ACT.Square,
                                   accum_out=ss[:, t:t + 1]).then_inc(sq_done, 1)
                act.wait_ge(ms_done, 1)
                act.activation(rst, ss, ACT.Sqrt).then_inc(sqrt_done, 1)
                for n in range(2 * KT):
                    hh, k = divmod(n, KT)
                    act.wait_ge(xT, n + 1)
                    act.activation(xnT[:, k, hh * HALF:(hh + 1) * HALF], ps[:, n % 7, :], ACT.Copy).then_inc(xT_out, 1)
                act.wait_ge(ab_done, 2)
                for n in range(4):
                    act.wait_ge(xT, 2 * KT + n + 1)
                    for kk in range(2):
                        k = 2 * n + kk
                        last = act.activation(hc32[:, k, :], ps[:, (2 * KT + n) % 7, kk * CTX:(kk + 1) * CTX], ACT.Identity,
                                              scale=Ac[:, k:k + 1], bias=modc[:, k:k + 1])
                        last.then_inc(hc_mod, 1)
                for k in range(KT):
                    act.wait_ge(h_mod, k + 1)
                    act.activation(hx[:, k, 0, :], xnT[:, k, :], ACT.Copy).then_inc(h_hi, 1)
                act.wait_ge(hc_mod, KT)
                act.activation(hcx[:, :, 0, :], hc32[:], ACT.Copy).then_inc(hc_hi, 1)

            @block.vector
            def _(dve):
                dve.wait_ge(vecT, 1)
                dve.tensor_copy(cols[:], ps[:, 7, 0:N_COLS]).then_inc(cols_done, 1)
                dve.wait_ge(sq_done, TT + CT)
                dve.tensor_scalar(ss, ss, 1.0 / D, EPS, ALU.mult, ALU.add).then_inc(ms_done, 1)
                dve.wait_ge(sqrt_done, 1)
                dve.reciprocal(rst, rst).then_inc(rst_done, 1)
                dve.wait_ge(rst_done, 1)
                for t in range(TT + CT):
                    v = xs[:, t, :] if t < TT else cx[:, t - TT, :]
                    dve.tensor_scalar(v, v, rst[:, t:t + 1], None, ALU.mult).then_inc(xn_done, 1)
                for i, c0 in enumerate((C_FW0, C_FW1, C_FW2, C_FB)):
                    for g in range(2):
                        dve.tensor_copy(ffs[:, :, 4 * g + i], cols[:, c0 + g * FT:c0 + (g + 1) * FT]).then_inc(ffs_done, 1)
                dve.wait_ge(row_in, 48)
                dve.tensor_scalar(sinks[:, 1, :], sinks[:, 0, :], -1.0, None, ALU.mult).then_inc(ffs_done, 1)
                dve.wait_ge(mod_mm, KT)
                m = ps[:, 7, 0:32].rearrange("p (j two) -> p j two", two=2)
                for i, dst in enumerate((modl, modc)):
                    dve.tensor_tensor(out=dst, in0=m[:, :, i], in1=cols[:, C_BMOD:C_BMOD + 16], op=ALU.add).then_inc(mod_done, 1)
                dve.wait_ge(mod_done, 2)
                for src, dst in ((modl, A1), (modc, Ac)):
                    dve.scalar_tensor_tensor(out=dst, in0=src[:, 8:16], scalar=1.0, in1=cols[:, C_NMIX:C_NMIX + KT],
                                             op0=ALU.add, op1=ALU.mult).then_inc(ab_done, 1)
                dve.wait_ge(ab_done, 2)
                dve.wait_ge(xT_out, 2 * KT)

                def low(k):
                    dve.wait_ge(h_hi, k + 1)
                    dve.tensor_tensor(out=hx[:, k, 1, :], in0=xnT[:, k, :], in1=f(hx[:, k, 0, :]), op=ALU.subtract).then_inc(h_lo, 1)

                for k in range(KT):
                    dve.tensor_scalar(xnT[:, k, :], xnT[:, k, :], A1[:, k:k + 1], modl[:, k:k + 1], ALU.mult, ALU.add).then_inc(h_mod, 1)
                    if k >= 1:
                        low(k - 1)
                low(KT - 1)
                dve.wait_ge(hc_hi, 1)
                dve.tensor_tensor(out=hcx[:, :, 1, :], in0=hc32[:], in1=f(hcx[:, :, 0, :]), op=ALU.subtract).then_inc(h_lo, 1)

        UW = T + 2 * PAD
        u = at(18, "u", [P, CTL, UW])
        cacc = at(34.75, "cacc", [P, CTL, T])
        qw_raw = at(75, "qw_raw", [P, 2, QKV])
        qwh = at(51, "qwh", [P, KT, QKV], F32R)
        qwl = at(119, "qwl", [P, KT, QKV], F32R)
        gw_raw = at(99, "gw_raw", [P, KT, P])
        gwh = at(103, "gwh", [P, 2, KT, P], F32R)
        gwl = at(111, "gwl", [P, 2, KT, P], F32R)
        qraw = at(83, "qraw", [P, TT, QC])
        kvraw = at(99, "kvraw", [P, CT + TT, KVC])
        ptmp = at(5.5, "ptmp", [P, T])
        POOL_CT = CTL - 2
        DVE_CT = [ct for ct in range(CTL) if ct != POOL_CT]
        NGL = 2 * CTL
        with ExitStack() as s2:
            sem2 = lambda n: s2.enter_context(nc.semaphore(n))
            gw_in, gw_hi, gw_lo, gl_mm = sem2("gw_in"), sem2("gw_hi"), sem2("gw_lo"), sem2("gl_mm")
            qw_in = [sem2("qw_in0"), sem2("qw_in1")]
            qw_hi, qw_lo, qkv_mm, qkv_out = sem2("qw_hi"), sem2("qw_lo"), sem2("qkv_mm"), sem2("qkv_out")
            pad_done, gate_done, u_done = sem2("pad_done"), sem2("gate_done"), sem2("u_done")
            tap_done, ptap_mul, ptap_add = sem2("tap_done"), sem2("ptap_mul"), sem2("ptap_add")
            block = s2.enter_context(nc.Block())
            win = w_in[0].rearrange("(k p) n -> p k n", p=P)

            def glu_col(n):
                return QKV + (CC if n % 2 == 0 else 0) + (n // 2) * P

            @block.sync
            def _(sp):
                for n in range(NGL):
                    if n:
                        sp.wait_ge(gw_lo, n)
                    sp.dma_start(gw_raw[:], win[:, :, glu_col(n):glu_col(n) + P]).then_inc(gw_in, 16)
                    if n >= 2:
                        sp.wait_ge(qw_lo, n - 1)
                    sp.dma_start(qw_raw[:, n % 2, :], w_in[0, n * P:(n + 1) * P, 0:QKV]).then_inc(qw_in[n % 2], 16)

            @block.tensor
            def _(pe):
                for n in range(NGL):
                    b = 2 * (n % 4)
                    pe.wait_ge(gw_lo, n + 1)
                    if n >= 4:
                        pe.wait_ge(u_done, (n - 4) // 2 + 1)
                    for k in range(KT):
                        for hh in range(2):
                            o, s = ps[:, b + hh, :], slice(hh * HALF, (hh + 1) * HALF)
                            pe.matmul(o, gwh[:, n % 2, k, :], hx[:, k, 0, s], start=(k == 0), stop=False)
                            pe.matmul(o, gwh[:, n % 2, k, :], hx[:, k, 1, s], start=False, stop=False)
                        for hh in range(2):
                            o, s = ps[:, b + hh, :], slice(hh * HALF, (hh + 1) * HALF)
                            last = pe.matmul(o, gwl[:, n % 2, k, :], hx[:, k, 0, s], start=False, stop=(k == KT - 1))
                    last.then_inc(gl_mm, 1)
                pe.wait_ge(qw_lo, KT)
                for m in range(CT + TT):
                    b = 2 * (m % 4)
                    pe.wait_ge(u_done, 3 if m < 2 else CTL)
                    if m >= 4:
                        pe.wait_ge(qkv_out, m - 3)
                    for k in range(KT):
                        if m < CT:
                            h = [hcx[:, k, v, m * P:(m + 1) * P] for v in range(2)]
                        else:
                            h = [hx[:, k, v, (m - CT) * P:(m - CT + 1) * P] for v in range(2)]
                        for v in range(2):
                            for lo in range(2 - v):
                                w = (qwh, qwl)[lo]
                                first, end = (k == 0 and v == 0 and lo == 0), (k == KT - 1 and v == 1)
                                if m >= CT:
                                    pe.matmul(ps[:, b, :], h[v], w[:, k, 0:QC], start=first, stop=end)
                                last = pe.matmul(ps[:, b + 1, 0:KVC], h[v], w[:, k, QC:QKV], start=first, stop=end)
                    last.then_inc(qkv_mm, 1)

            @block.scalar
            def _(act):
                def split_glu(n):
                    act.wait_ge(gw_in, 16 * (n + 1))
                    if n >= 2:
                        act.wait_ge(gl_mm, n - 1)
                    act.activation(gwh[:, n % 2], gw_raw[:], ACT.Copy).then_inc(gw_hi, 1)

                def split_qkv(k):
                    act.wait_ge(qw_in[k % 2], 16 * (k // 2 + 1))
                    act.activation(qwh[:, k, :], qw_raw[:, k % 2, :], ACT.Copy).then_inc(qw_hi, 1)

                split_glu(0)
                split_qkv(0)
                split_glu(1)
                split_qkv(1)
                act.wait_ge(pad_done, 1)
                for n in range(NGL):
                    act.wait_ge(gl_mm, n + 1)
                    if n % 2 == 0:
                        ct, b = n // 2, 2 * (n % 4)
                        act.activation(u[:, ct, PAD:PAD + T], ps[:, b:b + 2, :].rearrange("p b n -> p (b n)"),
                                       ACT.Sigmoid).then_inc(gate_done, 1)
                    if n + 2 < NGL:
                        split_glu(n + 2)
                        split_qkv(n + 2)
                for m in range(CT + TT):
                    b = 2 * (m % 4)
                    act.wait_ge(qkv_mm, m + 1)
                    if m >= CT:
                        act.activation(qraw[:, m - CT, :], ps[:, b, :], ACT.Copy)
                    act.activation(kvraw[:, m, :], ps[:, b + 1, 0:KVC], ACT.Copy).then_inc(qkv_out, 1)

            @block.gpsimd
            def _(pool):
                pool.memset(u[:], 0.0).then_inc(pad_done, 1)
                ct = POOL_CT
                pool.wait_ge(u_done, ct + 1)
                for i in range(TAPS):
                    w = cols[:, C_CONVW + i * CTL + ct:C_CONVW + i * CTL + ct + 1]
                    if i == 0:
                        pool.tensor_scalar(cacc[:, ct, :], u[:, ct, 0:T], w, cols[:, C_CONVB + ct:C_CONVB + ct + 1],
                                           ALU.mult, ALU.add).then_inc(ptap_add, 1)
                        continue
                    if i > 1:
                        pool.wait_ge(ptap_add, i)
                    pool.tensor_scalar(ptmp[:], u[:, ct, i:i + T], w, 1.0, ALU.mult, ALU.mult).then_inc(ptap_mul, 1)
                    pool.wait_ge(ptap_mul, i)
                    pool.wait_ge(ptap_add, i)
                    pool.tensor_tensor(out=cacc[:, ct, :], in0=cacc[:, ct, :], in1=ptmp[:], op=ALU.add).then_inc(ptap_add, 1)

            @block.vector
            def _(dve):
                def split_glu(n):
                    dve.wait_ge(gw_hi, n + 1)
                    dve.tensor_tensor(out=gwl[:, n % 2], in0=gw_raw[:], in1=f(gwh[:, n % 2]), op=ALU.subtract).then_inc(gw_lo, 1)

                def split_qkv(k):
                    dve.wait_ge(qw_hi, k + 1)
                    dve.tensor_tensor(out=qwl[:, k, :], in0=qw_raw[:, k % 2, :], in1=f(qwh[:, k, :]), op=ALU.subtract).then_inc(qw_lo, 1)

                done = [0]

                def taps(count):
                    for _ in range(count):
                        if done[0] == len(DVE_CT) * TAPS:
                            return
                        ct, i = DVE_CT[done[0] // TAPS], done[0] % TAPS
                        w = cols[:, C_CONVW + i * CTL + ct:C_CONVW + i * CTL + ct + 1]
                        if i == 0:
                            dve.wait_ge(u_done, ct + 1)
                            ins = dve.tensor_scalar(cacc[:, ct, :], u[:, ct, 0:T], w, cols[:, C_CONVB + ct:C_CONVB + ct + 1],
                                                    ALU.mult, ALU.add)
                        else:
                            dve.wait_ge(tap_done, done[0])
                            ins = dve.scalar_tensor_tensor(out=cacc[:, ct, :], in0=u[:, ct, i:i + T], scalar=w,
                                                           in1=cacc[:, ct, :], op0=ALU.mult, op1=ALU.add)
                        ins.then_inc(tap_done, 1)
                        done[0] += 1

                for n in range(2):
                    split_glu(n)
                    split_qkv(n)
                for n in range(NGL):
                    if n + 2 < NGL:
                        split_glu(n + 2)
                        split_qkv(n + 2)
                    if n % 2 == 1:
                        ct, b = n // 2, 2 * (n % 4)
                        dve.wait_ge(gate_done, ct + 1)
                        dve.wait_ge(gl_mm, n + 1)
                        dve.tensor_tensor(out=u[:, ct, PAD:PAD + T], in0=ps[:, b:b + 2, :].rearrange("p b n -> p (b n)"),
                                          in1=u[:, ct, PAD:PAD + T], op=ALU.mult).then_inc(u_done, 1)
                    if n:
                        taps(7)
                taps(len(DVE_CT) * TAPS)

        NK = CT + TT
        tabs = at(18, "tabs", [P, 4, TT, HD])
        qst = [at(26, "qst0", [P, NH, 2, HD], F32R), at(139, "qst1", [P, NH, 2, HD], F32R)]
        cs = at(30, "cs", [P, 2, TT, HD])
        qT = at(51, "qT", [P, NH, T], F32R)
        ka = at(129, "ka", [P, NK, NG, HD])
        kb = at(134, "kb", [P, NK, NG, HD])
        kst = at(143, "kst", [P, NK, NG, 2, P], F32R)
        sqq = at(163, "sqq", [P, 2, QC])
        qa = at(167, "qa", [P, 2, QC])
        qb = at(171, "qb", [P, 2, QC])
        kT = at(109, "kT", [P, NG, 2, KEYS], F32R)
        ko = at(195, "ko", [P, NK, NG, HD])
        sqk = at(200, "sqk", [P, NK, NG, HD])
        kraw = kvraw[:, :, 0:NG * HD].rearrange("p t (g d) -> p t g d", g=NG)
        vraw = kvraw[:, :, NG * HD:KVC].rearrange("p t (g d) -> p t g d", g=NG)
        with ExitStack() as s3:
            sem3 = lambda n: s3.enter_context(nc.semaphore(n))
            cs_in, tab_done, sq_k, sq_q, sum_done = sem3("cs_in"), sem3("tab_done"), sem3("sq_k"), sem3("sq_q"), sem3("sum_done")
            ms3, sqrt3, rs3 = sem3("ms3"), sem3("sqrt3"), sem3("rs3")
            k_norm, k_mul, k_rot, k_hi, k_lo = sem3("k_norm"), sem3("k_mul"), sem3("k_rot"), sem3("k_hi"), sem3("k_lo")
            q_norm, q_sin, q_cos, q_rot, q_hi, q_lo = (sem3(n) for n in ("q_norm", "q_sin", "q_cos", "q_rot", "q_hi", "q_lo"))
            qkT, qkT_out = sem3("qkT"), sem3("qkT_out")
            block = s3.enter_context(nc.Block())
            h3 = lambda ap: ap.rearrange("p (h d) -> p h d", h=NH)

            @block.sync
            def _(sp):
                sp.dma_start(cs[:], rope.rearrange("w (t p) d -> p w t d", p=P)).then_inc(cs_in, 16)

            @block.scalar
            def _(act):
                act.activation(sqk[:], kraw, ACT.Square).then_inc(sq_k, 1)
                for t in range(TT):
                    if t >= 2:
                        act.wait_ge(sum_done, t)
                    act.activation(sqq[:, t % 2, :], qraw[:, t, :], ACT.Square).then_inc(sq_q, 1)
                act.wait_ge(ms3, 1)
                act.activation(msq[:], msq[:], ACT.Sqrt).then_inc(sqrt3, 1)
                act.wait_ge(k_rot, 2)
                for r in range(2):
                    act.activation(kst[:, :, :, 0, r * HD:(r + 1) * HD], ko[:], ACT.Copy).then_inc(k_hi, 1)

                def q_high(t):
                    act.wait_ge(q_rot, t + 1)
                    if t >= 2:
                        act.wait_ge(qkT, NK + 2 * (t - 1))
                    act.activation(qst[t % 2][:, :, 0, :], h3(qa[:, t % 2, :]), ACT.Copy).then_inc(q_hi, 1)

                q_high(0)
                for n in range(NK):
                    act.wait_ge(qkT, n + 1)
                    act.activation(kT[:, :, :, n * P:(n + 1) * P],
                                   ps[:, n % 8, :].rearrange("p (g v k) -> p g v k", g=NG, v=2), ACT.Copy).then_inc(qkT_out, 1)
                for t in range(TT):
                    if t + 1 < TT:
                        q_high(t + 1)
                    for hh in range(2):
                        n = NK + 2 * t + hh
                        act.wait_ge(qkT, n + 1)
                        act.activation(qT[:, 4 * hh:4 * hh + 4, t * P:(t + 1) * P],
                                       ps[:, n % 8, :].rearrange("p (h k) -> p h k", h=4), ACT.Copy).then_inc(qkT_out, 1)

            @block.gpsimd
            def _(pool):
                for t in range(TT):
                    pool.wait_ge(q_norm, t + 1)
                    if t >= 2:
                        pool.wait_ge(q_rot, t - 1)
                    a4 = qa[:, t % 2, :].rearrange("p (e x d) -> p e x d", e=2 * NH, x=2)
                    b4 = qb[:, t % 2, :].rearrange("p (e x d) -> p e x d", e=2 * NH, x=2)
                    sn = tabs[:, 1, t, :].rearrange("p (a x d) -> p a x d", a=2, x=2)
                    for half in range(2):
                        for a in range(2):
                            last = pool.tensor_tensor(out=b4[:, a::2, half, :], in0=a4[:, a::2, 1 - half, :],
                                                      in1=sn[:, a:a + 1, half, :].to_broadcast([P, NH, 16]), op=ALU.mult)
                            last.then_inc(q_sin, 1)

            @block.vector
            def _(dve):
                dve.wait_ge(cs_in, 16)
                sn = cs[:, 1].rearrange("p t (a x d) -> p t a x d", a=2, x=2)
                for i in range(2):
                    dve.tensor_tensor(out=tabs[:, 2 * i], in0=cs[:, 0], in1=qkw[:, i:i + 1, :].to_broadcast([P, TT, HD]),
                                      op=ALU.mult).then_inc(tab_done, 1)
                    w4 = qkw[:, i, :].rearrange("p (a x d) -> p a x d", a=2, x=2)
                    dst = tabs[:, 2 * i + 1].rearrange("p t (a x d) -> p t a x d", a=2, x=2)
                    for half in range(2):
                        for a in range(2):
                            dve.tensor_tensor(out=dst[:, :, a, half, :], in0=sn[:, :, a, half, :],
                                              in1=w4[:, a:a + 1, 1 - half, :].to_broadcast([P, TT, 16]), op=ALU.mult).then_inc(tab_done, 1)
                for m in range(CT):
                    dve.memset(msq[:, m, 0:NH], 1.0).then_inc(tab_done, 1)
                dve.wait_ge(sq_k, 1)
                dve.tensor_reduce(out=msq[:, :, NH:NH + NG], in_=sqk[:], axis=AX.X, op=ALU.add).then_inc(sum_done, 1)
                for t in range(TT):
                    dve.wait_ge(sq_q, t + 1)
                    dve.tensor_reduce(out=msq[:, CT + t, 0:NH], in_=h3(sqq[:, t % 2, :]), axis=AX.X, op=ALU.add).then_inc(sum_done, 1)
                dve.wait_ge(tab_done, 12)
                dve.wait_ge(sum_done, TT + 1)
                dve.tensor_scalar(msq[:], msq[:], 1.0 / HD, EPS, ALU.mult, ALU.add).then_inc(ms3, 1)
                dve.wait_ge(sqrt3, 1)
                dve.reciprocal(msq[:], msq[:]).then_inc(rs3, 1)
                dve.wait_ge(rs3, 1)
                dve.tensor_tensor(out=ka[:], in0=kraw, in1=msq[:, :, NH:NH + NG].unsqueeze(3).to_broadcast([P, NK, NG, HD]),
                                  op=ALU.mult).then_inc(k_norm, 1)

                def q_normed(t):
                    if t >= 2:
                        dve.wait_ge(q_lo, t - 1)
                    dve.tensor_tensor(out=h3(qa[:, t % 2, :]), in0=h3(qraw[:, t, :]),
                                      in1=msq[:, CT + t, 0:NH].unsqueeze(2).to_broadcast([P, NH, HD]), op=ALU.mult).then_inc(q_norm, 1)

                q_normed(0)
                q_normed(1)
                dve.wait_ge(k_norm, 1)
                dve.tensor_tensor(out=ko[:, 0:CT], in0=ka[:, 0:CT], in1=qkw[:, 1:2, :].unsqueeze(1).to_broadcast([P, CT, NG, HD]),
                                  op=ALU.mult).then_inc(k_rot, 1)
                dve.tensor_tensor(out=ko[:, CT:], in0=ka[:, CT:], in1=tabs[:, 2].unsqueeze(2).to_broadcast([P, TT, NG, HD]),
                                  op=ALU.mult).then_inc(k_mul, 1)
                ka5 = ka[:].rearrange("p t g (a x d) -> p t g a x d", a=2, x=2)
                kb5 = kb[:].rearrange("p t g (a x d) -> p t g a x d", a=2, x=2)
                sk = tabs[:, 3].rearrange("p t (a x d) -> p t a x d", a=2, x=2)
                for g in range(NG):
                    for half in range(2):
                        dve.tensor_tensor(out=kb5[:, CT:, g, :, half, :], in0=ka5[:, CT:, g, :, 1 - half, :], in1=sk[:, :, :, half, :],
                                          op=ALU.mult).then_inc(k_mul, 1)
                dve.wait_ge(k_mul, 5)
                dve.tensor_tensor(out=ko[:, CT:], in0=ko[:, CT:], in1=kb[:, CT:], op=ALU.add).then_inc(k_rot, 1)

                def q_rotate(t):
                    dve.wait_ge(q_sin, 4 * (t + 1))
                    dve.tensor_tensor(out=h3(qa[:, t % 2, :]), in0=h3(qa[:, t % 2, :]), in1=tabs[:, 0, t:t + 1, :].to_broadcast([P, NH, HD]),
                                      op=ALU.mult).then_inc(q_cos, 1)
                    dve.wait_ge(q_cos, t + 1)
                    dve.tensor_tensor(out=qa[:, t % 2, :], in0=qa[:, t % 2, :], in1=qb[:, t % 2, :], op=ALU.add).then_inc(q_rot, 1)

                q_rotate(0)
                for r in range(2):
                    dve.wait_ge(k_hi, r + 1)
                    dve.tensor_tensor(out=kst[:, :, :, 1, r * HD:(r + 1) * HD], in0=ko[:], in1=f(kst[:, :, :, 0, r * HD:(r + 1) * HD]),
                                      op=ALU.subtract).then_inc(k_lo, 1)
                for t in range(TT):
                    dve.wait_ge(q_hi, t + 1)
                    dve.tensor_tensor(out=qst[t % 2][:, :, 1, :], in0=h3(qa[:, t % 2, :]), in1=f(qst[t % 2][:, :, 0, :]),
                                      op=ALU.subtract).then_inc(q_lo, 1)
                    if t + 2 < TT:
                        q_normed(t + 2)
                    if t + 1 < TT:
                        q_rotate(t + 1)

            @block.tensor
            def _(pe):
                pe.wait_ge(k_lo, 2)
                for n in range(NK + 2 * TT):
                    if n >= 8:
                        pe.wait_ge(qkT_out, n - 7)
                    if n < NK:
                        src = [kst[:, n, j // 2, j % 2, :] for j in range(4)]
                    else:
                        t, hh = divmod(n - NK, 2)
                        pe.wait_ge(q_lo, t + 1)
                        src = [qst[t % 2][:, 4 * hh + j].rearrange("p v d -> p (v d)") for j in range(4)]
                    for j in range(4):
                        last = pe.transpose(ps[:, n % 8, j * P:(j + 1) * P].bitcast(F32R), src[j], identr[:])
                    last.then_inc(qkT, 1)

        SW = CTX + 3 * P
        NGRP = 2 * TT
        NPT = 3
        NW = 4
        wm2 = at(18, "wm2", [P, NW, D])
        pbuf = [at(129, "p0", [P, GQ, SW]), at(83, "p1", [P, GQ, SW])]
        pt = at(93, "pt", [P, NPT, HALF])
        on = at(15, "on", [P, GQ * HD])
        sqc = at(175, "sqc", [P, CTL, T])
        rstd = at(191, "rstd", [P, T])
        shift2, scale2 = at(195, "shift2", [P, D]), at(199, "scale2", [P, D])
        st = [scal[:, 144 + 16 * i:160 + 16 * i].rearrange("p (s h) -> p s h", s=4) for i in range(2)]
        wo_raw = at(18, "wo_raw", [P, 4, D])

        def key_tiles(i):
            return [0, 1] + [CT + j for j in (i - 1, i, i + 1) if 0 <= j < TT]

        first_item = [0]
        for n in range(NGRP):
            first_item.append(first_item[-1] + len(key_tiles(n // NG)))
        SECTIONS = [(2, g1b), (3, shift2), (4, scale2), (5, g2b)]
        NMOD = len(SECTIONS) * KT
        with ExitStack() as s4:
            sem4 = lambda n: s4.enter_context(nc.semaphore(n))
            wm2_in = [sem4(f"wm2_in{i}") for i in range(NW)]
            zero_done, brow_in, mod_mul, mod_acc, row_mm, row_out = (
                sem4(n) for n in ("zero_done", "brow_in", "mod_mul", "mod_acc", "row_mm", "row_out"))
            col_mm, col_add, a2_done = sem4("col_mm"), sem4("col_add"), sem4("a2_done")
            qk_mm, max_done, negm_done, exp_done = sem4("qk_mm"), sem4("max_done"), sem4("negm_done"), sem4("exp_done")
            arg_done, sexp_done, den_done, rec_done = (sem4(n) for n in ("arg_done", "sexp_done", "den_done", "rec_done"))
            pt_T, pt_out, pv_mm, on_done, oT, o_hi, o_lo = (sem4(n) for n in ("pt_T", "pt_out", "pv_mm", "on_done", "oT", "o_hi", "o_lo"))
            mean_mm, cent, sq5, var_mm, eps_done, sqrt5, rec5, scaled, silu5, u_hi, u_lo = (
                sem4(n) for n in ("mean_mm", "cent", "sq5", "var_mm", "eps_done", "sqrt5", "rec5", "scaled", "silu5", "u_hi", "u_lo"))
            block = s4.enter_context(nc.Block())
            half = lambda hh: slice(hh * HALF, (hh + 1) * HALF)

            @block.sync
            def _(sp):
                for n in range(NMOD):
                    if n >= NW:
                        sp.wait_ge(mod_acc, n - NW + 1)
                    sec, k = SECTIONS[n // KT][0], n % KT
                    sp.dma_start(wm2[:, n % NW, :], w_mod[0, k * P:(k + 1) * P, sec * D:(sec + 1) * D]).then_inc(wm2_in[n % NW], 16)
                    if n == NW - 1:
                        sp.wait_ge(zero_done, 2)
                        for sec, dst in (SECTIONS[0], SECTIONS[3]):
                            sp.dma_start(dst[0:1, :], b_mod[0:1, sec * D:(sec + 1) * D]).then_inc(brow_in, 16)
                for k in range(4):
                    sp.wait_ge(mod_acc, NMOD - 3 + k)
                    sp.dma_start(wo_raw[:, k, :], w_out[0, k * P:(k + 1) * P, :]).then_inc(wo_in[k], 16)

            @block.gpsimd
            def _(pool):
                for dst in (g1b, g2b):
                    pool.memset(dst[:], 0.0).then_inc(zero_done, 1)
                muls = 0
                for n in range(NMOD):
                    k, dst, w = n % KT, SECTIONS[n // KT][1], wm2[:, n % NW, :]
                    pool.wait_ge(wm2_in[n % NW], 16 * (n // NW + 1))
                    if n == 3 * KT:
                        pool.wait_ge(rec5, 4)
                        for ct in range(CTL):
                            pool.tensor_tensor(out=cacc[:, ct, :], in0=cacc[:, ct, :], in1=rstd[:], op=ALU.mult).then_inc(scaled, 1)
                    if k == 0 and dst in (shift2, scale2):
                        pool.tensor_scalar(dst[:], w, nat[:, k, 0:1], 1.0, ALU.mult, ALU.mult).then_inc(mod_acc, 1)
                        continue
                    pool.tensor_scalar(w, w, nat[:, k, 0:1], 1.0, ALU.mult, ALU.mult).then_inc(mod_mul, 1)
                    muls += 1
                    pool.wait_ge(mod_mul, muls)
                    if n == 0:
                        pool.wait_ge(brow_in, 32)
                    else:
                        pool.wait_ge(mod_acc, n)
                    pool.tensor_tensor(out=dst[:], in0=dst[:], in1=w, op=ALU.add).then_inc(mod_acc, 1)

            def head_steps(n):
                i, g = divmod(n, NG)
                return i, g, key_tiles(i)

            @block.tensor
            def _(pe):
                def scores(n, hl):
                    i, g, kts = head_steps(n)
                    hh = GQ * n + hl
                    b = 2 * (hh % 2)
                    if hh >= 2:
                        pe.wait_ge(exp_done, hh - 1)
                    q = qT[:, GQ * g + hl, i * P:(i + 1) * P]
                    lat = kts[2] * P
                    pe.matmul(ps[:, b, 0:CTX], q, kT[:, g, 0, 0:CTX], start=True, stop=False)
                    pe.matmul(ps[:, b, 0:CTX], q, kT[:, g, 1, 0:CTX], start=False, stop=True)
                    o = ps[:, b, CTX:CTX + 2 * P]
                    pe.matmul(o, q, kT[:, g, 0, lat:lat + 2 * P], start=True, stop=False)
                    last = pe.matmul(o, q, kT[:, g, 1, lat:lat + 2 * P], start=False, stop=False)
                    if i > 0:
                        last = pe.matmul(ps[:, b, CTX:CTX + P], identr[:], mask_prev[:], start=False, stop=True)
                    else:
                        last = pe.matmul(ps[:, b, CTX + P:CTX + 2 * P], identr[:], mask_next[:], start=False, stop=True)
                    if 0 < i < TT - 1:
                        o = ps[:, b + 1, 0:P]
                        pe.matmul(o, q, kT[:, g, 0, lat + 2 * P:lat + 3 * P], start=True, stop=False)
                        pe.matmul(o, q, kT[:, g, 1, lat + 2 * P:lat + 3 * P], start=False, stop=False)
                        last = pe.matmul(o, identr[:], mask_next[:], start=False, stop=True)
                    last.then_inc(qk_mm, 1)

                def turn(n, j):
                    it = first_item[n] + j
                    if j == 0:
                        pe.wait_ge(exp_done, GQ * (n + 1))
                    if it >= 2:
                        pe.wait_ge(pt_out, it - 1)
                    for hl in range(GQ):
                        last = pe.transpose(ps[:, 4 + it % 2, hl * P:(hl + 1) * P], pbuf[n % 2][:, hl, j * P:(j + 1) * P], ident[:])
                    last.then_inc(pt_T, 1)

                def values(n, j):
                    i, g, kts = head_steps(n)
                    it = first_item[n] + j
                    if j == 0 and n:
                        pe.wait_ge(on_done, n)
                    pe.wait_ge(pt_out, it + 1)
                    for hl in range(GQ):
                        last = pe.matmul(ps[:, 6, hl * HD:(hl + 1) * HD], pt[:, it % NPT, hl * P:(hl + 1) * P], vraw[:, kts[j], g, :],
                                         start=(j == 0 and hl == 0), stop=(j == len(kts) - 1), skip_group_check=True)
                    last.then_inc(pv_mm, 1)

                def turn_outputs(n):
                    pe.wait_ge(on_done, n + 1)
                    bank_read(n + 1)
                    for r in range(2):
                        last = pe.transpose(ps[:, 7, r * P:(r + 1) * P], on[:, r * P:(r + 1) * P], ident[:])
                    last.then_inc(oT, 1)

                def mean_of(buf, hh, signal):
                    for ct in range(CTL):
                        last = pe.matmul(ps[:, 7, :], meanw[:], buf[:, ct, half(hh)], start=(ct == 0), stop=(ct == CTL - 1))
                    last.then_inc(signal, 1)

                def beside(n):
                    if n >= 2:
                        pe.wait_ge(o_lo, n - 1)
                    if n in (0, 1):
                        if n:
                            pe.wait_ge(cent, CTL)
                        mean_of(cacc, n, mean_mm)
                    elif n in (2, 3):
                        pe.wait_ge(sq5, CTL * (n - 1))
                        mean_of(sqc, n - 2, var_mm)

                def bank_read(n):
                    if n in (0, 1):
                        pe.wait_ge(cent, CTL * (n + 1))
                    elif n in (2, 3):
                        pe.wait_ge(eps_done, n - 1)
                    if n >= 2:
                        pe.wait_ge(o_lo, n - 1)

                for hl in range(GQ):
                    scores(0, hl)
                for n in range(NGRP):
                    m = len(key_tiles(n // NG))
                    for j in range(m):
                        if n + 1 < NGRP and j < GQ:
                            scores(n + 1, j)
                        turn(n, j)
                        if j == 1 and n < 4:
                            beside(n)
                        if j == 3 and n:
                            turn_outputs(n - 1)
                        if j:
                            values(n, j - 1)
                    values(n, m - 1)
                for c, dst in enumerate((shift2, scale2)):
                    pe.wait_ge(mod_acc, (2 + c) * KT)
                    pe.wait_ge(pt_out, first_item[NGRP])
                    for j in range(KT):
                        last = pe.matmul(ps[:, 4, c * KT + j:c * KT + j + 1], dst[:, j * P:(j + 1) * P], ones[:, 0:1], start=True, stop=True)
                last.then_inc(col_mm, 1)
                pe.wait_ge(mod_acc, NMOD)
                for r in range(2):
                    for hh in range(2):
                        pe.matmul(ps[:, 2 * r + hh, :], ones[:], (g1b, g2b)[r][:, half(hh)], start=True, stop=True).then_inc(row_mm, 1)
                turn_outputs(NGRP - 1)

            def score_ap(hh, w):
                b = 2 * (hh % 2)
                return ps[:, b:b + 2, :].rearrange("p b n -> p (b n)")[:, 0:w]

            @block.scalar
            def _(act):
                def exps(n, hl):
                    hh = GQ * n + hl
                    w = P * len(key_tiles(n // NG))
                    act.wait_ge(negm_done, hh + 1)
                    if hl == 0 and n >= 2:
                        act.wait_ge(pt_T, first_item[n - 1])
                    act.activation(pbuf[n % 2][:, hl, 0:w], score_ap(hh, w), ACT.Exp, scale=SCALE,
                                   bias=st[n % 2][:, 1, hl:hl + 1], accum_out=st[n % 2][:, 2, hl:hl + 1]).then_inc(exp_done, 1)

                def output_high(n):
                    i, g = divmod(n, NG)
                    act.wait_ge(oT, n + 1)
                    act.activation(hx[:, 2 * g:2 * g + 2, 0, i * P:(i + 1) * P],
                                   ps[:, 7, 0:2 * P].rearrange("p (r q) -> p r q", r=2), ACT.Copy).then_inc(o_hi, 1)

                def beside(n):
                    if n in (0, 1):
                        hh = n
                        for ct in range(CTL):
                            act.wait_ge(cent, CTL * hh + ct + 1)
                            act.activation(sqc[:, ct, half(hh)], cacc[:, ct, half(hh)], ACT.Square).then_inc(sq5, 1)
                    elif n == 4:
                        act.wait_ge(eps_done, 2)
                        act.activation(rstd[:], rstd[:], ACT.Sqrt).then_inc(sqrt5, 1)

                for hl in range(GQ):
                    exps(0, hl)
                for n in range(NGRP):
                    i, g, kts = head_steps(n)
                    act.wait_ge(arg_done, n + 1)
                    act.activation(st[n % 2][:, 3, :], st[n % 2][:, 3, :], ACT.Exp).then_inc(sexp_done, 1)
                    for j in range(len(kts)):
                        it = first_item[n] + j
                        act.wait_ge(pt_T, it + 1)
                        if it >= NPT:
                            act.wait_ge(pv_mm, it - NPT + 1)
                        act.activation(pt[:, it % NPT, :], ps[:, 4 + it % 2, :], ACT.Copy).then_inc(pt_out, 1)
                        if n + 1 < NGRP and j < GQ:
                            exps(n + 1, j)
                        if j == 3 and n:
                            output_high(n - 1)
                    beside(n)
                act.wait_ge(var_mm, 2)
                for ct in range(CTL):
                    act.wait_ge(scaled, CTL)
                    act.activation(cacc[:, ct, :], cacc[:, ct, :], ACT.Silu, scale=cols[:, C_CNW + ct:C_CNW + ct + 1],
                                   bias=cols[:, C_CNB + ct:C_CNB + ct + 1]).then_inc(silu5, 1)
                output_high(NGRP - 1)
                for ct in range(CTL):
                    act.wait_ge(silu5, ct + 1)
                    act.activation(hx[:, CTL + ct, 0, :], cacc[:, ct, :], ACT.Copy).then_inc(u_hi, 1)
                    r, hh = divmod(ct, 2)
                    act.wait_ge(row_mm, 4)
                    act.activation((g1b, g2b)[r][:, half(hh)], ps[:, 2 * r + hh, :], ACT.Copy).then_inc(row_out, 1)

            @block.vector
            def _(dve):
                def maxima(n, hl):
                    hh = GQ * n + hl
                    w = P * len(key_tiles(n // NG))
                    s = st[n % 2]
                    dve.wait_ge(qk_mm, hh + 1)
                    dve.reduce_max(s[:, 0, hl:hl + 1], score_ap(hh, w), axis=AX.X).then_inc(max_done, 1)
                    dve.wait_ge(max_done, hh + 1)
                    h = GQ * (n % NG) + hl
                    dve.tensor_scalar(s[:, 1, hl:hl + 1], s[:, 0, hl:hl + 1], -SCALE, sinks[:, 1, h:h + 1],
                                      ALU.mult, ALU.min).then_inc(negm_done, 1)

                def output_low(n):
                    i, g = divmod(n, NG)
                    dve.wait_ge(o_hi, n + 1)
                    dve.tensor_tensor(out=hx[:, 2 * g:2 * g + 2, 1, i * P:(i + 1) * P],
                                      in0=ps[:, 7, 0:2 * P].rearrange("p (r q) -> p r q", r=2),
                                      in1=f(hx[:, 2 * g:2 * g + 2, 0, i * P:(i + 1) * P]), op=ALU.subtract).then_inc(o_lo, 1)

                def beside(n):
                    if n in (0, 1):
                        hh = n
                        dve.wait_ge(mean_mm, n + 1)
                        for ct in range(CTL):
                            dve.tensor_tensor(out=cacc[:, ct, half(hh)], in0=cacc[:, ct, half(hh)], in1=ps[:, 7, :],
                                              op=ALU.subtract).then_inc(cent, 1)
                    elif n in (2, 3):
                        hh = n - 2
                        dve.wait_ge(var_mm, n - 1)
                        dve.tensor_scalar(rstd[:, half(hh)], ps[:, 7, :], EPS, None, ALU.add).then_inc(eps_done, 1)
                    elif n in (5, 6, 7, 8):
                        q = slice((n - 5) * CTX, (n - 4) * CTX)
                        if n == 5:
                            dve.wait_ge(sqrt5, 1)
                        dve.reciprocal(rstd[:, q], rstd[:, q]).then_inc(rec5, 1)

                for hl in range(GQ):
                    maxima(0, hl)
                for n in range(NGRP):
                    i, g, kts = head_steps(n)
                    s = st[n % 2]
                    dve.wait_ge(negm_done, GQ * (n + 1))
                    dve.tensor_tensor(out=s[:, 3, :], in0=sinks[:, 0, GQ * g:GQ * (g + 1)], in1=s[:, 1, :], op=ALU.add).then_inc(arg_done, 1)
                    for j in range(len(kts)):
                        if n + 1 < NGRP and j < GQ:
                            maxima(n + 1, j)
                        if j == 2:
                            beside(n)
                        if j == 3 and n:
                            output_low(n - 1)
                    dve.wait_ge(sexp_done, n + 1)
                    dve.wait_ge(exp_done, GQ * (n + 1))
                    dve.tensor_tensor(out=s[:, 2, :], in0=s[:, 2, :], in1=s[:, 3, :], op=ALU.add).then_inc(den_done, 1)
                    dve.wait_ge(den_done, n + 1)
                    dve.reciprocal(s[:, 2, :], s[:, 2, :]).then_inc(rec_done, 1)
                    dve.wait_ge(rec_done, n + 1)
                    dve.wait_ge(pv_mm, first_item[n + 1])
                    if n:
                        dve.wait_ge(oT, n)
                    dve.tensor_tensor(out=on[:].rearrange("p (h d) -> p h d", h=GQ),
                                      in0=ps[:, 6, 0:GQ * HD].rearrange("p (h d) -> p h d", h=GQ),
                                      in1=s[:, 2, :].unsqueeze(2).to_broadcast([P, GQ, HD]), op=ALU.mult).then_inc(on_done, 1)
                dve.wait_ge(col_mm, 1)
                dve.tensor_tensor(out=mod2, in0=ps[:, 4, 0:2 * KT], in1=cols[:, C_BMOD + 3 * KT:C_BMOD + 5 * KT], op=ALU.add).then_inc(col_add, 1)
                dve.wait_ge(col_add, 1)
                dve.scalar_tensor_tensor(out=A2, in0=mod2[:, KT:], scalar=1.0, in1=cols[:, C_NFFN:C_NFFN + KT],
                                         op0=ALU.add, op1=ALU.mult).then_inc(a2_done, 1)
                output_low(NGRP - 1)
                for ct in range(CTL):
                    dve.wait_ge(u_hi, ct + 1)
                    dve.tensor_tensor(out=hx[:, CTL + ct, 1, :], in0=cacc[:, ct, :], in1=f(hx[:, CTL + ct, 0, :]), op=ALU.subtract).then_inc(u_lo, 1)

        NXT = 4
        woh = at(51, "woh", [P, KT, D], F32R)
        wol = at(83, "wol", [P, KT, D], F32R)
        xt = at(34.75, "xt", [P, NXT, D])
        hm = at(115, "hm", [P, 2, KT, P])
        gm = at(123, "gm", [P, 2, D])
        up_raw = at(131, "up_raw", [P, 2, KT, P])
        wup = w_up[0].rearrange("(k p) n -> p k n", p=P)
        with ExitStack() as s5:
            sem5 = lambda n: s5.enter_context(nc.semaphore(n))
            wo_hi, wo_lo, xt_in = sem5("wo_hi"), sem5("wo_lo"), [sem5(f"xt_in{i}") for i in range(NXT)]
            wo_mm, gated, x1_done, x1_out = sem5("wo_mm"), sem5("gated"), sem5("x1_done"), sem5("x1_out")
            ssq, ms5, sq2, r5, xn5, xT5, mod5, h2_hi, h2_lo = (
                sem5(n) for n in ("ssq", "ms5", "sq2", "r5", "xn5", "xT5", "mod5", "h2_hi", "h2_lo"))
            block = s5.enter_context(nc.Block())

            @block.sync
            def _(sp):
                for k in range(4, KT):
                    sp.wait_ge(wo_lo, k - 3)
                    sp.dma_start(wo_raw[:, k % 4, :], w_out[0, k * P:(k + 1) * P, :]).then_inc(wo_in[k % 4], 16)
                for t in range(TT):
                    if t >= NXT:
                        sp.wait_ge(xT5, t - NXT + 1)
                    sp.dma_start(xt[:, t % NXT, :], x[0, t * P:(t + 1) * P, :]).then_inc(xt_in[t % NXT], 16)
                for g in range(2):
                    sp.dma_start(up_raw[:, g], wup[:, :, g * FF:g * FF + P]).then_inc(up_in[g], 16)

            @block.gpsimd
            def _(pool):
                for t in range(TT):
                    pool.wait_ge(x1_done, t + 1)
                    pool.dma_start(x1_dram[t * P:(t + 1) * P, :], xt[:, t % NXT, :]).then_inc(x1_out, 16)
                pool.wait_ge(x1_out, 16 * TT)

            @block.tensor
            def _(pe):
                def project(t, k):
                    b = 4 + 2 * (t % 2)
                    if k == 0 and t >= 2:
                        pe.wait_ge(gated, t - 1)
                    for v in range(2):
                        a = hx[:, k, v, t * P:(t + 1) * P]
                        for lo in range(2 - v):
                            for hh in range(2):
                                last = pe.matmul(ps[:, b + hh, :], a, (woh, wol)[lo][:, k, hh * HALF:(hh + 1) * HALF],
                                                 start=(k == 0 and v == 0 and lo == 0), stop=(k == KT - 1 and v == 1))
                    if k == KT - 1:
                        last.then_inc(wo_mm, 1)

                def turn(t):
                    b = 2 * (t % 2)
                    pe.wait_ge(xn5, t + 1)
                    if t >= 2:
                        pe.wait_ge(mod5, t - 1)
                    for k in range(KT):
                        last = pe.transpose(ps[:, b + k // 4, (k % 4) * P:(k % 4 + 1) * P], xt[:, t % NXT, k * P:(k + 1) * P], ident[:])
                    last.then_inc(xT5, 1)

                for k in range(KT):
                    pe.wait_ge(wo_lo, k + 1)
                    for t in range(2):
                        project(t, k)
                for t in range(2, TT):
                    for k in range(KT):
                        project(t, k)
                    turn(t - 2)
                for t in range(TT - 2, TT):
                    turn(t)

            @block.scalar
            def _(act):
                for k in range(KT):
                    act.wait_ge(wo_in[k % 4], 16 * (k // 4 + 1))
                    act.activation(woh[:, k, :], wo_raw[:, k % 4, :], ACT.Copy).then_inc(wo_hi, 1)

                def square(t):
                    act.wait_ge(x1_done, t + 1)
                    if t >= 2:
                        act.wait_ge(h2_lo, t - 1)
                    act.activation(hm[:, t % 2].rearrange("p k n -> p (k n)"), xt[:, t % NXT, :], ACT.Square,
                                   accum_out=ss2[:, t:t + 1]).then_inc(ssq, 1)
                    act.wait_ge(ms5, t + 1)
                    act.activation(ss2[:, t:t + 1], ss2[:, t:t + 1], ACT.Sqrt).then_inc(sq2, 1)

                def modulate(t):
                    act.wait_ge(xT5, t + 1)
                    b = 2 * (t % 2)
                    for k in range(KT):
                        ins = act.activation(hm[:, t % 2, k, :], ps[:, b + k // 4, (k % 4) * P:(k % 4 + 1) * P], ACT.Identity,
                                             scale=A2[:, k:k + 1], bias=mod2[:, k:k + 1])
                    ins.then_inc(mod5, 1)
                    act.wait_ge(mod5, t + 1)
                    act.activation(hx[:, :, 0, t * P:(t + 1) * P], hm[:, t % 2], ACT.Copy).then_inc(h2_hi, 1)

                for t in range(TT):
                    square(t)
                    if t:
                        modulate(t - 1)
                modulate(TT - 1)

            @block.vector
            def _(dve):
                both = lambda b: ps[:, b:b + 2, :].rearrange("p b n -> p (b n)")
                for k in range(KT):
                    dve.wait_ge(wo_hi, k + 1)
                    dve.tensor_tensor(out=wol[:, k, :], in0=wo_raw[:, k % 4, :], in1=f(woh[:, k, :]), op=ALU.subtract).then_inc(wo_lo, 1)

                def residual(t):
                    b = 4 + 2 * (t % 2)
                    v = xt[:, t % NXT, :]
                    dve.wait_ge(wo_mm, t + 1)
                    dve.tensor_tensor(out=gm[:, t % 2], in0=both(b), in1=g1b[:], op=ALU.mult).then_inc(gated, 1)
                    dve.wait_ge(xt_in[t % NXT], 16 * (t // NXT + 1))
                    dve.wait_ge(gated, t + 1)
                    dve.tensor_tensor(out=v, in0=v, in1=gm[:, t % 2], op=ALU.add).then_inc(x1_done, 1)
                    dve.wait_ge(ssq, t + 1)
                    dve.tensor_scalar(ss2[:, t:t + 1], ss2[:, t:t + 1], 1.0 / D, EPS, ALU.mult, ALU.add).then_inc(ms5, 1)
                    dve.wait_ge(sq2, t + 1)
                    dve.reciprocal(rs2[:, t:t + 1], ss2[:, t:t + 1]).then_inc(r5, 1)
                    dve.wait_ge(r5, t + 1)
                    dve.wait_ge(x1_out, 16 * (t + 1))
                    dve.tensor_scalar(v, v, rs2[:, t:t + 1], None, ALU.mult).then_inc(xn5, 1)

                def low(t):
                    dve.wait_ge(h2_hi, t + 1)
                    dve.tensor_tensor(out=hx[:, :, 1, t * P:(t + 1) * P], in0=hm[:, t % 2], in1=f(hx[:, :, 0, t * P:(t + 1) * P]),
                                      op=ALU.subtract).then_inc(h2_lo, 1)

                for t in range(TT):
                    residual(t)
                    if t:
                        low(t - 1)
                low(TT - 1)

        hid = at(18, "hid", [P, FT, T])
        uph = at(114, "uph", [P, 2, KT, P], F32R)
        upl = at(122, "upl", [P, 2, KT, P], F32R)
        y = at(106, "y", [P, 2, T])
        dn_raw = at(139, "dn_raw", [P, 2, HALF])
        with ExitStack() as s6:
            sem6 = lambda n: s6.enter_context(nc.semaphore(n))
            up_hi, up_lo, up_mm = sem6("up_hi"), sem6("up_lo"), sem6("up_mm")
            cur_done, mid_tap, left_tap, side_taps, act_done, hid_done = (
                sem6(n) for n in ("cur_done", "mid_tap", "left_tap", "side_taps", "act_done", "hid_done"))
            block = s6.enter_context(nc.Block())

            def pairs(eng, body):
                for j in range(2):
                    body(j, j % 2, True, False)
                with eng.Fori(2, FT - 2, 2) as i:
                    for s in range(2):
                        body(i + s, s, False, False)
                for j in range(FT - 2, FT):
                    body(j, j % 2, False, True)

            @block.sync
            def _(sp):
                for s in range(2):
                    sp.dma_start(dn_raw[:, s, :], w_down[0, s * P:(s + 1) * P, 0:HALF]).then_inc(dn_in[s], 16)
                with sp.Fori(1, FT) as j:
                    for g in range(2):
                        sp.wait_ge(up_lo, 2 * j + g - 1)
                        sp.dma_start(up_raw[:, g], wup[:, :, bass.ds(g * FF + j * P, P)]).then_inc(up_in[g], 16)

            @block.tensor
            def _(pe):
                def body(j, s, first, final):
                    for g in range(2):
                        b = 4 * s + 2 * g
                        pe.wait_ge(up_lo, 2 * j + g + 1)
                        if not first:
                            pe.wait_ge(side_taps, 2 * (j - 2) + g + 1)
                        for k in range(KT):
                            for hh in range(2):
                                o, c_ = ps[:, b + hh, :], slice(hh * HALF, (hh + 1) * HALF)
                                pe.matmul(o, uph[:, g, k, :], hx[:, k, 0, c_], start=(k == 0), stop=False)
                                pe.matmul(o, uph[:, g, k, :], hx[:, k, 1, c_], start=False, stop=False)
                            for hh in range(2):
                                o, c_ = ps[:, b + hh, :], slice(hh * HALF, (hh + 1) * HALF)
                                last = pe.matmul(o, upl[:, g, k, :], hx[:, k, 0, c_], start=False, stop=(k == KT - 1))
                        last.then_inc(up_mm, 1)

                pairs(pe, body)

            def bank_pair(s, g):
                return ps[:, 4 * s + 2 * g:4 * s + 2 * g + 2, :].rearrange("p b n -> p (b n)")

            @block.scalar
            def _(act):
                def split(j, g, first):
                    act.wait_ge(up_in[g], 16 * (j + 1))
                    if not first:
                        act.wait_ge(up_mm, 2 * (j - 1) + g + 1)
                    act.activation(uph[:, g], up_raw[:, g], ACT.Copy).then_inc(up_hi, 1)

                def body(j, s, first, final, last=False):
                    for g in range(2):
                        if not last:
                            split(j + 1, g, False)
                        act.wait_ge(up_mm, 2 * j + g + 1)
                        act.wait_ge(cur_done, j + 1)
                        if not (first and s == 0):
                            act.wait_ge(hid_done, j)
                        act.activation(y[:, g, :], bank_pair(s, g), ACT.Identity, scale=ffcur[s][:, 4 * g + 1:4 * g + 2],
                                       bias=ffcur[s][:, 4 * g + 3:4 * g + 4]).then_inc(mid_tap, 1)
                    act.wait_ge(side_taps, 2 * j + 1)
                    act.activation(y[:, 0, :], y[:, 0, :], ACT.Silu).then_inc(act_done, 1)

                split(0, 0, True)
                split(0, 1, True)
                for j in range(2):
                    body(j, j % 2, True, False)
                with act.Fori(2, FT - 2, 2) as i:
                    for s in range(2):
                        body(i + s, s, False, False)
                body(FT - 2, 0, False, True)
                body(FT - 1, 1, False, True, last=True)

            @block.vector
            def _(dve):
                def split(j, g):
                    dve.wait_ge(up_hi, 2 * j + g + 1)
                    dve.tensor_tensor(out=upl[:, g], in0=up_raw[:, g], in1=f(uph[:, g]), op=ALU.subtract).then_inc(up_lo, 1)

                def body(j, s, first, final, last=False):
                    dve.tensor_scalar(ffcur[s].unsqueeze(1), ffs[:, bass.ds(j, 1), :], 1.0, None, ALU.mult).then_inc(cur_done, 1)
                    dve.wait_ge(cur_done, j + 1)
                    for g in range(2):
                        if not last:
                            split(j + 1, g)
                        p = bank_pair(s, g)
                        dve.wait_ge(mid_tap, 2 * j + g + 1)
                        dve.scalar_tensor_tensor(out=y[:, g, 1:T], in0=p[:, 0:T - 1], scalar=ffcur[s][:, 4 * g:4 * g + 1],
                                                 in1=y[:, g, 1:T], op0=ALU.mult, op1=ALU.add).then_inc(left_tap, 1)
                        dve.wait_ge(left_tap, 2 * j + g + 1)
                        dve.scalar_tensor_tensor(out=y[:, g, 0:T - 1], in0=p[:, 1:T], scalar=ffcur[s][:, 4 * g + 2:4 * g + 3],
                                                 in1=y[:, g, 0:T - 1], op0=ALU.mult, op1=ALU.add).then_inc(side_taps, 1)
                    dve.wait_ge(act_done, j + 1)
                    dve.wait_ge(side_taps, 2 * j + 2)
                    dve.tensor_tensor(out=hid[:, bass.ds(j, 1), :], in0=y[:, 0:1, :], in1=y[:, 1:2, :], op=ALU.mult).then_inc(hid_done, 1)

                split(0, 0)
                split(0, 1)
                for j in range(2):
                    body(j, j % 2, True, False)
                with dve.Fori(2, FT - 2, 2) as i:
                    for s in range(2):
                        body(i + s, s, False, False)
                body(FT - 2, 0, False, True)
                body(FT - 1, 1, False, True, last=True)

        dnh = at(110, "dnh", [P, 2, HALF], F32R)
        dnl = at(114, "dnl", [P, 2, HALF], F32R)
        ah = at(118, "ah", [P, 2, T], F32R)
        al = at(126, "al", [P, 2, T], F32R)
        x1 = at(143, "x1", [P, TT, D])
        gout = at(175, "gout", [P, TT, HALF])
        with ExitStack() as s7:
            sem7 = lambda n: s7.enter_context(nc.semaphore(n))
            x1_in = sem7("x1_in")
            dn_hi, dn_lo, a_hi, a_lo, dn_mm, bank_mm, bank_out, res_done, stored = (
                sem7(n) for n in ("dn_hi", "dn_lo", "a_hi", "a_lo", "dn_mm", "bank_mm", "bank_out", "res_done", "stored"))
            block = s7.enter_context(nc.Block())

            def steps(eng, body):
                for half in range(2):
                    n0 = half * FT
                    for k in range(2):
                        body(n0 + k, k, half, k % 2, "first" if k == 0 else "peeled")
                    with eng.Fori(2, FT - 2, 2) as i:
                        for s in range(2):
                            body(i + (n0 + s), i + s, half, s, "loop")
                    for k in range(FT - 2, FT):
                        body(n0 + k, k, half, k % 2, "last" if k == FT - 1 else "loop")

            def early(kind, half):
                return half == 0 and kind in ("first", "peeled")

            @block.sync
            def _(sp):
                sp.dma_start(x1[:], x1_dram.rearrange("(t p) d -> p t d", p=P)).then_inc(x1_in, 16)

                def body(n, k, half, s, kind):
                    if early(kind, half):
                        return
                    sp.wait_ge(dn_lo, n - 1)
                    sp.dma_start(dn_raw[:, s, :], w_down[0, bass.ds(k * P, P), half * HALF:(half + 1) * HALF]).then_inc(dn_in[s], 16)

                steps(sp, body)

            @block.tensor
            def _(pe):
                def body(n, k, half, s, kind):
                    pe.wait_ge(dn_lo, n + 1)
                    pe.wait_ge(a_lo, n + 1)
                    for t in range(TT):
                        if kind == "first" and half:
                            pe.wait_ge(bank_out, t + 1)
                        c_ = slice(t * P, (t + 1) * P)
                        pe.matmul(ps[:, t, :], ah[:, s, c_], dnh[:, s, :], start=(kind == "first"), stop=False)
                        pe.matmul(ps[:, t, :], ah[:, s, c_], dnl[:, s, :], start=False, stop=False)
                        last = pe.matmul(ps[:, t, :], al[:, s, c_], dnh[:, s, :], start=False, stop=(kind == "last"))
                        if kind == "last":
                            last.then_inc(bank_mm, 1)
                        elif t == TT - 1:
                            last.then_inc(dn_mm, 1)

                steps(pe, body)

            def wait_step_done(eng, n, half, kind, k):
                if early(kind, half):
                    return
                if half and kind in ("first", "peeled"):
                    if kind == "first":
                        eng.wait_ge(dn_mm, FT - 1)
                    else:
                        eng.wait_ge(bank_mm, TT)
                    return
                eng.wait_ge(dn_mm, n - 1 - half)

            @block.scalar
            def _(act):
                def body(n, k, half, s, kind):
                    act.wait_ge(dn_in[s], 8 * (n - s) + 16)
                    wait_step_done(act, n, half, kind, k)
                    act.activation(dnh[:, s, :], dn_raw[:, s, :], ACT.Copy).then_inc(dn_hi, 1)

                steps(act, body)

            @block.vector
            def _(dve):
                def drain(half):
                    for t in range(TT):
                        dve.wait_ge(bank_mm, half * TT + t + 1)
                        if half and t == 0:
                            dve.wait_ge(stored, 16 * TT)
                        dve.tensor_tensor(out=gout[:, t, :], in0=ps[:, t, :], in1=g2b[:, half * HALF:(half + 1) * HALF],
                                          op=ALU.mult).then_inc(bank_out, 1)

                def body(n, k, half, s, kind):
                    wait_step_done(dve, n, half, kind, k)
                    dve.tensor_scalar(ah[:, s:s + 1, :], hid[:, bass.ds(k, 1), :], 1.0, None, ALU.mult).then_inc(a_hi, 1)
                    dve.wait_ge(dn_hi, n + 1)
                    dve.tensor_tensor(out=dnl[:, s, :], in0=dn_raw[:, s, :], in1=f(dnh[:, s, :]), op=ALU.subtract).then_inc(dn_lo, 1)
                    dve.wait_ge(a_hi, n + 1)
                    dve.tensor_tensor(out=al[:, s:s + 1, :], in0=hid[:, bass.ds(k, 1), :], in1=f(ah[:, s:s + 1, :]),
                                      op=ALU.subtract).then_inc(a_lo, 1)

                for half in range(2):
                    n0 = half * FT
                    for k in range(2):
                        if half and k == 0:
                            body(n0, 0, 1, 0, "first")
                            drain(0)
                        else:
                            body(n0 + k, k, half, k % 2, "first" if k == 0 else "peeled")
                    with dve.Fori(2, FT - 2, 2) as i:
                        for s in range(2):
                            body(i + (n0 + s), i + s, half, s, "loop")
                    for k in range(FT - 2, FT):
                        body(n0 + k, k, half, k % 2, "last" if k == FT - 1 else "loop")
                drain(1)

            @block.gpsimd
            def _(pool):
                pool.wait_ge(x1_in, 16)
                for half in range(2):
                    for t in range(TT):
                        pool.wait_ge(bank_out, half * TT + t + 1)
                        v = gout[:, t, :]
                        pool.tensor_tensor(out=v, in0=v, in1=x1[:, t, half * HALF:(half + 1) * HALF], op=ALU.add).then_inc(res_done, 1)
                        pool.wait_ge(res_done, half * TT + t + 1)
                        pool.dma_start(out[0, t * P:(t + 1) * P, half * HALF:(half + 1) * HALF], v).then_inc(stored, 16)
                pool.wait_ge(stored, 2 * TT * 16)


def rope_table(np):
    axis = HD // 2
    inv = (np.float32(10000.0) ** (-np.arange(0, axis, 2, dtype=np.float32) / np.float32(axis))).astype(np.float32)
    pos = np.arange(T)
    ang_r = (pos // 64).astype(np.float32)[:, None] * inv
    ang_c = (pos % 64).astype(np.float32)[:, None] * inv
    sign = np.repeat(np.array([-1.0, 1.0, -1.0, 1.0], np.float32), axis // 2)
    ang = np.concatenate([ang_r, ang_r, ang_c, ang_c], axis=-1)
    return np.stack([np.cos(ang), np.sin(ang) * sign]).astype(np.float32)


INPUTS = ["x", "c", "ctx", "c_ctx", "w_mod", "b_mod", "norm_mix_w", "w_in", "q_norm_w", "k_norm_w", "sink_logit",
          "conv_w", "conv_b", "conv_norm_w", "conv_norm_b", "w_out", "norm_ffn_w", "w_up", "ffn_conv_w",
          "ffn_conv_b", "w_down"]


def kernel(**inputs):
    import numpy as np
    import concourse.bacc as bacc
    from concourse.bass_utils import run_bass_kernel_spmd

    nc = bacc.Bacc("TRN2", target_bir_lowering=False, num_devices=1)
    arrays, args = {}, []
    for name in INPUTS + ["rope"]:
        a = np.ascontiguousarray(rope_table(np) if name == "rope" else inputs[name])
        arrays[f"in_{name}"] = a
        args.append(nc.dram_tensor(f"in_{name}", a.shape, mybir.dt.from_np(a.dtype), kind="ExternalInput").ap())
    args.append(nc.dram_tensor("out_latent", (1, T, D), F32, kind="ExternalOutput").ap())
    build(nc, *args)
    result = run_bass_kernel_spmd(nc, [arrays], core_ids=[0])
    return result.results[0]["out_latent"]
```

```python
import math
from contextlib import ExitStack

import concourse.bass as bass
from concourse import mybir

F32 = mybir.dt.float32
F32R = mybir.dt.float32r
ALU = mybir.AluOpType
ACT = mybir.ActivationFunctionType
AX = mybir.AxisListType

P = 128
D = 1024
T = 1024
CTX = 256
KT = D // P
TT = T // P
CT = CTX // P
HALF = 512
HD = 64
NH = 8
NG = 2
GQ = NH // NG
QC = NH * HD
KVC = 2 * NG * HD
QKV = QC + KVC
CC = 512
CTL = CC // P
TAPS = 31
PAD = TAPS // 2
FF = 2816
FT = FF // P
EPS = 1e-6
SCALE = 1.0 / math.sqrt(HD)
MASKED = -1e30
KEYS = CTX + T

C_C, C_CTX, C_NMIX, C_NFFN, C_BMOD = 0, 8, 16, 24, 32
C_CONVB, C_CNW, C_CNB = 80, 84, 88
N_A = 92
C_FB, C_FW0 = N_A, N_A + FT * 2
C_FW1, C_FW2 = N_A + FT * 4, N_A + FT * 6
C_CONVW = N_A + FT * 8
N_COLS = C_CONVW + CTL * TAPS


class Memory:

    def __init__(self, nc, base):
        self.nc, self.base = nc, base

    def at(self, kib, name, shape, dt=F32):
        return self.nc.alloc_sbuf_tensor_at(name, shape, dt, offset=self.base + int(kib * 1024))


def build(nc, x, c, ctx, c_ctx, w_mod, b_mod, norm_mix_w, w_in, q_norm_w, k_norm_w, sink_logit,
          conv_w, conv_b, conv_norm_w, conv_norm_b, w_out, norm_ffn_w, w_up, ffn_conv_w,
          ffn_conv_b, w_down, rope, out):
    es = ExitStack()
    with es:
        mem = Memory(nc, 16512)
        at = mem.at
        ps = es.enter_context(nc.psum_tensor("ps", [P, 8, HALF], F32))
        x1_dram = nc.dram_tensor("x1_scratch", (T, D), F32, kind="Internal").ap()

        def sem(name):
            return es.enter_context(nc.semaphore(name))

        cs_in = sem("cs_in")
        wo_in = [sem(f"wo_in{i}") for i in range(4)]
        up_in = [sem("up_in0"), sem("up_in1")]
        up_hi, up_lo = sem("up_hi"), sem("up_lo")
        dn_in = [sem("dn_in0"), sem("dn_in1")]

        ident = at(0, "ident", [P, P])
        identr = at(0.5, "identr", [P, P], F32R)
        ones = at(1, "ones", [P, P])
        mask_prev = at(1.5, "mask_prev", [P, P], F32R)
        mask_next = at(2, "mask_next", [P, P], F32R)
        cols = at(2.5, "cols", [P, N_COLS])
        scal = at(4.25, "scal", [P, 256])
        g1b = at(5.5, "g1b", [P, D])
        g2b = at(9.5, "g2b", [P, D])
        ffs = at(13.5, "ffs", [P, FT, 8])
        meanw = at(14.5, "meanw", [P, P])
        maskf = at(15, "maskf", [P, 2, P])
        sinks = at(16, "sinks", [P, 2, NH])
        qkw = at(16.25, "qkw", [P, 2, HD])
        nat = scal[:, 0:16].rearrange("p (k two) -> p k two", two=2)
        ss = scal[:, 16:26]
        rst = scal[:, 26:36]
        modl = scal[:, 36:52]
        modc = scal[:, 52:68]
        A1, Ac = scal[:, 68:76], scal[:, 76:84]
        mod2 = scal[:, 84:100]
        A2 = scal[:, 100:108]
        ss2 = scal[:, 108:116]
        rs2 = scal[:, 116:124]
        ffcur = [scal[:, 128:136], scal[:, 136:144]]
        msq = at(16.75, "msq", [P, TT + CT, NH + NG])
        hx = at(143, "hx", [P, KT, 2, T], F32R)

        def f(ap):
            return ap.bitcast(F32)

        xs = at(18, "xs", [P, TT, D])
        xnT = at(50, "xnT", [P, KT, T])
        hc32 = at(42.75, "hc32", [P, KT, CTX])
        hcx = at(83, "hcx", [P, KT, 2, CTX], F32R)
        wm = at(143, "wm", [P, KT, 2 * D])
        junk = at(123, "junk", [P, D])
        cx = at(131, "cx", [P, CT, D])
        vecs = at(139, "vecs", [P, 4, P])
        cvecs = at(141, "cvecs", [P, P])
        mrow = at(123, "mrow", [2, 2 * D])
        UW = T + 2 * PAD
        u = at(18, "u", [P, CTL, UW])
        cacc = at(34.75, "cacc", [P, CTL, T])
        qw_raw = at(75, "qw_raw", [P, 2, QKV])
        qwh = at(51, "qwh", [P, KT, QKV], F32R)
        qwl = at(119, "qwl", [P, KT, QKV], F32R)
        gw_raw = at(99, "gw_raw", [P, KT, P])
        gwh = at(103, "gwh", [P, 2, KT, P], F32R)
        gwl = at(111, "gwl", [P, 2, KT, P], F32R)
        qraw = at(83, "qraw", [P, TT, QC])
        kvraw = at(99, "kvraw", [P, CT + TT, KVC])
        ptmp = at(5.5, "ptmp", [P, T])
        POOL_CT = 1
        DVE_CT = [ct for ct in range(CTL) if ct != POOL_CT]
        NGL = 2 * CTL
        cs = at(109, "cs", [P, 2, TT, HD])
        sqj = at(113, "sqj", [P, 2, NH + NG, HD])
        with ExitStack() as s1:
            sem1 = lambda n: s1.enter_context(nc.semaphore(n))
            c_in, vec_in, row_in = sem1("c_in"), sem1("vec_in"), sem1("row_in")
            x_in = [sem1(f"x_in{t}") for t in range((TT + CT) // 2)]
            wm_in = [sem1(f"wm_in{i}") for i in range(KT // 2)]
            const_step, const_done = sem1("const_step"), sem1("const_done")
            vecT, cols_done, silu_done = sem1("vecT"), sem1("cols_done"), sem1("silu_done")
            sq_done, ms_done, sqrt_done, rst_done = sem1("sq_done"), sem1("ms_done"), sem1("sqrt_done"), sem1("rst_done")
            xn_done, xT, xT_out = sem1("xn_done"), sem1("xT"), sem1("xT_out")
            mod_mm, mrow_out, mod_T, mod_done, ab_done = (sem1(n) for n in ("mod_mm", "mrow_out", "mod_T", "mod_done", "ab_done"))
            h_mod, h_hi, h_lo = sem1("h_mod"), sem1("h_hi"), sem1("h_lo")
            hc_hi, hc_lo = sem1("hc_hi"), sem1("hc_lo")
            ffs_done = sem1("ffs_done")
            gw_in, gw_hi, gw_lo, gl_mm = sem1("gw_in"), sem1("gw_hi"), sem1("gw_lo"), sem1("gl_mm")
            qw_in = [sem1("qw_in0"), sem1("qw_in1")]
            qw_hi, qw_lo, qkv_mm, qkv_out = sem1("qw_hi"), sem1("qw_lo"), sem1("qkv_mm"), sem1("qkv_out")
            st_done = sem1("st_done")
            pad_done, gate_done, u_done = sem1("pad_done"), sem1("gate_done"), sem1("u_done")
            tap_done, ptap_mul, ptap_add = sem1("tap_done"), sem1("ptap_mul"), sem1("ptap_add")
            win = w_in[0].rearrange("(k p) n -> p k n", p=P)

            def glu_col(n):
                return QKV + (CC if n % 2 == 0 else 0) + (n // 2) * P

            block = s1.enter_context(nc.Block())
            BATCHES = [(0, 4), (4, TT), (TT, TT + CT)]
            NXB = 3

            def x_bank(n):
                return 4 + n % NXB

            rows = lambda v, n: v.rearrange("(r q) -> r q", q=P)
            C0 = C_NMIX
            parts = [(0, C_NMIX - C0, 8, norm_mix_w[0]), (0, C_NFFN - C0, 8, norm_ffn_w[0]), (0, C_BMOD - C0, 48, b_mod[0]),
                     (0, C_CONVB - C0, 4, conv_b[0]), (0, C_CNW - C0, 4, conv_norm_w[0]), (0, C_CNB - C0, 4, conv_norm_b[0]),
                     (1, 0, 2 * FT, ffn_conv_b[0]), (1, 2 * FT, 2 * FT, ffn_conv_w[0, 0]),
                     (2, 0, 2 * FT, ffn_conv_w[0, 1]), (2, 2 * FT, 2 * FT, ffn_conv_w[0, 2])]
            vec_total = 16 * (len(parts) + 1)

            @block.sync
            def _(sp):
                sp.dma_start(cvecs[0:KT, :], rows(c[0], KT)).then_inc(c_in, 16)
                sp.dma_start(cvecs[KT:2 * KT, :], rows(c_ctx, KT)).then_inc(c_in, 16)
                for k in range(KT):
                    sp.dma_start(wm[:, k, :], w_mod[0, k * P:(k + 1) * P, 0:2 * D]).then_inc(wm_in[k // 2], 16)
                sp.dma_start(gw_raw[:], win[:, :, glu_col(0):glu_col(0) + P]).then_inc(gw_in, 16)
                for t in range(CT):
                    sp.dma_start(cx[:, t, :], ctx[0, t * P:(t + 1) * P, :]).then_inc(x_in[(TT + t) // 2], 16)
                sp.dma_start(sinks[:, 0, :], sink_logit[0].partition_broadcast(P)).then_inc(row_in, 16)
                sp.dma_start(qkw[:, 0, :], q_norm_w[0].partition_broadcast(P)).then_inc(row_in, 16)
                sp.dma_start(qkw[:, 1, :], k_norm_w[0].partition_broadcast(P)).then_inc(row_in, 16)

                for n in range(NGL):
                    if n + 1 < NGL:
                        sp.wait_ge(gw_lo, n + 1)
                        sp.dma_start(gw_raw[:], win[:, :, glu_col(n + 1):glu_col(n + 1) + P]).then_inc(gw_in, 16)
                    if n == 0:
                        sp.wait_ge(h_lo, KT)
                    if n >= 2:
                        sp.wait_ge(qw_lo, n - 1)
                    sp.dma_start(qw_raw[:, n % 2, :], w_in[0, n * P:(n + 1) * P, 0:QKV]).then_inc(qw_in[n % 2], 16)
                sp.wait_ge(gl_mm, NGL)
                sp.dma_start(cs[:], rope.rearrange("w (t p) d -> p w t d", p=P)).then_inc(cs_in, 16)

            @block.gpsimd
            def _(pool):
                pool.memset(ident[:], 0.0).then_inc(const_step, 1)
                pool.memset(maskf[:], 0.0).then_inc(const_step, 1)
                pool.memset(ones[:], 1.0).then_inc(const_done, 1)
                pool.memset(meanw[:], 1.0 / CC).then_inc(const_done, 1)
                pool.wait_ge(const_step, 2)
                pool.affine_select(out=ident[:], in_=ident[:], compare_op=ALU.not_equal, fill=1.0, base=0,
                                   pattern=[[-1, P]], channel_multiplier=1).then_inc(const_done, 1)
                pool.affine_select(out=maskf[:, 0, :], in_=maskf[:, 0, :], compare_op=ALU.is_ge, fill=MASKED,
                                   base=0, pattern=[[1, P]], channel_multiplier=-1).then_inc(const_step, 1)
                pool.affine_select(out=maskf[:, 1, :], in_=maskf[:, 1, :], compare_op=ALU.is_ge, fill=MASKED,
                                   base=0, pattern=[[-1, P]], channel_multiplier=1).then_inc(const_step, 1)
                pool.wait_ge(const_done, 3)
                pool.tensor_copy(identr[:], ident[:]).then_inc(const_done, 1)
                pool.wait_ge(const_step, 4)
                pool.tensor_copy(mask_prev[:], maskf[:, 0, :]).then_inc(const_done, 1)
                pool.tensor_copy(mask_next[:], maskf[:, 1, :]).then_inc(const_done, 1)
                for v, r0, n, src in parts:
                    pool.dma_start(vecs[r0:r0 + n, v, :], rows(src, n)).then_inc(vec_in, 16)
                pool.dma_start(vecs[0:TAPS * CTL, 3, :], conv_w[0].rearrange("w (r q) -> (w r) q", q=P)).then_inc(vec_in, 16)

                pool.wait_ge(xT, 2 * KT)
                pool.memset(u[:], 0.0).then_inc(pad_done, 1)
                ct = POOL_CT
                pool.wait_ge(u_done, ct + 1)
                for i in range(TAPS):
                    w = cols[:, C_CONVW + i * CTL + ct:C_CONVW + i * CTL + ct + 1]
                    if i == 0:
                        pool.tensor_scalar(cacc[:, ct, :], u[:, ct, 0:T], w, cols[:, C_CONVB + ct:C_CONVB + ct + 1],
                                           ALU.mult, ALU.add).then_inc(ptap_add, 1)
                        continue
                    if i > 1:
                        pool.wait_ge(ptap_add, i)
                    pool.tensor_scalar(ptmp[:], u[:, ct, i:i + T], w, 1.0, ALU.mult, ALU.mult).then_inc(ptap_mul, 1)
                    pool.wait_ge(ptap_mul, i)
                    pool.wait_ge(ptap_add, i)
                    pool.tensor_tensor(out=cacc[:, ct, :], in0=cacc[:, ct, :], in1=ptmp[:], op=ALU.add).then_inc(ptap_add, 1)

            @block.tensor
            def _(pe):
                pe.wait_ge(const_done, 3)
                pe.wait_ge(c_in, 32)
                pe.transpose(ps[:, 7, 0:2 * KT], cvecs[0:2 * KT, :], ident[0:2 * KT, 0:2 * KT]).then_inc(vecT, 1)

                def vectors():
                    pe.wait_ge(silu_done, 2)
                    pe.wait_ge(vec_in, vec_total)
                    off = 2 * KT
                    for v, n in enumerate((N_A - 2 * KT, 4 * FT, 4 * FT, TAPS * CTL)):
                        last = pe.transpose(ps[:, 7, off:off + n], vecs[0:n, v, :], ident[0:n, 0:n])
                        off += n
                    last.then_inc(vecT, 1)

                def x_item(n):
                    hh, k = divmod(n, KT)
                    if n % KT == 0:
                        pe.wait_ge(xn_done, 4 * (hh + 1))
                    if n >= NXB:
                        pe.wait_ge(xT_out, n - NXB + 1)
                    for t in range(4):
                        last = pe.transpose(ps[:, x_bank(n), t * P:(t + 1) * P], xs[:, 4 * hh + t, k * P:(k + 1) * P], ident[:])
                    last.then_inc(xT, 1)

                def ctx_item(n):
                    pe.wait_ge(xT_out, n - NXB + 1)
                    if n == 2 * KT:
                        pe.wait_ge(xn_done, TT + CT)
                    for kk in range(2):
                        for t in range(CT):
                            k = 2 * (n - 2 * KT) + kk
                            last = pe.transpose(ps[:, x_bank(n), (2 * kk + t) * P:(2 * kk + t + 1) * P],
                                                cx[:, t, k * P:(k + 1) * P], ident[:])
                    last.then_inc(xT, 1)

                def mod_item(k):
                    pe.wait_ge(wm_in[k // 2], 32)
                    if k == 0:
                        pe.wait_ge(silu_done, 2)
                    for q in range(4):
                        last = pe.matmul(ps[0:2, q, :], nat[:, k, :], wm[:, k, q * HALF:(q + 1) * HALF], start=(k == 0), stop=(k == KT - 1))
                    last.then_inc(mod_mm, 1)

                for k in range(2):
                    mod_item(k)
                for n in range(KT):
                    x_item(n)
                for k in range(2, KT - 2):
                    mod_item(k)
                for n in range(KT, 2 * KT):
                    x_item(n)
                mod_item(KT - 2)
                vectors()
                mod_item(KT - 1)
                pe.wait_ge(mrow_out, 4)
                pe.wait_ge(cols_done, 2)
                for j in range(2 * KT):
                    last = pe.transpose(ps[:, 7, 2 * j:2 * j + 2], mrow[:, j * P:(j + 1) * P], ident[0:2, 0:2])
                last.then_inc(mod_T, 1)

                for n in range(NGL):
                    b = 2 * (n % 4)
                    pe.wait_ge(gw_lo, n + 1)
                    if n == 1:
                        for i in range(2 * KT, 2 * KT + 4):
                            ctx_item(i)
                    if n == 2:
                        pe.wait_ge(xT_out, 2 * KT + 4)
                    if n >= 4:
                        pe.wait_ge(u_done, (n - 4) // 2 + 1)
                    for k in range(KT):
                        if n == 0:
                            pe.wait_ge(h_lo, k + 1)
                        for hh in range(2):
                            o, s = ps[:, b + hh, :], slice(hh * HALF, (hh + 1) * HALF)
                            pe.matmul(o, gwh[:, n % 2, k, :], hx[:, k, 0, s], start=(k == 0), stop=False)
                            pe.matmul(o, gwh[:, n % 2, k, :], hx[:, k, 1, s], start=False, stop=False)
                        for hh in range(2):
                            o, s = ps[:, b + hh, :], slice(hh * HALF, (hh + 1) * HALF)
                            last = pe.matmul(o, gwl[:, n % 2, k, :], hx[:, k, 0, s], start=False, stop=(k == KT - 1))
                    last.then_inc(gl_mm, 1)
                pe.wait_ge(qw_lo, KT)
                pe.wait_ge(hc_lo, 1)
                for m in range(CT + TT):
                    b = 2 * (m % 4)
                    pe.wait_ge(u_done, 3 if m < 2 else CTL)
                    if m >= 4:
                        pe.wait_ge(qkv_out, m - 3)
                    for k in range(KT):
                        if m < CT:
                            h = [hcx[:, k, v, m * P:(m + 1) * P] for v in range(2)]
                        else:
                            h = [hx[:, k, v, (m - CT) * P:(m - CT + 1) * P] for v in range(2)]
                        for v in range(2):
                            for lo in range(2 - v):
                                w = (qwh, qwl)[lo]
                                first, end = (k == 0 and v == 0 and lo == 0), (k == KT - 1 and v == 1)
                                if m >= CT:
                                    pe.matmul(ps[:, b, :], h[v], w[:, k, 0:QC], start=first, stop=end)
                                last = pe.matmul(ps[:, b + 1, 0:KVC], h[v], w[:, k, QC:QKV], start=first, stop=end)
                    last.then_inc(qkv_mm, 1)

            @block.scalar
            def _(act):
                for t in range(TT):
                    act.dma_start(xs[:, t, :], x[0, t * P:(t + 1) * P, :]).then_inc(x_in[t // 2], 16)
                act.wait_ge(vecT, 1)
                for i in range(2):
                    act.activation(nat[:, :, i], ps[:, 7, i * KT:(i + 1) * KT], ACT.Silu).then_inc(silu_done, 1)

                def square(t):
                    act.wait_ge(x_in[t // 2], 32)
                    if t:
                        act.wait_ge(sq_done, t)
                    act.activation(junk[:], xs[:, t, :] if t < TT else cx[:, t - TT, :], ACT.Square,
                                   accum_out=ss[:, t:t + 1]).then_inc(sq_done, 1)

                def copy_x(n):
                    hh, k = divmod(n, KT)
                    act.wait_ge(xT, n + 1)
                    act.activation(xnT[:, k, hh * HALF:(hh + 1) * HALF], ps[:, x_bank(n), :], ACT.Copy).then_inc(xT_out, 1)

                def norms(r):
                    t0, t1 = BATCHES[r]
                    for t in range(t0, t1):
                        square(t)
                    act.wait_ge(ms_done, r + 1)
                    act.activation(rst[:, t0:t1], ss[:, t0:t1], ACT.Sqrt).then_inc(sqrt_done, 1)

                def split_glu(n):
                    act.wait_ge(gw_in, 16 * (n + 1))
                    if n >= 2:
                        act.wait_ge(gl_mm, n - 1)
                    act.activation(gwh[:, n % 2], gw_raw[:], ACT.Copy).then_inc(gw_hi, 1)

                def split_qkv(k):
                    act.wait_ge(qw_in[k % 2], 16 * (k // 2 + 1))
                    act.activation(qwh[:, k, :], qw_raw[:, k % 2, :], ACT.Copy).then_inc(qw_hi, 1)

                for r in range(2):
                    norms(r)
                    for n in range(r * KT, (r + 1) * KT):
                        copy_x(n)
                split_glu(0)
                act.wait_ge(mod_mm, KT)
                for q in range(2):
                    act.activation(mrow[:, q * HALF:(q + 1) * HALF], ps[0:2, q, :], ACT.Copy).then_inc(mrow_out, 1)
                act.wait_ge(ab_done, 2)
                act.wait_ge(xT_out, 2 * KT)
                for k in range(KT):
                    act.activation(hx[:, k, 0, :], xnT[:, k, :], ACT.Identity, scale=A1[:, k:k + 1], bias=modl[:, k:k + 1]).then_inc(h_hi, 1)
                norms(2)
                split_glu(1)
                act.wait_ge(pad_done, 1)
                for n in range(NGL):
                    if n == 1:
                        for i in range(4):
                            act.wait_ge(xT, 2 * KT + i + 1)
                            act.activation(hc32[:, 2 * i:2 * i + 2, :], ps[:, x_bank(2 * KT + i), :].rearrange("p (k n) -> p k n", k=2),
                                           ACT.Copy).then_inc(xT_out, 1)
                    if n and n + 1 < NGL:
                        split_glu(n + 1)
                    if n:
                        split_qkv(n - 1)
                    if n == 1:
                        act.wait_ge(xT_out, 2 * KT + 4)
                        for k in range(KT):
                            act.activation(hcx[:, k, 0, :], hc32[:, k, :], ACT.Identity, scale=Ac[:, k:k + 1], bias=modc[:, k:k + 1]).then_inc(hc_hi, 1)
                    if n == NGL - 1:
                        split_qkv(n)

                    act.wait_ge(gl_mm, n + 1)
                    if n % 2 == 0:
                        ct, b = n // 2, 2 * (n % 4)
                        act.activation(u[:, ct, PAD:PAD + T], ps[:, b:b + 2, :].rearrange("p b n -> p (b n)"),
                                       ACT.Sigmoid).then_inc(gate_done, 1)
                for m in range(CT + TT):
                    b = 2 * (m % 4)
                    act.wait_ge(qkv_mm, m + 1)
                    if m >= CT:
                        act.activation(qraw[:, m - CT, :], ps[:, b, :], ACT.Copy)
                    act.activation(kvraw[:, m, :], ps[:, b + 1, 0:KVC], ACT.Copy).then_inc(qkv_out, 1)
                    act.wait_ge(qkv_out, m + 1)
                    if m >= 2:
                        act.wait_ge(st_done, m - 1)
                    for h in range(0 if m >= CT else NH, NH + NG):
                        v = qraw[:, m - CT, h * HD:(h + 1) * HD] if h < NH else kvraw[:, m, (h - NH) * HD:(h - NH + 1) * HD]
                        last = act.activation(sqj[:, m % 2, h, :], v, ACT.Square, accum_out=msq[:, m, h:h + 1])
                    last.then_inc(st_done, 1)

            @block.vector
            def _(dve):
                def norms(r):
                    t0, t1 = BATCHES[r]
                    dve.wait_ge(sq_done, t1)
                    dve.tensor_scalar(ss[:, t0:t1], ss[:, t0:t1], 1.0 / D, EPS, ALU.mult, ALU.add).then_inc(ms_done, 1)
                    dve.wait_ge(sqrt_done, r + 1)
                    dve.reciprocal(rst[:, t0:t1], rst[:, t0:t1]).then_inc(rst_done, 1)
                    dve.wait_ge(rst_done, r + 1)
                    for t in range(t0, t1):
                        v = xs[:, t, :] if t < TT else cx[:, t - TT, :]
                        dve.tensor_scalar(v, v, rst[:, t:t + 1], None, ALU.mult).then_inc(xn_done, 1)

                def split_glu(n):
                    dve.wait_ge(gw_hi, n + 1)
                    dve.tensor_tensor(out=gwl[:, n % 2], in0=gw_raw[:], in1=f(gwh[:, n % 2]), op=ALU.subtract).then_inc(gw_lo, 1)

                def split_qkv(k):
                    dve.wait_ge(qw_hi, k + 1)
                    dve.tensor_tensor(out=qwl[:, k, :], in0=qw_raw[:, k % 2, :], in1=f(qwh[:, k, :]), op=ALU.subtract).then_inc(qw_lo, 1)

                done = [0]

                def taps(count):
                    for _ in range(count):
                        if done[0] == len(DVE_CT) * TAPS:
                            return
                        ct, i = DVE_CT[done[0] // TAPS], done[0] % TAPS
                        w = cols[:, C_CONVW + i * CTL + ct:C_CONVW + i * CTL + ct + 1]
                        if i == 0:
                            dve.wait_ge(u_done, ct + 1)
                            ins = dve.tensor_scalar(cacc[:, ct, :], u[:, ct, 0:T], w, cols[:, C_CONVB + ct:C_CONVB + ct + 1],
                                                    ALU.mult, ALU.add)
                        else:
                            dve.wait_ge(tap_done, done[0])
                            ins = dve.scalar_tensor_tensor(out=cacc[:, ct, :], in0=u[:, ct, i:i + T], scalar=w,
                                                           in1=cacc[:, ct, :], op0=ALU.mult, op1=ALU.add)
                        ins.then_inc(tap_done, 1)
                        done[0] += 1

                norms(0)
                norms(1)
                dve.wait_ge(vecT, 2)
                dve.tensor_copy(cols[:, 2 * KT:], ps[:, 7, 2 * KT:N_COLS]).then_inc(cols_done, 2)
                dve.wait_ge(cols_done, 2)
                for i, c0 in enumerate((C_FW0, C_FW1, C_FW2, C_FB)):
                    for g in range(2):
                        dve.tensor_copy(ffs[:, :, 4 * g + i], cols[:, c0 + g * FT:c0 + (g + 1) * FT]).then_inc(ffs_done, 1)
                split_glu(0)
                dve.wait_ge(mod_mm, KT)
                for q in range(2, 4):
                    dve.tensor_copy(mrow[:, q * HALF:(q + 1) * HALF], ps[0:2, q, :]).then_inc(mrow_out, 1)
                dve.wait_ge(mod_T, 1)
                m = ps[:, 7, 0:4 * KT].rearrange("p (j two) -> p j two", two=2)
                for i, dst in enumerate((modl, modc)):
                    dve.tensor_tensor(out=dst, in0=m[:, :, i], in1=cols[:, C_BMOD:C_BMOD + 16], op=ALU.add).then_inc(mod_done, 1)
                dve.wait_ge(mod_done, 2)
                for src, dst in ((modl, A1), (modc, Ac)):
                    dve.scalar_tensor_tensor(out=dst, in0=src[:, 8:16], scalar=1.0, in1=cols[:, C_NMIX:C_NMIX + KT],
                                             op0=ALU.add, op1=ALU.mult).then_inc(ab_done, 1)
                dve.wait_ge(ab_done, 2)
                dve.wait_ge(xT_out, 2 * KT)
                for k in range(KT):
                    dve.wait_ge(h_hi, k + 1)
                    dve.tensor_scalar(xnT[:, k, :], xnT[:, k, :], A1[:, k:k + 1], modl[:, k:k + 1], ALU.mult, ALU.add).then_inc(h_mod, 1)
                    if k >= 1:
                        dve.wait_ge(h_mod, k)
                        dve.tensor_tensor(out=hx[:, k - 1, 1, :], in0=xnT[:, k - 1, :], in1=f(hx[:, k - 1, 0, :]), op=ALU.subtract).then_inc(h_lo, 1)
                dve.wait_ge(h_mod, KT)
                dve.tensor_tensor(out=hx[:, KT - 1, 1, :], in0=xnT[:, KT - 1, :], in1=f(hx[:, KT - 1, 0, :]), op=ALU.subtract).then_inc(h_lo, 1)
                dve.wait_ge(row_in, 48)
                dve.tensor_scalar(sinks[:, 1, :], sinks[:, 0, :], -1.0, None, ALU.mult).then_inc(ffs_done, 1)
                norms(2)
                split_glu(1)

                for n in range(NGL):
                    if n and n + 1 < NGL:
                        split_glu(n + 1)
                    if n:
                        split_qkv(n - 1)
                    if n == 1:
                        dve.wait_ge(xT_out, 2 * KT + 4)
                        for k in range(KT):
                            dve.wait_ge(hc_hi, k + 1)
                            dve.tensor_scalar(hc32[:, k, :], hc32[:, k, :], Ac[:, k:k + 1], modc[:, k:k + 1], ALU.mult, ALU.add).then_inc(h_mod, 1)
                        dve.wait_ge(h_mod, 2 * KT)
                        dve.tensor_tensor(out=hcx[:, :, 1, :], in0=hc32[:], in1=f(hcx[:, :, 0, :]), op=ALU.subtract).then_inc(hc_lo, 1)
                    if n == NGL - 1:
                        split_qkv(n)
                    if n % 2 == 1:
                        ct, b = n // 2, 2 * (n % 4)
                        dve.wait_ge(gate_done, ct + 1)
                        dve.wait_ge(gl_mm, n + 1)
                        dve.tensor_tensor(out=u[:, ct, PAD:PAD + T], in0=ps[:, b:b + 2, :].rearrange("p b n -> p (b n)"),
                                          in1=u[:, ct, PAD:PAD + T], op=ALU.mult).then_inc(u_done, 1)
                    if n:
                        taps(7)
                taps(len(DVE_CT) * TAPS)

        NK = CT + TT
        tabs = at(18, "tabs", [P, 4, TT, HD])
        qst = [at(26, "qst0", [P, NH, 2, HD], F32R), at(139, "qst1", [P, NH, 2, HD], F32R)]
        qT = at(51, "qT", [P, NH, T], F32R)
        ka = at(129, "ka", [P, NK, NG, HD])
        kb = at(134, "kb", [P, NK, NG, HD])
        kst = at(143, "kst", [P, NK, NG, 2, P], F32R)
        qa = at(167, "qa", [P, 2, QC])
        qb = at(171, "qb", [P, 2, QC])
        kT = at(109, "kT", [P, NG, 2, KEYS], F32R)
        ko = at(195, "ko", [P, NK, NG, HD])
        kraw = kvraw[:, :, 0:NG * HD].rearrange("p t (g d) -> p t g d", g=NG)
        vraw = kvraw[:, :, NG * HD:KVC].rearrange("p t (g d) -> p t g d", g=NG)
        with ExitStack() as s2:
            sem2 = lambda n: s2.enter_context(nc.semaphore(n))
            tab_done = sem2("tab_done")
            ms3, sqrt3, rs3 = sem2("ms3"), sem2("sqrt3"), sem2("rs3")
            k_norm, k_mul, k_rot, k_hi, k_lo = sem2("k_norm"), sem2("k_mul"), sem2("k_rot"), sem2("k_hi"), sem2("k_lo")
            q_norm, q_sin, q_cos, q_rot, q_hi, q_lo = (sem2(n) for n in ("q_norm", "q_sin", "q_cos", "q_rot", "q_hi", "q_lo"))
            qkT, qkT_out = sem2("qkT"), sem2("qkT_out")
            block = s2.enter_context(nc.Block())
            h3 = lambda ap: ap.rearrange("p (h d) -> p h d", h=NH)

            @block.scalar
            def _(act):
                act.wait_ge(ms3, 1)
                act.activation(msq[:], msq[:], ACT.Sqrt).then_inc(sqrt3, 1)
                act.wait_ge(k_rot, 2)
                for r in range(2):
                    act.activation(kst[:, :, :, 0, r * HD:(r + 1) * HD], ko[:], ACT.Copy).then_inc(k_hi, 1)

                def q_high(t):
                    act.wait_ge(q_rot, t + 1)
                    if t >= 2:
                        act.wait_ge(qkT, NK + 2 * (t - 1))
                    act.activation(qst[t % 2][:, :, 0, :], h3(qa[:, t % 2, :]), ACT.Copy).then_inc(q_hi, 1)

                q_high(0)
                for n in range(NK):
                    act.wait_ge(qkT, n + 1)
                    act.activation(kT[:, :, :, n * P:(n + 1) * P],
                                   ps[:, n % 8, :].rearrange("p (g v k) -> p g v k", g=NG, v=2), ACT.Copy).then_inc(qkT_out, 1)
                for t in range(TT):
                    if t + 1 < TT:
                        q_high(t + 1)
                    for hh in range(2):
                        n = NK + 2 * t + hh
                        act.wait_ge(qkT, n + 1)
                        act.activation(qT[:, 4 * hh:4 * hh + 4, t * P:(t + 1) * P],
                                       ps[:, n % 8, :].rearrange("p (h k) -> p h k", h=4), ACT.Copy).then_inc(qkT_out, 1)

            @block.gpsimd
            def _(pool):
                pool.wait_ge(tab_done, CT + 10)
                for t in range(TT):
                    pool.wait_ge(q_norm, t + 1)
                    if t >= 2:
                        pool.wait_ge(q_rot, t - 1)
                    a4 = qa[:, t % 2, :].rearrange("p (e x d) -> p e x d", e=2 * NH, x=2)
                    b4 = qb[:, t % 2, :].rearrange("p (e x d) -> p e x d", e=2 * NH, x=2)
                    sn = tabs[:, 1, t, :].rearrange("p (a x d) -> p a x d", a=2, x=2)
                    for half in range(2):
                        for a in range(2):
                            last = pool.tensor_tensor(out=b4[:, a::2, half, :], in0=a4[:, a::2, 1 - half, :],
                                                      in1=sn[:, a:a + 1, half, :].to_broadcast([P, NH, 16]), op=ALU.mult)
                            last.then_inc(q_sin, 1)

            @block.vector
            def _(dve):
                for m in range(CT):
                    dve.memset(msq[:, m, 0:NH], 1.0).then_inc(tab_done, 1)
                dve.wait_ge(tab_done, CT)
                dve.tensor_scalar(msq[:], msq[:], 1.0 / HD, EPS, ALU.mult, ALU.add).then_inc(ms3, 1)
                dve.wait_ge(cs_in, 16)
                sn = cs[:, 1].rearrange("p t (a x d) -> p t a x d", a=2, x=2)
                for i in range(2):
                    dve.tensor_tensor(out=tabs[:, 2 * i], in0=cs[:, 0], in1=qkw[:, i:i + 1, :].to_broadcast([P, TT, HD]),
                                      op=ALU.mult).then_inc(tab_done, 1)
                    w4 = qkw[:, i, :].rearrange("p (a x d) -> p a x d", a=2, x=2)
                    dst = tabs[:, 2 * i + 1].rearrange("p t (a x d) -> p t a x d", a=2, x=2)
                    for half in range(2):
                        for a in range(2):
                            dve.tensor_tensor(out=dst[:, :, a, half, :], in0=sn[:, :, a, half, :],
                                              in1=w4[:, a:a + 1, 1 - half, :].to_broadcast([P, TT, 16]), op=ALU.mult).then_inc(tab_done, 1)
                dve.wait_ge(sqrt3, 1)
                dve.reciprocal(msq[:], msq[:]).then_inc(rs3, 1)
                dve.wait_ge(rs3, 1)
                dve.tensor_tensor(out=ka[:], in0=kraw, in1=msq[:, :, NH:NH + NG].unsqueeze(3).to_broadcast([P, NK, NG, HD]),
                                  op=ALU.mult).then_inc(k_norm, 1)

                def q_normed(t):
                    if t >= 2:
                        dve.wait_ge(q_lo, t - 1)
                    dve.tensor_tensor(out=h3(qa[:, t % 2, :]), in0=h3(qraw[:, t, :]),
                                      in1=msq[:, CT + t, 0:NH].unsqueeze(2).to_broadcast([P, NH, HD]), op=ALU.mult).then_inc(q_norm, 1)

                q_normed(0)
                q_normed(1)
                dve.wait_ge(k_norm, 1)
                dve.wait_ge(tab_done, CT + 10)
                dve.tensor_tensor(out=ko[:, 0:CT], in0=ka[:, 0:CT], in1=qkw[:, 1:2, :].unsqueeze(1).to_broadcast([P, CT, NG, HD]),
                                  op=ALU.mult).then_inc(k_rot, 1)
                dve.tensor_tensor(out=ko[:, CT:], in0=ka[:, CT:], in1=tabs[:, 2].unsqueeze(2).to_broadcast([P, TT, NG, HD]),
                                  op=ALU.mult).then_inc(k_mul, 1)
                ka5 = ka[:].rearrange("p t g (a x d) -> p t g a x d", a=2, x=2)
                kb5 = kb[:].rearrange("p t g (a x d) -> p t g a x d", a=2, x=2)
                sk = tabs[:, 3].rearrange("p t (a x d) -> p t a x d", a=2, x=2)
                for g in range(NG):
                    for half in range(2):
                        dve.tensor_tensor(out=kb5[:, CT:, g, :, half, :], in0=ka5[:, CT:, g, :, 1 - half, :], in1=sk[:, :, :, half, :],
                                          op=ALU.mult).then_inc(k_mul, 1)
                dve.wait_ge(k_mul, 5)
                dve.tensor_tensor(out=ko[:, CT:], in0=ko[:, CT:], in1=kb[:, CT:], op=ALU.add).then_inc(k_rot, 1)

                def q_rotate(t):
                    dve.wait_ge(q_sin, 4 * (t + 1))
                    dve.tensor_tensor(out=h3(qa[:, t % 2, :]), in0=h3(qa[:, t % 2, :]), in1=tabs[:, 0, t:t + 1, :].to_broadcast([P, NH, HD]),
                                      op=ALU.mult).then_inc(q_cos, 1)
                    dve.wait_ge(q_cos, t + 1)
                    dve.tensor_tensor(out=qa[:, t % 2, :], in0=qa[:, t % 2, :], in1=qb[:, t % 2, :], op=ALU.add).then_inc(q_rot, 1)

                q_rotate(0)
                for r in range(2):
                    dve.wait_ge(k_hi, r + 1)
                    dve.tensor_tensor(out=kst[:, :, :, 1, r * HD:(r + 1) * HD], in0=ko[:], in1=f(kst[:, :, :, 0, r * HD:(r + 1) * HD]),
                                      op=ALU.subtract).then_inc(k_lo, 1)
                for t in range(TT):
                    dve.wait_ge(q_hi, t + 1)
                    dve.tensor_tensor(out=qst[t % 2][:, :, 1, :], in0=h3(qa[:, t % 2, :]), in1=f(qst[t % 2][:, :, 0, :]),
                                      op=ALU.subtract).then_inc(q_lo, 1)
                    if t + 2 < TT:
                        q_normed(t + 2)
                    if t + 1 < TT:
                        q_rotate(t + 1)

            @block.tensor
            def _(pe):
                pe.wait_ge(k_lo, 2)
                for n in range(NK + 2 * TT):
                    if n >= 8:
                        pe.wait_ge(qkT_out, n - 7)
                    if n < NK:
                        src = [kst[:, n, j // 2, j % 2, :] for j in range(4)]
                    else:
                        t, hh = divmod(n - NK, 2)
                        pe.wait_ge(q_lo, t + 1)
                        src = [qst[t % 2][:, 4 * hh + j].rearrange("p v d -> p (v d)") for j in range(4)]
                    for j in range(4):
                        last = pe.transpose(ps[:, n % 8, j * P:(j + 1) * P].bitcast(F32R), src[j], identr[:])
                    last.then_inc(qkT, 1)

        SW = CTX + 3 * P
        NGRP = 2 * TT
        NPT = 3
        NW = 4
        wm2 = at(18, "wm2", [P, NW, D])
        pbuf = [at(129, "p0", [P, GQ, SW]), at(83, "p1", [P, GQ, SW])]
        pt = at(93, "pt", [P, NPT, HALF])
        on = at(15, "on", [P, GQ * HD])
        sqc = at(175, "sqc", [P, CTL, T])
        rstd = at(191, "rstd", [P, T])
        shift2, scale2 = at(195, "shift2", [P, D]), at(199, "scale2", [P, D])
        st = [scal[:, 144 + 16 * i:160 + 16 * i].rearrange("p (s h) -> p s h", s=4) for i in range(2)]
        wo_raw = at(18, "wo_raw", [P, 4, D])

        def key_tiles(i):
            return [0, 1] + [CT + j for j in (i - 1, i, i + 1) if 0 <= j < TT]

        first_item = [0]
        for n in range(NGRP):
            first_item.append(first_item[-1] + len(key_tiles(n // NG)))
        SECTIONS = [(2, g1b), (3, shift2), (4, scale2), (5, g2b)]
        NMOD = len(SECTIONS) * KT
        with ExitStack() as s3:
            sem3 = lambda n: s3.enter_context(nc.semaphore(n))
            wm2_in = [sem3(f"wm2_in{i}") for i in range(NW)]
            zero_done, brow_in, mod_mul, mod_acc, row_mm, row_out = (
                sem3(n) for n in ("zero_done", "brow_in", "mod_mul", "mod_acc", "row_mm", "row_out"))
            col_mm, col_add, a2_done = sem3("col_mm"), sem3("col_add"), sem3("a2_done")
            qk_mm, max_done, negm_done, exp_done = sem3("qk_mm"), sem3("max_done"), sem3("negm_done"), sem3("exp_done")
            arg_done, sexp_done, den_done, rec_done = (sem3(n) for n in ("arg_done", "sexp_done", "den_done", "rec_done"))
            pt_T, pt_out, pv_mm, on_done, oT, o_hi, o_lo = (sem3(n) for n in ("pt_T", "pt_out", "pv_mm", "on_done", "oT", "o_hi", "o_lo"))
            mean_mm, cent, sq5, var_mm, eps_done, sqrt5, rec5, scaled, silu5, u_hi, u_lo = (
                sem3(n) for n in ("mean_mm", "cent", "sq5", "var_mm", "eps_done", "sqrt5", "rec5", "scaled", "silu5", "u_hi", "u_lo"))
            block = s3.enter_context(nc.Block())
            half = lambda hh: slice(hh * HALF, (hh + 1) * HALF)

            @block.sync
            def _(sp):
                for n in range(NMOD):
                    if n >= NW:
                        sp.wait_ge(mod_acc, n - NW + 1)
                    sec, k = SECTIONS[n // KT][0], n % KT
                    sp.dma_start(wm2[:, n % NW, :], w_mod[0, k * P:(k + 1) * P, sec * D:(sec + 1) * D]).then_inc(wm2_in[n % NW], 16)
                    if n == NW - 1:
                        sp.wait_ge(zero_done, 2)
                        for sec, dst in (SECTIONS[0], SECTIONS[3]):
                            sp.dma_start(dst[0:1, :], b_mod[0:1, sec * D:(sec + 1) * D]).then_inc(brow_in, 16)
                for k in range(4):
                    sp.wait_ge(mod_acc, NMOD - 3 + k)
                    sp.dma_start(wo_raw[:, k, :], w_out[0, k * P:(k + 1) * P, :]).then_inc(wo_in[k], 16)

            @block.gpsimd
            def _(pool):
                for dst in (g1b, g2b):
                    pool.memset(dst[:], 0.0).then_inc(zero_done, 1)
                muls = 0
                for n in range(NMOD):
                    k, dst, w = n % KT, SECTIONS[n // KT][1], wm2[:, n % NW, :]
                    pool.wait_ge(wm2_in[n % NW], 16 * (n // NW + 1))
                    if n == 3 * KT:
                        pool.wait_ge(rec5, 4)
                        for ct in range(CTL):
                            pool.tensor_tensor(out=cacc[:, ct, :], in0=cacc[:, ct, :], in1=rstd[:], op=ALU.mult).then_inc(scaled, 1)
                    if k == 0 and dst in (shift2, scale2):
                        pool.tensor_scalar(dst[:], w, nat[:, k, 0:1], 1.0, ALU.mult, ALU.mult).then_inc(mod_acc, 1)
                        continue
                    pool.tensor_scalar(w, w, nat[:, k, 0:1], 1.0, ALU.mult, ALU.mult).then_inc(mod_mul, 1)
                    muls += 1
                    pool.wait_ge(mod_mul, muls)
                    if n == 0:
                        pool.wait_ge(brow_in, 32)
                    else:
                        pool.wait_ge(mod_acc, n)
                    pool.tensor_tensor(out=dst[:], in0=dst[:], in1=w, op=ALU.add).then_inc(mod_acc, 1)

            def head_steps(n):
                i, g = divmod(n, NG)
                return i, g, key_tiles(i)

            @block.tensor
            def _(pe):
                def scores(n, hl):
                    i, g, kts = head_steps(n)
                    hh = GQ * n + hl
                    b = 2 * (hh % 2)
                    if hh >= 2:
                        pe.wait_ge(exp_done, hh - 1)
                    q = qT[:, GQ * g + hl, i * P:(i + 1) * P]
                    lat = kts[2] * P
                    pe.matmul(ps[:, b, 0:CTX], q, kT[:, g, 0, 0:CTX], start=True, stop=False)
                    pe.matmul(ps[:, b, 0:CTX], q, kT[:, g, 1, 0:CTX], start=False, stop=True)
                    o = ps[:, b, CTX:CTX + 2 * P]
                    pe.matmul(o, q, kT[:, g, 0, lat:lat + 2 * P], start=True, stop=False)
                    last = pe.matmul(o, q, kT[:, g, 1, lat:lat + 2 * P], start=False, stop=False)
                    if i > 0:
                        last = pe.matmul(ps[:, b, CTX:CTX + P], identr[:], mask_prev[:], start=False, stop=True)
                    else:
                        last = pe.matmul(ps[:, b, CTX + P:CTX + 2 * P], identr[:], mask_next[:], start=False, stop=True)
                    if 0 < i < TT - 1:
                        o = ps[:, b + 1, 0:P]
                        pe.matmul(o, q, kT[:, g, 0, lat + 2 * P:lat + 3 * P], start=True, stop=False)
                        pe.matmul(o, q, kT[:, g, 1, lat + 2 * P:lat + 3 * P], start=False, stop=False)
                        last = pe.matmul(o, identr[:], mask_next[:], start=False, stop=True)
                    last.then_inc(qk_mm, 1)

                def turn(n, j):
                    it = first_item[n] + j
                    if j == 0:
                        pe.wait_ge(exp_done, GQ * (n + 1))
                    if it >= 2:
                        pe.wait_ge(pt_out, it - 1)
                    for hl in range(GQ):
                        last = pe.transpose(ps[:, 4 + it % 2, hl * P:(hl + 1) * P], pbuf[n % 2][:, hl, j * P:(j + 1) * P], ident[:])
                    last.then_inc(pt_T, 1)

                def values(n, j):
                    i, g, kts = head_steps(n)
                    it = first_item[n] + j
                    if j == 0 and n:
                        pe.wait_ge(on_done, n)
                    pe.wait_ge(pt_out, it + 1)
                    for hl in range(GQ):
                        last = pe.matmul(ps[:, 6, hl * HD:(hl + 1) * HD], pt[:, it % NPT, hl * P:(hl + 1) * P], vraw[:, kts[j], g, :],
                                         start=(j == 0 and hl == 0), stop=(j == len(kts) - 1), skip_group_check=True)
                    last.then_inc(pv_mm, 1)

                def turn_outputs(n):
                    pe.wait_ge(on_done, n + 1)
                    bank_read(n + 1)
                    for r in range(2):
                        last = pe.transpose(ps[:, 7, r * P:(r + 1) * P], on[:, r * P:(r + 1) * P], ident[:])
                    last.then_inc(oT, 1)

                def mean_of(buf, hh, signal):
                    for ct in range(CTL):
                        last = pe.matmul(ps[:, 7, :], meanw[:], buf[:, ct, half(hh)], start=(ct == 0), stop=(ct == CTL - 1))
                    last.then_inc(signal, 1)

                def beside(n):
                    if n >= 2:
                        pe.wait_ge(o_lo, n - 1)
                    if n in (0, 1):
                        if n:
                            pe.wait_ge(cent, CTL)
                        mean_of(cacc, n, mean_mm)
                    elif n in (2, 3):
                        pe.wait_ge(sq5, CTL * (n - 1))
                        mean_of(sqc, n - 2, var_mm)

                def bank_read(n):
                    if n in (0, 1):
                        pe.wait_ge(cent, CTL * (n + 1))
                    elif n in (2, 3):
                        pe.wait_ge(eps_done, n - 1)
                    if n >= 2:
                        pe.wait_ge(o_lo, n - 1)

                for hl in range(GQ):
                    scores(0, hl)
                for n in range(NGRP):
                    m = len(key_tiles(n // NG))
                    for j in range(m):
                        if n + 1 < NGRP and j < GQ:
                            scores(n + 1, j)
                        turn(n, j)
                        if j == 1 and n < 4:
                            beside(n)
                        if j == 3 and n:
                            turn_outputs(n - 1)
                        if j:
                            values(n, j - 1)
                    values(n, m - 1)
                for c, dst in enumerate((shift2, scale2)):
                    pe.wait_ge(mod_acc, (2 + c) * KT)
                    pe.wait_ge(pt_out, first_item[NGRP])
                    for j in range(KT):
                        last = pe.matmul(ps[:, 4, c * KT + j:c * KT + j + 1], dst[:, j * P:(j + 1) * P], ones[:, 0:1], start=True, stop=True)
                last.then_inc(col_mm, 1)
                pe.wait_ge(mod_acc, NMOD)
                for r in range(2):
                    for hh in range(2):
                        pe.matmul(ps[:, 2 * r + hh, :], ones[:], (g1b, g2b)[r][:, half(hh)], start=True, stop=True).then_inc(row_mm, 1)
                turn_outputs(NGRP - 1)

            def score_ap(hh, w):
                b = 2 * (hh % 2)
                return ps[:, b:b + 2, :].rearrange("p b n -> p (b n)")[:, 0:w]

            @block.scalar
            def _(act):
                def exps(n, hl):
                    hh = GQ * n + hl
                    w = P * len(key_tiles(n // NG))
                    act.wait_ge(negm_done, hh + 1)
                    if hl == 0 and n >= 2:
                        act.wait_ge(pt_T, first_item[n - 1])
                    act.activation(pbuf[n % 2][:, hl, 0:w], score_ap(hh, w), ACT.Exp, scale=SCALE,
                                   bias=st[n % 2][:, 1, hl:hl + 1], accum_out=st[n % 2][:, 2, hl:hl + 1]).then_inc(exp_done, 1)

                def output_high(n):
                    i, g = divmod(n, NG)
                    act.wait_ge(oT, n + 1)
                    act.activation(hx[:, 2 * g:2 * g + 2, 0, i * P:(i + 1) * P],
                                   ps[:, 7, 0:2 * P].rearrange("p (r q) -> p r q", r=2), ACT.Copy).then_inc(o_hi, 1)

                def beside(n):
                    if n in (0, 1):
                        hh = n
                        for ct in range(CTL):
                            act.wait_ge(cent, CTL * hh + ct + 1)
                            act.activation(sqc[:, ct, half(hh)], cacc[:, ct, half(hh)], ACT.Square).then_inc(sq5, 1)
                    elif n == 4:
                        act.wait_ge(eps_done, 2)
                        act.activation(rstd[:], rstd[:], ACT.Sqrt).then_inc(sqrt5, 1)

                for hl in range(GQ):
                    exps(0, hl)
                for n in range(NGRP):
                    i, g, kts = head_steps(n)
                    act.wait_ge(arg_done, n + 1)
                    act.activation(st[n % 2][:, 3, :], st[n % 2][:, 3, :], ACT.Exp).then_inc(sexp_done, 1)
                    for j in range(len(kts)):
                        it = first_item[n] + j
                        act.wait_ge(pt_T, it + 1)
                        if it >= NPT:
                            act.wait_ge(pv_mm, it - NPT + 1)
                        act.activation(pt[:, it % NPT, :], ps[:, 4 + it % 2, :], ACT.Copy).then_inc(pt_out, 1)
                        if n + 1 < NGRP and j < GQ:
                            exps(n + 1, j)
                        if j == 3 and n:
                            output_high(n - 1)
                    beside(n)
                act.wait_ge(var_mm, 2)
                for ct in range(CTL):
                    act.wait_ge(scaled, CTL)
                    act.activation(cacc[:, ct, :], cacc[:, ct, :], ACT.Silu, scale=cols[:, C_CNW + ct:C_CNW + ct + 1],
                                   bias=cols[:, C_CNB + ct:C_CNB + ct + 1]).then_inc(silu5, 1)
                act.wait_ge(col_mm, 1)
                for ct in range(CTL):
                    act.wait_ge(silu5, ct + 1)
                    act.activation(hx[:, CTL + ct, 0, :], cacc[:, ct, :], ACT.Copy).then_inc(u_hi, 1)
                output_high(NGRP - 1)
                for i in range(4):
                    act.wait_ge(row_mm, 4)
                    act.activation((g1b, g2b)[i // 2][:, half(i % 2)], ps[:, i, :], ACT.Copy).then_inc(row_out, 1)

            @block.vector
            def _(dve):
                def maxima(n, hl):
                    hh = GQ * n + hl
                    w = P * len(key_tiles(n // NG))
                    s = st[n % 2]
                    dve.wait_ge(qk_mm, hh + 1)
                    dve.reduce_max(s[:, 0, hl:hl + 1], score_ap(hh, w), axis=AX.X).then_inc(max_done, 1)
                    dve.wait_ge(max_done, hh + 1)
                    h = GQ * (n % NG) + hl
                    dve.tensor_scalar(s[:, 1, hl:hl + 1], s[:, 0, hl:hl + 1], -SCALE, sinks[:, 1, h:h + 1],
                                      ALU.mult, ALU.min).then_inc(negm_done, 1)

                def output_low(n):
                    i, g = divmod(n, NG)
                    dve.wait_ge(o_hi, n + 1)
                    dve.tensor_tensor(out=hx[:, 2 * g:2 * g + 2, 1, i * P:(i + 1) * P],
                                      in0=ps[:, 7, 0:2 * P].rearrange("p (r q) -> p r q", r=2),
                                      in1=f(hx[:, 2 * g:2 * g + 2, 0, i * P:(i + 1) * P]), op=ALU.subtract).then_inc(o_lo, 1)

                def beside(n):
                    if n in (0, 1):
                        hh = n
                        dve.wait_ge(mean_mm, n + 1)
                        for ct in range(CTL):
                            dve.tensor_tensor(out=cacc[:, ct, half(hh)], in0=cacc[:, ct, half(hh)], in1=ps[:, 7, :],
                                              op=ALU.subtract).then_inc(cent, 1)
                    elif n in (2, 3):
                        hh = n - 2
                        dve.wait_ge(var_mm, n - 1)
                        dve.tensor_scalar(rstd[:, half(hh)], ps[:, 7, :], EPS, None, ALU.add).then_inc(eps_done, 1)
                    elif n in (5, 6, 7, 8):
                        q = slice((n - 5) * CTX, (n - 4) * CTX)
                        if n == 5:
                            dve.wait_ge(sqrt5, 1)
                        dve.reciprocal(rstd[:, q], rstd[:, q]).then_inc(rec5, 1)

                for hl in range(GQ):
                    maxima(0, hl)
                for n in range(NGRP):
                    i, g, kts = head_steps(n)
                    s = st[n % 2]
                    dve.wait_ge(negm_done, GQ * (n + 1))
                    dve.tensor_tensor(out=s[:, 3, :], in0=sinks[:, 0, GQ * g:GQ * (g + 1)], in1=s[:, 1, :], op=ALU.add).then_inc(arg_done, 1)
                    for j in range(len(kts)):
                        if n + 1 < NGRP and j < GQ:
                            maxima(n + 1, j)
                        if j == 2:
                            beside(n)
                        if j == 3 and n:
                            output_low(n - 1)
                    dve.wait_ge(sexp_done, n + 1)
                    dve.wait_ge(exp_done, GQ * (n + 1))
                    dve.tensor_tensor(out=s[:, 2, :], in0=s[:, 2, :], in1=s[:, 3, :], op=ALU.add).then_inc(den_done, 1)
                    dve.wait_ge(den_done, n + 1)
                    dve.reciprocal(s[:, 2, :], s[:, 2, :]).then_inc(rec_done, 1)
                    dve.wait_ge(rec_done, n + 1)
                    dve.wait_ge(pv_mm, first_item[n + 1])
                    if n:
                        dve.wait_ge(oT, n)
                    dve.tensor_tensor(out=on[:].rearrange("p (h d) -> p h d", h=GQ),
                                      in0=ps[:, 6, 0:GQ * HD].rearrange("p (h d) -> p h d", h=GQ),
                                      in1=s[:, 2, :].unsqueeze(2).to_broadcast([P, GQ, HD]), op=ALU.mult).then_inc(on_done, 1)
                dve.wait_ge(col_mm, 1)
                dve.tensor_tensor(out=mod2, in0=ps[:, 4, 0:2 * KT], in1=cols[:, C_BMOD + 3 * KT:C_BMOD + 5 * KT], op=ALU.add).then_inc(col_add, 1)
                dve.wait_ge(col_add, 1)
                dve.scalar_tensor_tensor(out=A2, in0=mod2[:, KT:], scalar=1.0, in1=cols[:, C_NFFN:C_NFFN + KT],
                                         op0=ALU.add, op1=ALU.mult).then_inc(a2_done, 1)
                for ct in range(CTL):
                    dve.wait_ge(u_hi, ct + 1)
                    dve.tensor_tensor(out=hx[:, CTL + ct, 1, :], in0=cacc[:, ct, :], in1=f(hx[:, CTL + ct, 0, :]), op=ALU.subtract).then_inc(u_lo, 1)
                output_low(NGRP - 1)

        NXT = 4
        woh = at(51, "woh", [P, KT, D], F32R)
        wol = at(83, "wol", [P, KT, D], F32R)
        xt = at(34.75, "xt", [P, NXT, D])
        hm = at(18, "hm", [P, 2, KT, P])
        gm = at(26, "gm", [P, 2, D])
        uph = at(115, "uph", [P, 2, KT, P], F32R)
        upl = at(123, "upl", [P, 2, KT, P], F32R)
        up_raw = at(131, "up_raw", [P, 2, KT, P])
        wup = w_up[0].rearrange("(k p) n -> p k n", p=P)

        def up_half(pe, g, bank, hh):
            o, c_ = ps[:, bank, :], slice(hh * HALF, (hh + 1) * HALF)
            for k in range(KT):
                pe.matmul(o, uph[:, g, k, :], hx[:, k, 0, c_], start=(k == 0), stop=False)
                pe.matmul(o, uph[:, g, k, :], hx[:, k, 1, c_], start=False, stop=False)
                last = pe.matmul(o, upl[:, g, k, :], hx[:, k, 0, c_], start=False, stop=(k == KT - 1))
            return last

        def up_split_high(act, g):
            act.activation(uph[:, g], up_raw[:, g], ACT.Copy).then_inc(up_hi, 1)

        def up_split_low(dve, g):
            dve.tensor_tensor(out=upl[:, g], in0=up_raw[:, g], in1=f(uph[:, g]), op=ALU.subtract).then_inc(up_lo, 1)

        SPLIT_T = 5
        with ExitStack() as s4:
            sem4 = lambda n: s4.enter_context(nc.semaphore(n))
            wo_hi, wo_lo, xt_in = sem4("wo_hi"), sem4("wo_lo"), [sem4(f"xt_in{i}") for i in range(NXT)]
            wo_mm, gated, x1_done, x1_out = sem4("wo_mm"), sem4("gated"), sem4("x1_done"), sem4("x1_out")
            ssq, ms5, sq2, r5, xn5, xT5, mod5, h2_hi, h2_lo = (
                sem4(n) for n in ("ssq", "ms5", "sq2", "r5", "xn5", "xT5", "mod5", "h2_hi", "h2_lo"))
            block = s4.enter_context(nc.Block())

            @block.sync
            def _(sp):
                for k in range(4, KT):
                    sp.wait_ge(wo_lo, k - 3)
                    sp.dma_start(wo_raw[:, k % 4, :], w_out[0, k * P:(k + 1) * P, :]).then_inc(wo_in[k % 4], 16)
                for t in range(NXT):
                    sp.dma_start(xt[:, t, :], x[0, t * P:(t + 1) * P, :]).then_inc(xt_in[t], 16)
                for g in range(2):
                    sp.dma_start(up_raw[:, g], wup[:, :, g * FF:g * FF + P]).then_inc(up_in[g], 16)
                for t in range(TT):
                    sp.wait_ge(x1_done, t + 1)
                    sp.dma_start(x1_dram[t * P:(t + 1) * P, :], xt[:, t % NXT, :]).then_inc(x1_out, 16)
                    sp.wait_ge(x1_out, 16 * (t + 1))
                    if t + NXT < TT:
                        sp.wait_ge(xn5, t + 1)
                        sp.dma_start(xt[:, t % NXT, :], x[0, (t + NXT) * P:(t + NXT + 1) * P, :]).then_inc(xt_in[t % NXT], 16)

            @block.tensor
            def _(pe):
                def project(t, k):
                    b = 4 + 2 * (t % 2)
                    if k == 0 and t >= 2:
                        pe.wait_ge(gated, t - 1)
                    for v in range(2):
                        a = hx[:, k, v, t * P:(t + 1) * P]
                        for lo in range(2 - v):
                            for hh in range(2):
                                last = pe.matmul(ps[:, b + hh, :], a, (woh, wol)[lo][:, k, hh * HALF:(hh + 1) * HALF],
                                                 start=(k == 0 and v == 0 and lo == 0), stop=(k == KT - 1 and v == 1))
                    if k == KT - 1:
                        last.then_inc(wo_mm, 1)

                def turn(t):
                    b = 2 * (t % 2)
                    pe.wait_ge(xn5, t + 1)
                    if t >= 2:
                        pe.wait_ge(mod5, t - 1)
                    for k in range(KT):
                        last = pe.transpose(ps[:, b + k // 4, (k % 4) * P:(k % 4 + 1) * P], gm[:, t % 2, k * P:(k + 1) * P], ident[:])
                    last.then_inc(xT5, 1)

                for k in range(KT):
                    pe.wait_ge(wo_lo, k + 1)
                    for t in range(2):
                        project(t, k)
                for t in range(2, TT):
                    for k in range(KT):
                        project(t, k)
                        if t == 2 and k == 3:
                            turn(0)
                        if k == 5:
                            turn(t - 1)
                pe.wait_ge(h2_lo, TT // 2)
                pe.wait_ge(up_lo, 1)
                up_half(pe, 0, 4, 0)
                turn(TT - 1)
                pe.wait_ge(up_lo, 2)
                pe.wait_ge(gated, TT)
                up_half(pe, 1, 6, 0)

            @block.scalar
            def _(act):
                for k in range(KT):
                    act.wait_ge(wo_in[k % 4], 16 * (k // 4 + 1))
                    act.activation(woh[:, k, :], wo_raw[:, k % 4, :], ACT.Copy).then_inc(wo_hi, 1)

                def square(t):
                    act.wait_ge(x1_done, t + 1)
                    if t >= 2:
                        act.wait_ge(h2_lo, t - 1)
                    act.activation(hm[:, t % 2].rearrange("p k n -> p (k n)"), xt[:, t % NXT, :], ACT.Square,
                                   accum_out=ss2[:, t:t + 1]).then_inc(ssq, 1)
                    act.wait_ge(ms5, t + 1)
                    act.activation(ss2[:, t:t + 1], ss2[:, t:t + 1], ACT.Sqrt).then_inc(sq2, 1)

                def modulate(t):
                    act.wait_ge(xT5, t + 1)
                    b = 2 * (t % 2)
                    for k in range(KT):
                        ins = act.activation(hm[:, t % 2, k, :], ps[:, b + k // 4, (k % 4) * P:(k % 4 + 1) * P], ACT.Identity,
                                             scale=A2[:, k:k + 1], bias=mod2[:, k:k + 1])
                    ins.then_inc(mod5, 1)
                    act.wait_ge(mod5, t + 1)
                    act.activation(hx[:, :, 0, t * P:(t + 1) * P], hm[:, t % 2], ACT.Copy).then_inc(h2_hi, 1)

                for t in range(2):
                    square(t)
                for t in range(2):
                    modulate(t)
                for t in range(2, TT):
                    square(t)
                    modulate(t)
                    if t == SPLIT_T:
                        for g in range(2):
                            act.wait_ge(up_in[g], 16)
                            up_split_high(act, g)

            @block.vector
            def _(dve):
                both = lambda b: ps[:, b:b + 2, :].rearrange("p b n -> p (b n)")
                for k in range(KT):
                    dve.wait_ge(wo_hi, k + 1)
                    dve.tensor_tensor(out=wol[:, k, :], in0=wo_raw[:, k % 4, :], in1=f(woh[:, k, :]), op=ALU.subtract).then_inc(wo_lo, 1)

                def residual(t):
                    b = 4 + 2 * (t % 2)
                    v = xt[:, t % NXT, :]
                    dve.wait_ge(wo_mm, t + 1)
                    if t >= 2:
                        dve.wait_ge(xT5, t - 1)
                    dve.tensor_tensor(out=gm[:, t % 2], in0=both(b), in1=g1b[:], op=ALU.mult).then_inc(gated, 1)
                    dve.wait_ge(xt_in[t % NXT], 16 * (t // NXT + 1))
                    dve.wait_ge(gated, t + 1)
                    dve.tensor_tensor(out=v, in0=v, in1=gm[:, t % 2], op=ALU.add).then_inc(x1_done, 1)
                    dve.wait_ge(ssq, t + 1)
                    dve.tensor_scalar(ss2[:, t:t + 1], ss2[:, t:t + 1], 1.0 / D, EPS, ALU.mult, ALU.add).then_inc(ms5, 1)
                    dve.wait_ge(sq2, t + 1)
                    dve.reciprocal(rs2[:, t:t + 1], ss2[:, t:t + 1]).then_inc(r5, 1)
                    dve.wait_ge(r5, t + 1)
                    dve.wait_ge(x1_done, t + 1)
                    dve.tensor_scalar(gm[:, t % 2], v, rs2[:, t:t + 1], None, ALU.mult).then_inc(xn5, 1)

                def low(t):
                    dve.wait_ge(h2_hi, t + 1)
                    dve.tensor_tensor(out=hx[:, :, 1, t * P:(t + 1) * P], in0=hm[:, t % 2], in1=f(hx[:, :, 0, t * P:(t + 1) * P]),
                                      op=ALU.subtract).then_inc(h2_lo, 1)

                for t in range(2):
                    residual(t)
                for t in range(2):
                    low(t)
                for t in range(2, TT):
                    residual(t)
                    low(t)
                    if t == SPLIT_T:
                        for g in range(2):
                            dve.wait_ge(up_hi, g + 1)
                            up_split_low(dve, g)

        hid = at(18, "hid", [P, FT, T])
        y = at(106, "y", [P, 2, T])
        dn_raw = at(139, "dn_raw", [P, 2, HALF])
        with ExitStack() as s5:
            sem5 = lambda n: s5.enter_context(nc.semaphore(n))
            up_mm = sem5("up_mm")
            cur_done, mid_tap, left_tap, side_taps, act_done, hid_done = (
                sem5(n) for n in ("cur_done", "mid_tap", "left_tap", "side_taps", "act_done", "hid_done"))
            block = s5.enter_context(nc.Block())

            def pairs(eng, body):
                for j in range(2):
                    body(j, j % 2, True, False)
                with eng.Fori(2, FT - 2, 2) as i:
                    for s in range(2):
                        body(i + s, s, False, False)
                for j in range(FT - 2, FT):
                    body(j, j % 2, False, True)

            @block.sync
            def _(sp):
                for s in range(2):
                    sp.dma_start(dn_raw[:, s, :], w_down[0, s * P:(s + 1) * P, 0:HALF]).then_inc(dn_in[s], 16)
                with sp.Fori(1, FT) as j:
                    for g in range(2):
                        sp.wait_ge(up_lo, 2 * j + g - 1)
                        sp.dma_start(up_raw[:, g], wup[:, :, bass.ds(g * FF + j * P, P)]).then_inc(up_in[g], 16)

            @block.tensor
            def _(pe):
                def body(j, s, first, final):
                    for g in range(2):
                        b = 4 * (1 - s) + 2 * g
                        pe.wait_ge(up_lo, 2 * j + g + 1)
                        if not first:
                            pe.wait_ge(side_taps, 2 * (j - 2) + g + 1)
                        if first and s == 0:
                            up_half(pe, g, b + 1, 1).then_inc(up_mm, 1)
                            continue
                        for k in range(KT):
                            for hh in range(2):
                                o, c_ = ps[:, b + hh, :], slice(hh * HALF, (hh + 1) * HALF)
                                pe.matmul(o, uph[:, g, k, :], hx[:, k, 0, c_], start=(k == 0), stop=False)
                                pe.matmul(o, uph[:, g, k, :], hx[:, k, 1, c_], start=False, stop=False)
                            for hh in range(2):
                                o, c_ = ps[:, b + hh, :], slice(hh * HALF, (hh + 1) * HALF)
                                last = pe.matmul(o, upl[:, g, k, :], hx[:, k, 0, c_], start=False, stop=(k == KT - 1))
                        last.then_inc(up_mm, 1)

                pairs(pe, body)

            def bank_pair(s, g):
                b = 4 * (1 - s) + 2 * g
                return ps[:, b:b + 2, :].rearrange("p b n -> p (b n)")

            @block.scalar
            def _(act):
                def split(j, g):
                    act.wait_ge(up_in[g], 16 * (j + 1))
                    act.wait_ge(up_mm, 2 * (j - 1) + g + 1)
                    up_split_high(act, g)

                def body(j, s, first, final, last=False):
                    for g in range(2):
                        if not last:
                            split(j + 1, g)
                        act.wait_ge(up_mm, 2 * j + g + 1)
                        act.wait_ge(cur_done, j + 1)
                        if not (first and s == 0):
                            act.wait_ge(hid_done, j)
                        act.activation(y[:, g, :], bank_pair(s, g), ACT.Identity, scale=ffcur[s][:, 4 * g + 1:4 * g + 2],
                                       bias=ffcur[s][:, 4 * g + 3:4 * g + 4]).then_inc(mid_tap, 1)
                    act.wait_ge(side_taps, 2 * j + 1)
                    act.activation(y[:, 0, :], y[:, 0, :], ACT.Silu).then_inc(act_done, 1)

                for j in range(2):
                    body(j, j % 2, True, False)
                with act.Fori(2, FT - 2, 2) as i:
                    for s in range(2):
                        body(i + s, s, False, False)
                body(FT - 2, 0, False, True)
                body(FT - 1, 1, False, True, last=True)

            @block.vector
            def _(dve):
                def split(j, g):
                    dve.wait_ge(up_hi, 2 * j + g + 1)
                    up_split_low(dve, g)

                def body(j, s, first, final, last=False):
                    dve.tensor_scalar(ffcur[s].unsqueeze(1), ffs[:, bass.ds(j, 1), :], 1.0, None, ALU.mult).then_inc(cur_done, 1)
                    dve.wait_ge(cur_done, j + 1)
                    for g in range(2):
                        if not last:
                            split(j + 1, g)
                        p = bank_pair(s, g)
                        dve.wait_ge(mid_tap, 2 * j + g + 1)
                        dve.scalar_tensor_tensor(out=y[:, g, 1:T], in0=p[:, 0:T - 1], scalar=ffcur[s][:, 4 * g:4 * g + 1],
                                                 in1=y[:, g, 1:T], op0=ALU.mult, op1=ALU.add).then_inc(left_tap, 1)
                        dve.wait_ge(left_tap, 2 * j + g + 1)
                        dve.scalar_tensor_tensor(out=y[:, g, 0:T - 1], in0=p[:, 1:T], scalar=ffcur[s][:, 4 * g + 2:4 * g + 3],
                                                 in1=y[:, g, 0:T - 1], op0=ALU.mult, op1=ALU.add).then_inc(side_taps, 1)
                    dve.wait_ge(act_done, j + 1)
                    dve.wait_ge(side_taps, 2 * j + 2)
                    dve.tensor_tensor(out=hid[:, bass.ds(j, 1), :], in0=y[:, 0:1, :], in1=y[:, 1:2, :], op=ALU.mult).then_inc(hid_done, 1)

                for j in range(2):
                    body(j, j % 2, True, False)
                with dve.Fori(2, FT - 2, 2) as i:
                    for s in range(2):
                        body(i + s, s, False, False)
                body(FT - 2, 0, False, True)
                body(FT - 1, 1, False, True, last=True)

        dnh = at(110, "dnh", [P, 2, HALF], F32R)
        dnl = at(114, "dnl", [P, 2, HALF], F32R)
        ah = at(118, "ah", [P, 2, T], F32R)
        al = at(126, "al", [P, 2, T], F32R)
        x1 = at(143, "x1", [P, TT, D])
        gout = at(175, "gout", [P, TT, HALF])
        with ExitStack() as s6:
            sem6 = lambda n: s6.enter_context(nc.semaphore(n))
            x1_in = sem6("x1_in")
            dn_hi, dn_lo, a_hi, a_lo, dn_mm, bank_mm, bank_out, res_done, odd_done, stored, last_stored = (
                sem6(n) for n in ("dn_hi", "dn_lo", "a_hi", "a_lo", "dn_mm", "bank_mm", "bank_out", "res_done", "odd_done", "stored", "last_stored"))
            block = s6.enter_context(nc.Block())

            def steps(eng, body):
                for half in range(2):
                    n0 = half * FT
                    for k in range(2):
                        body(n0 + k, k, half, k % 2, "first" if k == 0 else "peeled")
                    with eng.Fori(2, FT - 2, 2) as i:
                        for s in range(2):
                            body(i + (n0 + s), i + s, half, s, "loop")
                    for k in range(FT - 2, FT):
                        body(n0 + k, k, half, k % 2, "last" if k == FT - 1 else "loop")

            def early(kind, half):
                return half == 0 and kind in ("first", "peeled")

            @block.sync
            def _(sp):
                sp.dma_start(x1[:], x1_dram.rearrange("(t p) d -> p t d", p=P)).then_inc(x1_in, 16)

                def body(n, k, half, s, kind):
                    if early(kind, half):
                        return
                    sp.wait_ge(dn_lo, n - 1)
                    sp.dma_start(dn_raw[:, s, :], w_down[0, bass.ds(k * P, P), half * HALF:(half + 1) * HALF]).then_inc(dn_in[s], 16)

                steps(sp, body)
                for t in range(TT):
                    if t % 2:
                        sp.wait_ge(odd_done, t // 2 + 1)
                    else:
                        sp.wait_ge(res_done, TT + t // 2 + 1)
                    sp.dma_start(out[0, t * P:(t + 1) * P, HALF:D], gout[:, t, :]).then_inc(last_stored, 16)
                sp.wait_ge(last_stored, 16 * TT)

            @block.tensor
            def _(pe):
                def body(n, k, half, s, kind):
                    pe.wait_ge(dn_lo, n + 1)
                    pe.wait_ge(a_lo, n + 1)
                    for t in range(TT):
                        if kind == "first" and half:
                            pe.wait_ge(bank_out, t + 1)
                        c_ = slice(t * P, (t + 1) * P)
                        pe.matmul(ps[:, t, :], ah[:, s, c_], dnh[:, s, :], start=(kind == "first"), stop=False)
                        pe.matmul(ps[:, t, :], ah[:, s, c_], dnl[:, s, :], start=False, stop=False)
                        last = pe.matmul(ps[:, t, :], al[:, s, c_], dnh[:, s, :], start=False, stop=(kind == "last"))
                        if kind == "last":
                            last.then_inc(bank_mm, 1)
                        elif t == TT - 1:
                            last.then_inc(dn_mm, 1)

                steps(pe, body)

            def wait_step_done(eng, n, half, kind, k):
                if early(kind, half):
                    return
                if half and kind in ("first", "peeled"):
                    if kind == "first":
                        eng.wait_ge(dn_mm, FT - 1)
                    else:
                        eng.wait_ge(bank_mm, TT)
                    return
                eng.wait_ge(dn_mm, n - 1 - half)

            @block.scalar
            def _(act):
                def body(n, k, half, s, kind):
                    act.wait_ge(dn_in[s], 8 * (n - s) + 16)
                    wait_step_done(act, n, half, kind, k)
                    act.activation(dnh[:, s, :], dn_raw[:, s, :], ACT.Copy).then_inc(dn_hi, 1)

                steps(act, body)

            @block.vector
            def _(dve):
                def drain(half):
                    for t in range(TT):
                        dve.wait_ge(bank_mm, half * TT + t + 1)
                        if half and t == 0:
                            dve.wait_ge(stored, 16 * TT)
                        dve.tensor_tensor(out=gout[:, t, :], in0=ps[:, t, :], in1=g2b[:, half * HALF:(half + 1) * HALF],
                                          op=ALU.mult).then_inc(bank_out, 1)
                        if half and t % 2:
                            dve.wait_ge(bank_out, TT + t + 1)
                            dve.tensor_tensor(out=gout[:, t, :], in0=gout[:, t, :], in1=x1[:, t, HALF:D], op=ALU.add).then_inc(odd_done, 1)

                def body(n, k, half, s, kind):
                    wait_step_done(dve, n, half, kind, k)
                    dve.tensor_scalar(ah[:, s:s + 1, :], hid[:, bass.ds(k, 1), :], 1.0, None, ALU.mult).then_inc(a_hi, 1)
                    dve.wait_ge(dn_hi, n + 1)
                    dve.tensor_tensor(out=dnl[:, s, :], in0=dn_raw[:, s, :], in1=f(dnh[:, s, :]), op=ALU.subtract).then_inc(dn_lo, 1)
                    dve.wait_ge(a_hi, n + 1)
                    dve.tensor_tensor(out=al[:, s:s + 1, :], in0=hid[:, bass.ds(k, 1), :], in1=f(ah[:, s:s + 1, :]),
                                      op=ALU.subtract).then_inc(a_lo, 1)

                for half in range(2):
                    n0 = half * FT
                    for k in range(2):
                        if half and k == 0:
                            body(n0, 0, 1, 0, "first")
                            drain(0)
                        else:
                            body(n0 + k, k, half, k % 2, "first" if k == 0 else "peeled")
                    with dve.Fori(2, FT - 2, 2) as i:
                        for s in range(2):
                            body(i + (n0 + s), i + s, half, s, "loop")
                    for k in range(FT - 2, FT):
                        body(n0 + k, k, half, k % 2, "last" if k == FT - 1 else "loop")
                dve.wait_ge(x1_in, 16)
                drain(1)

            @block.gpsimd
            def _(pool):
                pool.wait_ge(x1_in, 16)
                for t in range(TT):
                    v = gout[:, t, :]
                    pool.wait_ge(bank_out, t + 1)
                    pool.tensor_tensor(out=v, in0=v, in1=x1[:, t, 0:HALF], op=ALU.add).then_inc(res_done, 1)
                    pool.wait_ge(res_done, t + 1)
                    pool.dma_start(out[0, t * P:(t + 1) * P, 0:HALF], v).then_inc(stored, 16)
                pool.wait_ge(stored, TT * 16)
                for t in range(0, TT, 2):
                    v = gout[:, t, :]
                    pool.wait_ge(bank_out, TT + t + 1)
                    pool.tensor_tensor(out=v, in0=v, in1=x1[:, t, HALF:D], op=ALU.add).then_inc(res_done, 1)


def rope_table(np):
    axis = HD // 2
    inv = (np.float32(10000.0) ** (-np.arange(0, axis, 2, dtype=np.float32) / np.float32(axis))).astype(np.float32)
    pos = np.arange(T)
    ang_r = (pos // 64).astype(np.float32)[:, None] * inv
    ang_c = (pos % 64).astype(np.float32)[:, None] * inv
    sign = np.repeat(np.array([-1.0, 1.0, -1.0, 1.0], np.float32), axis // 2)
    ang = np.concatenate([ang_r, ang_r, ang_c, ang_c], axis=-1)
    return np.stack([np.cos(ang), np.sin(ang) * sign]).astype(np.float32)


INPUTS = ["x", "c", "ctx", "c_ctx", "w_mod", "b_mod", "norm_mix_w", "w_in", "q_norm_w", "k_norm_w", "sink_logit",
          "conv_w", "conv_b", "conv_norm_w", "conv_norm_b", "w_out", "norm_ffn_w", "w_up", "ffn_conv_w",
          "ffn_conv_b", "w_down"]


def kernel(**inputs):
    import numpy as np
    import concourse.bacc as bacc
    from concourse.bass_utils import run_bass_kernel_spmd

    nc = bacc.Bacc("TRN2", target_bir_lowering=False, num_devices=1)
    arrays, args = {}, []
    for name in INPUTS + ["rope"]:
        a = np.ascontiguousarray(rope_table(np) if name == "rope" else inputs[name])
        arrays[f"in_{name}"] = a
        args.append(nc.dram_tensor(f"in_{name}", a.shape, mybir.dt.from_np(a.dtype), kind="ExternalInput").ap())
    args.append(nc.dram_tensor("out_latent", (1, T, D), F32, kind="ExternalOutput").ap())
    build(nc, *args)
    result = run_bass_kernel_spmd(nc, [arrays], core_ids=[0])
    return result.results[0]["out_latent"]
```
